# Optimizing a Trainium2 kernel written in Bass

```python
import jax, jax.numpy as jnp
from jax import lax
import numpy as np

"""One inference step (DEPTH layers) of a hybrid chunk-causal streaming encoder.

Each layer is a single post-norm DeepNorm sub-layer: x <- LayerNorm(ALPHA*x + W_out[ A*SiLU(z_A) ; B*SiLU(z_B) ]),
where one combined input projection feeds two parallel head groups:
  A: chunked gMLP spatial gating unit (128-frame chunks, 4 channel groups, lower-triangular 128x128 W_s per group)
  B: chunked band attention (64-frame chunks, own chunk + 8 previous chunks, 8 heads, learned clipped relative bias)

Inputs:
  x_prompt (BATCH, SEQ, D_MODEL)            first SEQ frames of BATCH new streams (positions 0..SEQ-1)
  x_sample (DEC_BATCH, DEC_SEQ, D_MODEL)    next frames of running streams (positions PAST_LEN..PAST_LEN+DEC_SEQ-1)
  cache_k, cache_v (DEPTH, DEC_BATCH, KV_PAST, N_HEADS_B, HEAD_DIM_B), KV_PAST = min(LEFT_CHUNKS*CHUNK, PAST_LEN):
      band-attention K/V rows of the newest KV_PAST cached frames
  weights stacked over DEPTH.
Outputs (tuple):
  y_prompt (BATCH, SEQ, D_MODEL)
  y_sample (DEC_BATCH, DEC_SEQ, D_MODEL)
  k_prompt_new, v_prompt_new (DEPTH, BATCH, min(LEFT_CHUNKS*CHUNK, SEQ), N_HEADS_B, HEAD_DIM_B): newest band K/V rows left by the prompt
  k_sample_new, v_sample_new (DEPTH, DEC_BATCH, DEC_SEQ, N_HEADS_B, HEAD_DIM_B): K/V rows of the new frames
  gmlp_v_sample_new (DEPTH, DEC_BATCH, DEC_SEQ, D_A): normalised gMLP v rows of the new (partial) 128-chunk
"""

D_MODEL = 1024
BATCH = 1
SEQ = 2048
DEPTH = 1
DEC_BATCH = 8
DEC_SEQ = 16
PAST_LEN = 128

CHUNK = 64
D_MIX = D_MODEL
D_A = D_MIX // 2
D_B = D_MIX - D_A
N_GROUPS_A = 4
GROUP_DIM_A = D_A // N_GROUPS_A
GMLP_CHUNK = 128
N_HEADS_B = 8
HEAD_DIM_B = D_B // N_HEADS_B
LEFT_CHUNKS = 8
BAND = (LEFT_CHUNKS + 1) * CHUNK
MAX_REL = 128
N_REL = 2 * MAX_REL + 1
D_IN = 3 * D_A + 4 * D_B
ALPHA = (2 * DEPTH) ** 0.25
BETA = (8 * DEPTH) ** -0.25
LN_EPS = 1e-5

kernel_name = "hybrid_gmlp_bandattn_stream_step"

def _layernorm(x, g, b):
    xf = x.astype(jnp.float32)
    mu = jnp.mean(xf, axis=-1, keepdims=True)
    var = jnp.mean(jnp.square(xf - mu), axis=-1, keepdims=True)
    return ((xf - mu) * lax.rsqrt(var + LN_EPS) * g.astype(jnp.float32) + b.astype(jnp.float32)).astype(x.dtype)

def _project(x, w_in, ln_v_g, ln_v_b):
    h = jnp.einsum('bsd,de->bse', x, w_in)
    o = np.cumsum([0, D_A, D_A, D_A, D_B, D_B, D_B, D_B])
    u_a = jax.nn.gelu(h[..., o[0]:o[1]], approximate=False)
    v_a = _layernorm(jax.nn.gelu(h[..., o[1]:o[2]], approximate=False), ln_v_g, ln_v_b)
    z_a = h[..., o[2]:o[3]]
    q = h[..., o[3]:o[4]]
    k = h[..., o[4]:o[5]]
    v_b = h[..., o[5]:o[6]]
    z_b = h[..., o[6]:o[7]]
    return u_a, v_a, z_a, q, k, v_b, z_b

def _sgu_prompt(u, v, w_s, b_s):
    b, s, _ = v.shape
    vc = v.reshape(b, s // GMLP_CHUNK, GMLP_CHUNK, N_GROUPS_A, GROUP_DIM_A)
    mix = jnp.einsum('gts,bnsgc->bntgc', jnp.tril(w_s), vc) + b_s.T[None, None, :, :, None]
    return u * mix.reshape(b, s, D_A)

def _sgu_sample(u, v, w_s, b_s):
    b, n, _ = v.shape
    wm = jnp.tril(w_s)[:, :n, :n]
    vc = v.reshape(b, n, N_GROUPS_A, GROUP_DIM_A)
    mix = jnp.einsum('gts,bsgc->btgc', wm, vc) + b_s[:, :n].T[None, :, :, None]
    return u * mix.reshape(b, n, D_A)

def _rel_bias(table, n_q, n_past, n_k):
    d = jnp.arange(n_q)[:, None] + n_past - jnp.arange(n_k)[None, :]
    idx = jnp.clip(d, -MAX_REL, MAX_REL) + MAX_REL
    return table[:, idx].astype(jnp.float32)

def _band_attn_prompt(q, k, v, rel_table):
    b, s, _ = q.shape
    nc = s // CHUNK
    shp = (b, nc, CHUNK, N_HEADS_B, HEAD_DIM_B)
    qc, kc, vc = q.reshape(shp), k.reshape(shp), v.reshape(shp)
    pad = ((0, 0), (LEFT_CHUNKS, 0), (0, 0), (0, 0), (0, 0))
    kp, vp = jnp.pad(kc, pad), jnp.pad(vc, pad)
    kb = jnp.concatenate([kp[:, o:o + nc] for o in range(LEFT_CHUNKS + 1)], axis=2)
    vb = jnp.concatenate([vp[:, o:o + nc] for o in range(LEFT_CHUNKS + 1)], axis=2)
    src_chunk = jnp.arange(nc)[:, None] - LEFT_CHUNKS + jnp.arange(LEFT_CHUNKS + 1)[None, :]
    valid = jnp.repeat(src_chunk >= 0, CHUNK, axis=1)
    bias = _rel_bias(rel_table, CHUNK, BAND - CHUNK, BAND)
    scores = jnp.einsum('bnqhd,bnkhd->bnhqk', qc, kb).astype(jnp.float32) * (HEAD_DIM_B ** -0.5) + bias[None, None]
    scores = jnp.where(valid[None, :, None, None, :], scores, -jnp.inf)
    p = jax.nn.softmax(scores, axis=-1).astype(v.dtype)
    o = jnp.einsum('bnhqk,bnkhd->bnqhd', p, vb)
    return o.reshape(b, s, D_B), kc.reshape(b, s, N_HEADS_B, HEAD_DIM_B), vc.reshape(b, s, N_HEADS_B, HEAD_DIM_B)

def _band_attn_sample(q, k, v, ck, cv, rel_table):
    b, n, _ = q.shape
    n_past = ck.shape[1]
    shp = (b, n, N_HEADS_B, HEAD_DIM_B)
    qh, kh, vh = q.reshape(shp), k.reshape(shp), v.reshape(shp)
    k_all = jnp.concatenate([ck.astype(kh.dtype), kh], axis=1)
    v_all = jnp.concatenate([cv.astype(vh.dtype), vh], axis=1)
    bias = _rel_bias(rel_table, n, n_past, n_past + n)
    scores = jnp.einsum('bqhd,bkhd->bhqk', qh, k_all).astype(jnp.float32) * (HEAD_DIM_B ** -0.5) + bias[None]
    p = jax.nn.softmax(scores, axis=-1).astype(v.dtype)
    o = jnp.einsum('bhqk,bkhd->bqhd', p, v_all)
    return o.reshape(b, n, D_B), kh, vh

def _merge(x, a_out, z_a, b_out, z_b, w_out, g, bb):
    y = jnp.concatenate([a_out * jax.nn.silu(z_a), b_out * jax.nn.silu(z_b)], axis=-1)
    out = jnp.einsum('bse,ed->bsd', y, w_out)
    return _layernorm(ALPHA * x + out, g, bb)

def setup_inputs(seed: int = 0) -> dict:
    key = jax.random.key(seed)
    ks = jax.random.split(key, 13)
    kv_past = min(LEFT_CHUNKS * CHUNK, PAST_LEN)

    def nrm(k, shape):
        return jax.random.normal(k, shape, jnp.float32)

    return {
        'x_prompt': nrm(ks[0], (BATCH, SEQ, D_MODEL)),
        'x_sample': nrm(ks[1], (DEC_BATCH, DEC_SEQ, D_MODEL)),
        'cache_k': nrm(ks[2], (DEPTH, DEC_BATCH, kv_past, N_HEADS_B, HEAD_DIM_B)),
        'cache_v': nrm(ks[3], (DEPTH, DEC_BATCH, kv_past, N_HEADS_B, HEAD_DIM_B)),
        'w_in': nrm(ks[4], (DEPTH, D_MODEL, D_IN)) * (D_MODEL ** -0.5),
        'w_sgu': nrm(ks[5], (DEPTH, N_GROUPS_A, GMLP_CHUNK, GMLP_CHUNK)) * (GMLP_CHUNK ** -0.5),
        'b_sgu': 1.0 + 0.1 * nrm(ks[6], (DEPTH, N_GROUPS_A, GMLP_CHUNK)),
        'ln_v_g': 1.0 + 0.1 * nrm(ks[7], (DEPTH, D_A)),
        'ln_v_b': 0.02 * nrm(ks[8], (DEPTH, D_A)),
        'rel_bias': 0.2 * nrm(ks[9], (DEPTH, N_HEADS_B, N_REL)),
        'w_out': nrm(ks[10], (DEPTH, D_MIX, D_MODEL)) * (D_MIX ** -0.5 * BETA),
        'ln_g': 1.0 + 0.1 * nrm(ks[11], (DEPTH, D_MODEL)),
        'ln_b': 0.02 * nrm(ks[12], (DEPTH, D_MODEL)),
    }

def reference(x_prompt, x_sample, cache_k, cache_v, w_in, w_sgu, b_sgu, ln_v_g, ln_v_b, rel_bias, w_out, ln_g, ln_b):
    xp, xs = x_prompt, x_sample
    keep = min(LEFT_CHUNKS * CHUNK, xp.shape[1])
    kp_l, vp_l, ks_l, vs_l, gv_l = [], [], [], [], []
    for l in range(DEPTH):
        u_a, v_a, z_a, q, k, v_b, z_b = _project(xp, w_in[l], ln_v_g[l], ln_v_b[l])
        a_out = _sgu_prompt(u_a, v_a, w_sgu[l], b_sgu[l])
        b_out, kh, vh = _band_attn_prompt(q, k, v_b, rel_bias[l])
        kp_l.append(kh[:, -keep:])
        vp_l.append(vh[:, -keep:])
        xp = _merge(xp, a_out, z_a, b_out, z_b, w_out[l], ln_g[l], ln_b[l])
        u_a, v_a, z_a, q, k, v_b, z_b = _project(xs, w_in[l], ln_v_g[l], ln_v_b[l])
        a_out = _sgu_sample(u_a, v_a, w_sgu[l], b_sgu[l])
        b_out, kh, vh = _band_attn_sample(q, k, v_b, cache_k[l], cache_v[l], rel_bias[l])
        ks_l.append(kh)
        vs_l.append(vh)
        gv_l.append(v_a)
        xs = _merge(xs, a_out, z_a, b_out, z_b, w_out[l], ln_g[l], ln_b[l])
    k_prompt_new = jnp.stack(kp_l)
    v_prompt_new = jnp.stack(vp_l)
    k_sample_new = jnp.stack(ks_l)
    v_sample_new = jnp.stack(vs_l)
    gmlp_v_sample_new = jnp.stack(gv_l)
    return (xp, xs, k_prompt_new, v_prompt_new, k_sample_new, v_sample_new, gmlp_v_sample_new)


_drawn_inputs = setup_inputs


def setup_inputs(seed=0):
    import zlib

    import numpy as np

    out = dict(_drawn_inputs(seed))
    spreads = {}
    factors = {'b_sgu': 4.051, 'ln_v_b': 2.957, 'rel_bias': 8.0, 'ln_b': 2.906}
    for name, (base, spread) in spreads.items():
        noise = np.random.default_rng([zlib.crc32(name.encode()), seed]).standard_normal(out[name].shape)
        drawn = base * np.exp(spread * noise) if base else spread * noise
        out[name] = __import__('jax').numpy.asarray(drawn.astype(out[name].dtype))
    for name, factor in factors.items():
        out[name] = (out[name] * factor).astype(out[name].dtype)
    return out
```

```python
import numpy as np
import concourse.bass as bass
from concourse import mybir
from contextlib import ExitStack

P = 128
D = 1024
KC = D // P
SEQ = 2048
SB, SN = 8, 16
T = SEQ + SB * SN
TILES = T // P
PTILES = SEQ // P
GRP = 4
HD = 64
HEADS = 8
PAST = 128
SKEYS = PAST + SN
WIN = 640
CLIP = 128
REL = 6 * P
KEEP = 512
NGROUPS = 28
CHUNKS = [(0, 512), (512, 512), (1024, 384), (1408, 384), (1792, 384)]
NCH = len(CHUNKS)
ALPHA = 2.0 ** 0.25
EPS = 1e-5
QSCALE = -(HD ** -0.5)
MASKED = 3.0e38

GELU_GROUPS = [("u", 0), ("za", 0), ("va", 0), ("u", 1), ("za", 1), ("va", 1)]
PAIR_GROUPS = ["q", "k", "v", "z"]
LOOP_A = 2
LOOP_B = 4


def hybrid_stream_step(nc, x, w_all, w_sgu, b_sgu, ln_v_g, ln_v_b, rel_rev, ln_g, ln_b,
                       cache_k, cache_v, y_out, v_all, k_tail, gv_out):
    f32, f32r = mybir.dt.float32, mybir.dt.float32r
    ALU = mybir.AluOpType
    ACT = mybir.ActivationFunctionType

    ctx = ExitStack()
    with ctx:
        def dram(name, shape, dt=f32):
            return nc.dram_tensor(name, shape, dt).ap()

        s_gate = dram("s_gate", [GRP, P, T])
        s_va = dram("s_va", [GRP, P, T])
        s_q = dram("s_q", [2, GRP, P, SEQ])
        s_k = dram("s_k", [2, GRP, P, SEQ])
        s_z = dram("s_z", [GRP, P, T])
        s_y = dram("s_y", [2 * GRP, P, T])
        s_rel = dram("s_rel", [HEADS, REL])
        s_skew = dram("s_skew", [HEADS, P, REL + 1])

        outer = ctx.enter_context(ExitStack())

        def sb(stack, name, shape, dt=f32):
            return stack.enter_context(nc.sbuf_tensor(name, shape, dt))

        ident = sb(outer, "ident", [P, P])
        qs = sb(outer, "qs", [P, GRP, P])
        ks = sb(outer, "ks", [P, GRP, P])

        input_projection(nc, x, w_all, w_sgu, b_sgu, ln_v_g, ln_v_b, rel_rev, s_gate, s_va, s_q, s_k, s_z, s_y,
                         s_rel, s_skew, v_all, k_tail, gv_out, ident, qs, ks)
        wo_h = sb(outer, "wo_h", [P, KC, D], mybir.dt.float32r)
        wo_l = sb(outer, "wo_l", [P, KC, D], mybir.dt.float32r)
        attention(nc, w_all, s_q, s_k, s_z, s_y, s_skew, v_all, ident, wo_h, wo_l)
        output_projection(nc, x, ln_g, ln_b, cache_k, cache_v, s_z, s_y, s_skew, v_all, y_out, ident, qs, ks, wo_h, wo_l)


def input_projection(nc, x, w_all, w_sgu, b_sgu, ln_v_g, ln_v_b, rel_rev, s_gate, s_va, s_q, s_k, s_z, s_y,
                     s_rel, s_skew, v_all, k_tail, gv_out, ident, qs, ks):
    f32, f32r = mybir.dt.float32, mybir.dt.float32r
    ALU = mybir.AluOpType
    ACT = mybir.ActivationFunctionType

    ctx = ExitStack()
    with ctx:
        def sb(name, shape, dt=f32):
            return ctx.enter_context(nc.sbuf_tensor(name, shape, dt))

        def sem(name):
            return ctx.enter_context(nc.semaphore(name))

        xh = sb("xh", [P, KC, T], f32r)
        xl = sb("xl", [P, KC, T], f32r)
        raw = [sb(f"raw{s}", [P, KC, P]) for s in range(2)]
        wh = [sb(f"wh{s}", [P, KC, P], f32r) for s in range(2)]
        wl = [sb(f"wl{s}", [P, KC, P], f32r) for s in range(2)]
        big = sb("big", [P, T])
        x_in = [big[:, s * D:(s + 1) * D] for s in range(2)]
        va_t = big[:, 0:512].rearrange("p (g t) -> p g t", g=GRP)
        gate_t = big[:, 512:1024].rearrange("p (g t) -> p g t", g=GRP)
        vn = big[:, 1024:1536]
        ya = big[:, 1536:2048].rearrange("p (g t) -> p g t", g=GRP)
        st_a = [sb(f"st_a{s}", [P, 512]) for s in range(2)]
        st_b = [sb(f"st_b{s}", [P, 512]) for s in range(2)]
        kf = sb("kf", [P, 640])
        kn = sb("kn", [P, 3, P])
        vt = sb("vt", [P, 512])
        lnvg = sb("lnvg", [P, 512])
        lnvb = sb("lnvb", [P, 512])
        wt = sb("wt", [P, GRP, P])
        wts = sb("wts", [P, GRP, P])
        bs = sb("bs", [P, GRP, P])
        bss = sb("bss", [P, GRP, P])
        minus_half = sb("minus_half_i", [P, 1])
        eps = sb("eps_i", [P, 1])
        stats = sb("stats", [P, 6])
        mv = sb("mv", [P, 2])
        rstd = sb("rstd", [P, 1])

        bank = [ctx.enter_context(nc.psum_tensor(f"bank{c}", [P, 512], f32)) for c in range(NCH)]
        tg_ps = ctx.enter_context(nc.psum_tensor("tg_ps", [P, 512], f32))
        tv_ps = ctx.enter_context(nc.psum_tensor("tv_ps", [P, 512], f32))
        mix_ps = ctx.enter_context(nc.psum_tensor("mix_ps", [P, 512], f32))

        par_loaded = sem("par_loaded")
        blocks_loaded = sem("blocks_loaded")
        const_ready = sem("const_ready")
        zeroed = sem("zeroed")
        wt_turned = sem("wt_turned")
        wt_ready = sem("wt_ready")
        bss_ready = sem("bss_ready")
        rel_loaded = sem("rel_loaded")
        rel_filled = sem("rel_filled")
        rel_negated = sem("rel_negated")
        rel_stored = sem("rel_stored")
        x_loaded = [sem(f"x_loaded{s}") for s in range(2)]
        x_turned = sem("x_turned")
        xh_done = sem("xh_done")
        xbank_free = sem("xbank_free")
        raw_loaded = [sem(f"raw_loaded{s}") for s in range(2)]
        wh_done = sem("wh_done")
        w_ready = sem("w_ready")
        proj_done = sem("proj_done")
        evac = [sem(f"evac{c}") for c in range(NCH)]
        act_read = sem("act_read")
        gate_full = sem("gate_full")
        st_a_stored = [sem(f"st_a_stored{s}") for s in range(2)]
        st_b_stored = [sem(f"st_b_stored{s}") for s in range(2)]
        kf_full = sem("kf_full")
        tv_done = sem("tv_done")
        tv_copied = sem("tv_copied")
        kn_stored = sem("kn_stored")
        va_loaded = sem("va_loaded")
        gate_loaded = sem("gate_loaded")
        tg_done = sem("tg_done")
        tg_read = sem("tg_read")
        stats_ready = sem("stats_ready")
        mv_ready = sem("mv_ready")
        var_eps = sem("var_eps")
        rstd_ready = sem("rstd_ready")
        vn_step = sem("vn_step")
        vn_ready = sem("vn_ready")
        mix_done = sem("mix_done")
        mix_read = sem("mix_read")
        ya_full = sem("ya_full")
        ya_stored = sem("ya_stored")
        gv_stored = sem("gv_stored")

        block = ctx.enter_context(nc.Block())

        N_A = LOOP_A * len(GELU_GROUPS)
        A_J, B_J = len(GELU_GROUPS), len(PAIR_GROUPS)
        XHALVES = 2 * TILES

        @block.sync
        def _(sp):
            for s in range(2):
                sp.sem_inc(st_a_stored[s], 16)
                sp.sem_inc(st_b_stored[s], 16)
            sp.sem_inc(kn_stored, 16)
            sp.sem_inc(ya_stored, 16)

            def load_x(tile, s):
                sp.dma_start(x_in[s], x[bass.ts(tile, P), :]).then_inc(x_loaded[s], 16)

            load_x(0, 0)
            load_x(1, 1)
            with sp.Fori(0, PTILES // 2 - 1) as i:
                for s in range(2):
                    sp.wait_ge(x_turned, i * 4 + 2 * s + 2)
                    load_x(i * 2 + 2 + s, s)
            sp.wait_ge(x_turned, 2 * (PTILES - 2) + 2)
            load_x(TILES - 1, 0)

            sp.dma_start(st_a[0][:].rearrange("p (g s) -> p g s", g=GRP),
                         w_sgu.rearrange("g t s -> t g s")).then_inc(par_loaded, 16)
            sp.dma_start(lnvg[:], ln_v_g.partition_broadcast(P)).then_inc(par_loaded, 16)
            sp.dma_start(lnvb[:], ln_v_b.partition_broadcast(P)).then_inc(par_loaded, 16)
            sp.dma_start(bs[:].rearrange("p g t -> p (g t)"), b_sgu.partition_broadcast(P)).then_inc(par_loaded, 16)
            sp.wait_ge(zeroed, 1)
            blk = st_b[0][:].rearrange("p (g s) -> p g s", g=GRP)
            for b in range(SB):
                sp.dma_start(blk[b * SN:(b + 1) * SN, :, b * SN:(b + 1) * SN],
                             w_sgu[:, 0:SN, 0:SN].rearrange("g t s -> t g s")).then_inc(blocks_loaded, 16)

            sp.dma_start(kf[0:HEADS, 0:2 * CLIP + 1], rel_rev).then_inc(rel_loaded, 16)
            sp.wait_ge(rel_negated, 2)
            flat = REL - (2 * CLIP + 1)
            sp.dma_start(s_rel[:, 0:flat], vt[0:HEADS, 0:flat]).then_inc(rel_stored, 16)
            sp.dma_start(s_rel[:, flat:REL], kf[0:HEADS, 0:2 * CLIP + 1]).then_inc(rel_stored, 16)
            sp.wait_ge(rel_stored, 32)
            for h in range(HEADS):
                sp.dma_start(s_skew[h, :, 0:REL], s_rel[h, :].partition_broadcast(P)).then_inc(rel_stored, 16)

            with sp.Fori(0, LOOP_A) as i:
                na = nb = 0
                for j, (kind, h) in enumerate(GELU_GROUPS):
                    for c, (t0, n) in enumerate(CHUNKS):
                        if kind == "za":
                            sp.wait_ge(gate_full, i * 10 + nb + 1)
                            sp.dma_start(s_gate[i * 2 + h, :, t0:t0 + n], st_b[nb % 2][:, 0:n]).then_inc(st_b_stored[nb % 2], 16)
                            nb += 1
                        elif kind == "va":
                            sp.wait_ge(evac[c], i * A_J + j + 2)
                            sp.dma_start(s_va[i * 2 + h, :, t0:t0 + n], st_a[na % 2][:, 0:n]).then_inc(st_a_stored[na % 2], 16)
                            na += 1

            def load_gmlp(tile):
                sp.dma_start(va_t, s_va[:, :, bass.ts(tile, P)].rearrange("g c t -> c g t")).then_inc(va_loaded, 16)
                sp.dma_start(gate_t, s_gate[:, :, bass.ts(tile, P)].rearrange("g c t -> c g t")).then_inc(gate_loaded, 16)

            for s in range(2):
                sp.wait_ge(st_a_stored[s], 16 + 16 * 10)
                sp.wait_ge(st_b_stored[s], 16 + 16 * 10)
            load_gmlp(0)

            def store_kn(c, p):
                t0, nt = ((1536, 2), (1792, 3))[c]
                sp.wait_ge(tv_copied, p * 7 + c + 2)
                sp.dma_start(k_tail[t0 - 1536:t0 - 1536 + nt * P, bass.ts(p, P)].rearrange("(n t) c -> t n c", t=P),
                             kn[:, 0:nt, :]).then_inc(kn_stored, 16)

            def store_vn(c, p):
                t0, n = CHUNKS[c]
                sp.wait_ge(tv_copied, p * 7 + c + 4)
                sp.dma_start(v_all[t0:t0 + n, bass.ts(p, P)].rearrange("(n t) c -> t n c", t=P),
                             st_b[c % 2][:, 0:n].rearrange("t (n c) -> t n c", c=P)).then_inc(st_b_stored[c % 2], 16)

            with sp.Fori(0, LOOP_B) as p:
                for j, kind in enumerate(PAIR_GROUPS):
                    for c, (t0, n) in enumerate(CHUNKS):
                        m = min(n, SEQ - t0)
                        if kind in "qk":
                            e = 5 * j + c
                            dst = s_q if kind == "q" else s_k
                            sp.wait_ge(evac[c], N_A + p * B_J + j + 2)
                            sp.dma_start(dst[0, p, :, t0:t0 + m], st_a[e % 2][:, 0:m]).then_inc(st_a_stored[e % 2], 16)
                            sp.dma_start(dst[1, p, :, t0:t0 + m], st_b[e % 2][:, 0:m]).then_inc(st_b_stored[e % 2], 16)
                        if kind == "z":
                            if c == 0:
                                store_vn(4, p)
                            e = 15 + c
                            sp.wait_ge(evac[c], N_A + p * B_J + j + 2)
                            sp.dma_start(s_z[p, :, t0:t0 + n], st_b[e % 2][:, 0:n]).then_inc(st_b_stored[e % 2], 16)
                        if kind == "k" and c == 4:
                            store_kn(0, p)
                        if kind == "v":
                            if c == 0:
                                store_kn(1, p)
                            else:
                                store_vn(c - 1, p)
                    sp.wait_ge(ya_full, p * 4 + j + 1)
                    sp.dma_start(s_y[0:GRP, :, bass.ts(p * 4 + j, P)].rearrange("g c t -> c g t"), ya).then_inc(ya_stored, 16)
                    load_gmlp(p * 4 + j + 1)

            sp.wait_ge(vn_ready, TILES)
            sp.dma_start(gv_out, vn).then_inc(gv_stored, 16)
            sp.wait_ge(ya_full, TILES)
            sp.dma_start(s_y[0:GRP, :, SEQ:T].rearrange("g c t -> c g t"), ya).then_inc(ya_stored, 16)
            sp.wait_ge(ya_stored, 16 + 16 * TILES)
            sp.wait_ge(gv_stored, 16)
            sp.wait_ge(kn_stored, 16 + 16 * 2 * LOOP_B)
            sp.wait_ge(rel_stored, 16 * (2 + HEADS))
            for s in range(2):
                sp.wait_ge(st_a_stored[s], 16 + 16 * 10 + 16 * 5 * LOOP_B)
                sp.wait_ge(st_b_stored[s], 16 + 16 * 10 + 16 * 10 * LOOP_B)

        @block.gpsimd
        def _(pool):
            nc.gpsimd.memset(minus_half[:], -0.5).then_inc(const_ready, 1)
            nc.gpsimd.memset(eps[:], EPS).then_inc(const_ready, 1)
            nc.gpsimd.memset(ident[:], 1.0).then_inc(const_ready, 1)
            nc.gpsimd.memset(st_b[0][:], 0.0).then_inc(zeroed, 1)
            nc.gpsimd.memset(vt[:], 0.0).then_inc(rel_filled, 1)
            pool.wait_ge(const_ready, 3)
            nc.gpsimd.affine_select(out=ident[:], in_=ident[:], compare_op=ALU.is_equal, fill=0.0, base=0,
                                    pattern=[[-1, P]], channel_multiplier=1).then_inc(const_ready, 1)
            for full, held, need in ((st_a[0], par_loaded, 64), (st_b[0], blocks_loaded, 16 * SB)):
                pool.wait_ge(held, need)
                v = full[:].rearrange("p (g s) -> p g s", g=GRP)
                nc.gpsimd.affine_select(out=v, in_=v, compare_op=ALU.is_ge, fill=0.0, base=0,
                                        pattern=[[0, GRP], [-1, P]], channel_multiplier=1).then_inc(const_ready, 1)

            def gmlp(n):
                pool.wait_ge(mv_ready, n + 1)
                nc.gpsimd.tensor_tensor(rstd[:], mv[:, 1:2], eps[:], ALU.add).then_inc(var_eps, 1)
                pool.wait_ge(var_eps, n + 1)
                nc.gpsimd.tensor_tensor(rstd[:], rstd[:], minus_half[:], ALU.pow).then_inc(rstd_ready, 1)
                pool.wait_ge(tg_read, n + 2)
                nc.gpsimd.tensor_tensor(vn, vn, lnvg[:], ALU.mult).then_inc(vn_step, 1)
                pool.wait_ge(vn_step, n + 1)
                nc.gpsimd.tensor_tensor(vn, vn, lnvb[:], ALU.add).then_inc(vn_ready, 1)
                pool.wait_ge(mix_read, n + 2)
                pool.wait_ge(gate_loaded, n * 16 + 16)
                nc.gpsimd.tensor_tensor(ya, ya, gate_t, ALU.mult).then_inc(ya_full, 1)

            with pool.Fori(0, TILES) as n:
                gmlp(n)

        @block.scalar
        def _(act):
            def load_w(n, s):
                act.dma_start(raw[s][:], w_all[n, :, :, :]).then_inc(raw_loaded[s], 16)

            def high_part(s, loads):
                act.wait_ge(raw_loaded[s], loads * 16)
                nc.scalar.activation(wh[s][:], raw[s][:], ACT.Copy).then_inc(wh_done, 1)

            load_w(0, 0)
            load_w(1, 1)
            high_part(0, 1)

            def x_high(n, b, tile):
                act.wait_ge(x_turned, n + 1)
                nc.scalar.activation(xh[:, 4 * (b % 2):4 * (b % 2) + 4, bass.ts(tile, P)],
                                     bank[b][:].rearrange("p (k t) -> p k t", k=4), ACT.Copy).then_inc(xh_done, 1)

            with act.Fori(0, PTILES // 2) as i:
                for b in range(4):
                    x_high(i * 4 + b, b, i * 2 + b // 2)
            for b in range(2):
                x_high(2 * PTILES + b, b, PTILES)

            def split(n, s, loads):
                act.wait_ge(w_ready, n)
                load_w(n + 1, 1 - s)
                high_part(s, loads)

            act.wait_ge(wt_turned, 2)
            with act.Fori(0, LOOP_A) as i:
                na = nb = 0
                for j, (kind, h) in enumerate(GELU_GROUPS):
                    for c, (t0, n) in enumerate(CHUNKS):
                        act.wait_ge(proj_done, i * (5 * A_J) + 5 * j + c + 1)
                        src = bank[c][:, 0:n]
                        if kind == "u":
                            nc.scalar.activation(big[:, t0:t0 + n], src, ACT.Gelu).then_inc(evac[c], 1)
                        elif kind == "za":
                            act.wait_ge(st_b_stored[nb % 2], i * 80 + 16 * (nb // 2) + 16)
                            nc.scalar.activation(st_b[nb % 2][:, 0:n], src, ACT.Tanh, scale=0.5).then_inc(act_read, 1)
                            nb += 1
                        else:
                            act.wait_ge(st_a_stored[na % 2], i * 80 + 16 * (na // 2) + 16)
                            nc.scalar.activation(st_a[na % 2][:, 0:n], src, ACT.Gelu).then_inc(evac[c], 1)
                            na += 1
                        if c == 1:
                            split(i * A_J + j + 1, (j + 1) % 2, i * (A_J // 2) + (j + 1) // 2 + 1)
            with act.Fori(0, LOOP_B) as p:
                for j, kind in enumerate(PAIR_GROUPS):
                    for c, (t0, n) in enumerate(CHUNKS):
                        act.wait_ge(proj_done, 5 * N_A + p * (5 * B_J) + 5 * j + c + 1)
                        src = bank[c][:, 0:n]
                        e = 5 * j + c
                        if kind in "qk":
                            act.wait_ge(st_a_stored[e % 2], 160 + p * 80 + 16 * (e // 2) + 16)
                            scale = QSCALE if kind == "q" else 1.0
                            if kind == "q" and c == 4:
                                nc.scalar.activation(qs[:, p, :], src[:, 256:384], ACT.Copy, scale=scale)
                            if kind == "k" and c == 3:
                                nc.scalar.activation(kf[:, 0:256], src[:, 128:384], ACT.Copy).then_inc(kf_full, 1)
                            if kind == "k" and c == 4:
                                nc.scalar.activation(ks[:, p, :], src[:, 256:384], ACT.Copy)
                                nc.scalar.activation(kf[:, 256:640], src, ACT.Copy).then_inc(kf_full, 1)
                            nc.scalar.activation(st_a[e % 2][:, 0:n].bitcast(f32r), src, ACT.Copy,
                                                 scale=scale).then_inc(act_read, 1)
                        elif kind == "v":
                            if c > 0:
                                act.wait_ge(tv_done, p * 7 + 2 + c)
                            nc.scalar.activation(vt[:, 0:n], src, ACT.Copy).then_inc(evac[c], 1)
                        else:
                            act.wait_ge(st_b_stored[e % 2], 160 + p * 160 + 16 * (e // 2) + 16)
                            nc.scalar.activation(st_b[e % 2][:, 0:n], src, ACT.Tanh, scale=0.5).then_inc(act_read, 1)
                        if c == 1:
                            split(N_A + p * B_J + j + 1, (j + 1) % 2, N_A // 2 + p * (B_J // 2) + (j + 1) // 2 + 1)

            act.wait_ge(raw_loaded[1], 16 * (NGROUPS // 2 + 1))

        @block.vector
        def _(dve):
            dve.sem_inc(xbank_free, 4)
            dve.sem_inc(tv_copied, 1)
            dve.sem_inc(tg_read, 1)
            dve.sem_inc(mix_read, 1)

            def low_part(n, s):
                dve.wait_ge(wh_done, n + 1)
                nc.vector.tensor_tensor(wl[s][:], raw[s][:], wh[s][:].bitcast(f32), ALU.subtract).then_inc(w_ready, 1)

            low_part(0, 0)

            def x_low(n, b, tile):
                dve.wait_ge(xh_done, n + 1)
                at = (slice(None), slice(4 * (b % 2), 4 * (b % 2) + 4), bass.ts(tile, P))
                nc.vector.tensor_tensor(xl[at], bank[b][:].rearrange("p (k t) -> p k t", k=4),
                                        xh[at].bitcast(f32), ALU.subtract).then_inc(xbank_free, 1)

            with dve.Fori(0, PTILES // 2) as i:
                for b in range(4):
                    x_low(i * 4 + b, b, i * 2 + b // 2)
            for b in range(2):
                x_low(2 * PTILES + b, b, PTILES)
            dve.wait_ge(rel_loaded, 16)
            dve.wait_ge(rel_filled, 1)
            nc.vector.tensor_scalar(kf[0:HEADS, 0:2 * CLIP + 1], kf[0:HEADS, 0:2 * CLIP + 1], -1.0, None,
                                    ALU.mult).then_inc(rel_negated, 1)
            dve.wait_ge(rel_negated, 1)
            nc.vector.tensor_scalar(vt[0:HEADS, :], vt[0:HEADS, :], kf[0:HEADS, 0:1], None, ALU.add).then_inc(rel_negated, 1)
            dve.wait_ge(wt_turned, 1)
            nc.vector.tensor_copy(wt[:].rearrange("p g t -> p (g t)"), tg_ps[:]).then_inc(wt_ready, 1)
            dve.wait_ge(wt_turned, 2)
            nc.vector.tensor_copy(wts[:].rearrange("p g t -> p (g t)"), tv_ps[:]).then_inc(wt_ready, 1)
            for b in range(SB):
                nc.vector.tensor_copy(bss[:, :, b * SN:(b + 1) * SN], bs[:, :, 0:SN]).then_inc(bss_ready, 1)
            for c in range(NCH):
                dve.sem_inc(evac[c], 1)

            def silu_twice(n, c, st, handed):
                dve.wait_ge(act_read, handed)
                nc.vector.scalar_tensor_tensor(out=st, in0=st, scalar=1.0, in1=bank[c][:, 0:n], op0=ALU.add,
                                               op1=ALU.mult).then_inc(evac[c], 1)

            with dve.Fori(0, LOOP_A) as i:
                nb = 0
                for j, (kind, h) in enumerate(GELU_GROUPS):
                    for c, (t0, n) in enumerate(CHUNKS):
                        if kind == "za":
                            st = st_b[nb % 2][:, 0:n]
                            silu_twice(n, c, st, i * 10 + nb + 1)
                            dve.wait_ge(evac[c], i * A_J + j + 2)
                            nc.vector.scalar_tensor_tensor(out=st, in0=st, scalar=0.5, in1=big[:, t0:t0 + n],
                                                           op0=ALU.mult, op1=ALU.mult).then_inc(gate_full, 1)
                            nb += 1
                        if c == 1:
                            low_part(i * A_J + j + 1, (j + 1) % 2)

            def gmlp_stats(n):
                dve.wait_ge(tg_done, n + 1)
                nc.vector.bn_stats(stats[:], tg_ps[:]).then_inc(stats_ready, 1)
                dve.wait_ge(stats_ready, n + 1)
                dve.nop(nofuse=True)
                nc.vector.bn_aggr(mv[:], stats[:]).then_inc(mv_ready, 1)

            def gmlp_normalise(n):
                dve.wait_ge(rstd_ready, n + 1)
                nc.vector.tensor_scalar(vn, tg_ps[:], mv[:, 0:1], rstd[:], ALU.subtract, ALU.mult).then_inc(tg_read, 1)

            def gmlp_mixed(n, offset):
                dve.wait_ge(mix_done, n + 1)
                dve.wait_ge(ya_stored, n * 16 + 16)
                nc.vector.tensor_tensor(ya, mix_ps[:].rearrange("p (g t) -> p g t", g=GRP), offset[:],
                                        ALU.add).then_inc(mix_read, 1)

            def copy_kn(c, p):
                nt = (2, 3)[c]
                dve.wait_ge(tv_done, p * 7 + c + 1)
                dve.wait_ge(kn_stored, p * 32 + 16 * c + 16)
                nc.vector.tensor_copy(kn[:, 0:nt, :].rearrange("t n c -> t (n c)"),
                                      tv_ps[:, 0:nt * P]).then_inc(tv_copied, 1)

            def copy_vn(c, p):
                n = CHUNKS[c][1]
                dve.wait_ge(tv_done, p * 7 + 3 + c)
                dve.wait_ge(st_b_stored[c % 2], 160 + p * 160 + 16 * ((10 + c) // 2) + 16)
                nc.vector.tensor_copy(st_b[c % 2][:, 0:n], tv_ps[:, 0:n]).then_inc(tv_copied, 1)

            with dve.Fori(0, LOOP_B) as p:
                for j, kind in enumerate(PAIR_GROUPS):
                    for c, (t0, n) in enumerate(CHUNKS):
                        e = 5 * j + c
                        if kind in "qk":
                            dve.wait_ge(act_read, 20 + p * 15 + e + 1)
                            dve.wait_ge(st_b_stored[e % 2], 160 + p * 160 + 16 * (e // 2) + 16)
                            nc.vector.scalar_tensor_tensor(
                                out=st_b[e % 2][:, 0:n].bitcast(f32r), in0=bank[c][:, 0:n],
                                scalar=QSCALE if kind == "q" else 1.0, in1=st_a[e % 2][:, 0:n],
                                op0=ALU.mult, op1=ALU.subtract).then_inc(evac[c], 1)
                        if kind == "z":
                            silu_twice(n, c, st_b[e % 2][:, 0:n], 20 + p * 15 + 10 + c + 1)
                        if c == 1:
                            low_part(N_A + p * B_J + j + 1, (j + 1) % 2)
                        if c == 0:
                            gmlp_stats(p * 4 + j)
                        if c == 1:
                            gmlp_normalise(p * 4 + j)
                        if c == 3:
                            gmlp_mixed(p * 4 + j, bs)
                        if kind == "k" and c == 4:
                            copy_kn(0, p)
                        if kind == "v":
                            if c == 0:
                                copy_kn(1, p)
                            else:
                                copy_vn(c - 1, p)
                        if kind == "z" and c == 0:
                            copy_vn(4, p)
            gmlp_stats(PTILES)
            gmlp_normalise(PTILES)
            gmlp_mixed(PTILES, bss)

        @block.tensor
        def _(pe):
            pe.wait_ge(const_ready, 4)

            def turn_x(n, b, s):
                pe.wait_ge(xbank_free, n + 1)
                for k in range(4):
                    kc = 4 * (b % 2) + k
                    last = nc.tensor.transpose(bank[b][:, k * P:(k + 1) * P], x_in[s][:, kc * P:(kc + 1) * P], ident[:])
                last.then_inc(x_turned, 1)

            with pe.Fori(0, PTILES // 2) as i:
                for s in range(2):
                    pe.wait_ge(x_loaded[s], i * 16 + 16)
                    for hf in range(2):
                        turn_x(i * 4 + 2 * s + hf, 2 * s + hf, s)
            pe.wait_ge(x_loaded[0], 16 * (PTILES // 2 + 1))
            for hf in range(2):
                turn_x(2 * PTILES + hf, hf, 0)

            for n, (src, dst) in enumerate(((st_a[0], tg_ps), (st_b[0], tv_ps))):
                pe.wait_ge(const_ready, 5 + n)
                for g in range(GRP):
                    last = nc.tensor.transpose(dst[:, g * P:(g + 1) * P], src[:, g * P:(g + 1) * P], ident[:])
                last.then_inc(wt_turned, 1)
            pe.wait_ge(wt_ready, 2)
            pe.wait_ge(xbank_free, XHALVES + 4)

            def project(n, c, s):
                t0, width = CHUNKS[c]
                if c == 0:
                    pe.wait_ge(w_ready, n + 1)
                pe.wait_ge(evac[c], n + 1)
                for kc in range(KC):
                    for a, (w, xx) in enumerate(((wh, xh), (wh, xl), (wl, xh))):
                        last = nc.tensor.matmul(bank[c][:, 0:width], w[s][:, kc, :], xx[:, kc, t0:t0 + width],
                                                start=kc == 0 and a == 0, stop=kc == KC - 1 and a == 2)
                last.then_inc(proj_done, 1)

            with pe.Fori(0, LOOP_A) as i:
                for j in range(A_J):
                    for c in range(NCH):
                        project(i * A_J + j, c, j % 2)

            def turn_va(n):
                pe.wait_ge(va_loaded, n * 16 + 16)
                pe.wait_ge(tg_read, n + 1)
                for g in range(GRP):
                    last = nc.tensor.transpose(tg_ps[:, g * P:(g + 1) * P], va_t[:, g, :], ident[:])
                last.then_inc(tg_done, 1)

            def mix(n, w):
                pe.wait_ge(vn_ready, n + 1)
                pe.wait_ge(mix_read, n + 1)
                for g in range(GRP):
                    last = nc.tensor.matmul(mix_ps[:, g * P:(g + 1) * P], vn[:, g * P:(g + 1) * P], w[:, g, :],
                                            start=True, stop=True)
                last.then_inc(mix_done, 1)

            def turn_k(c, p):
                pe.wait_ge(kf_full, p * 2 + c + 1)
                pe.wait_ge(tv_copied, p * 7 + c + 1)
                for n, t in enumerate(((0, 1), (2, 3, 4))[c]):
                    last = nc.tensor.transpose(tv_ps[:, n * P:(n + 1) * P], kf[:, t * P:(t + 1) * P], ident[:])
                last.then_inc(tv_done, 1)

            def turn_v(c, p):
                pe.wait_ge(evac[c], N_A + p * B_J + 2 + 2)
                pe.wait_ge(tv_copied, p * 7 + 3 + c)
                for n in range(CHUNKS[c][1] // P):
                    last = nc.tensor.transpose(tv_ps[:, n * P:(n + 1) * P], vt[:, n * P:(n + 1) * P], ident[:])
                last.then_inc(tv_done, 1)

            with pe.Fori(0, LOOP_B) as p:
                for j, kind in enumerate(PAIR_GROUPS):
                    for c in range(NCH):
                        project(N_A + p * B_J + j, c, j % 2)
                        if c == 0:
                            turn_va(p * 4 + j)
                        if c == 3:
                            mix(p * 4 + j, wt)
                        if kind == "k" and c == 4:
                            turn_k(0, p)
                        if kind == "v":
                            if c == 0:
                                turn_k(1, p)
                            else:
                                turn_v(c - 1, p)
                        if kind == "z" and c == 0:
                            turn_v(4, p)
            turn_va(PTILES)
            mix(PTILES, wts)


def skewed(s_skew, heads, queries, past, keys):
    first = WIN - 1 - past
    flat = s_skew.rearrange("h i m -> h (i m)")[heads, first:first + queries * REL]
    return flat.rearrange("h (i m) -> i h m", m=REL)[:, :, 0:keys]


def key_tiles(t):
    return min(t, 4) + 1


def turned_banks(t):
    return -(-2 * key_tiles(t) // 4)


def attention(nc, w_all, s_q, s_k, s_z, s_y, s_skew, v_all, ident, wo_h, wo_l):
    f32, f32r = mybir.dt.float32, mybir.dt.float32r
    ALU = mybir.AluOpType
    ACT = mybir.ActivationFunctionType

    ctx = ExitStack()
    with ctx:
        def sb(name, shape, dt=f32):
            return ctx.enter_context(nc.sbuf_tensor(name, shape, dt))

        def sem(name):
            return ctx.enter_context(nc.semaphore(name))

        q = sb("q", [P, 2, 2, SEQ], f32r)
        k = sb("k", [P, 2, SEQ], f32r)
        v = sb("v", [P, PTILES, P])
        z = sb("z", [P, SEQ])
        bias_next = sb("bias_next", [P, 2, WIN])
        bias = sb("bias", [P, 2, WIN])
        prob = [sb(f"prob{s}", [P, WIN]) for s in range(4)]
        low = sb("low", [P, 4])
        den = sb("den", [P, 4])
        rden = sb("rden", [P, 4])
        pt = [sb(f"pt{s}", [P, 10, P]) for s in range(2)]
        yst = [sb(f"yst{s}", [P, 512]) for s in range(2)]
        raw_o = [sb(f"raw_o{s}", [P, KC, P]) for s in range(2)]

        s_ps = [ctx.enter_context(nc.psum_tensor(f"s_ps{h}", [P, 2, 512], f32)) for h in range(2)]
        pt_ps = [ctx.enter_context(nc.psum_tensor(f"pt_ps{e}", [P, 4, P], f32)) for e in range(3)]
        o_ps = ctx.enter_context(nc.psum_tensor("o_ps", [P, 512], f32))

        chunk_loaded = [sem(f"chunk_loaded{c}") for c in range(4)]
        bias_loaded = sem("bias_loaded")
        masked = sem("masked")
        bias_ready = sem("bias_ready")
        scored = sem("scored")
        biased = sem("biased")
        expd = sem("expd")
        rden_ready = sem("rden_ready")
        normed = sem("normed")
        turned = sem("turned")
        pt_copied = sem("pt_copied")
        pv_done = sem("pv_done")
        y_ready = sem("y_ready")
        y_stored = [sem(f"y_stored{s}") for s in range(2)]
        raw_o_loaded = [sem(f"raw_o_loaded{s}") for s in range(2)]
        wo_high = sem("wo_high")
        wo_done = sem("wo_done")

        CHUNK_DMAS = 8
        BANKS = [0]
        for t in range(PTILES):
            BANKS.append(BANKS[-1] + turned_banks(t))
        assert BANKS[-1] % 3 == 0
        PER = BANKS[-1]

        block = ctx.enter_context(nc.Block())

        @block.sync
        def _(sp):
            for s in range(2):
                sp.sem_inc(y_stored[s], 16)

            def load_bias(pair):
                sp.dma_start(bias_next[:], skewed(s_skew, bass.ts(pair, 2), P, WIN - P, WIN)).then_inc(bias_loaded, 16)

            def load_chunk(pair, c):
                at = slice(512 * c, 512 * c + 512)
                for part in range(2):
                    qsrc = s_q[part, pair, :, at].rearrange("(h d) t -> d h t", h=2)
                    for half in range(2):
                        sp.dma_start(q[64 * half:64 * half + 64, :, part, at].bitcast(f32), qsrc).then_inc(chunk_loaded[c], 16)
                    ksrc = s_k[part, pair, :, at].rearrange("(h d) t -> d h t", h=2)
                    sp.dma_start(k[64 * part:64 * part + 64, :, at].bitcast(f32), ksrc).then_inc(chunk_loaded[c], 16)
                sp.dma_start(v[:, 4 * c:4 * c + 4, :],
                             v_all[at, bass.ts(pair, P)].rearrange("(n t) c -> t n c", t=P)).then_inc(chunk_loaded[c], 16)
                sp.dma_start(z[:, at], s_z[pair, :, at]).then_inc(chunk_loaded[c], 16)

            def store_y(pair, c):
                sp.wait_ge(y_ready, pair * PTILES + 4 * c + 4 + 1)
                sp.dma_start(s_y[pair + GRP, :, 512 * c:512 * c + 512], yst[c % 2][:]).then_inc(y_stored[c % 2], 16)

            load_bias(0)
            for c in range(4):
                load_chunk(0, c)
            with sp.Fori(0, GRP - 1) as pair:
                sp.wait_ge(bias_ready, pair * 2 + 2)
                load_bias(pair + 1)
                store_y(pair, 0)
                store_y(pair, 1)
                load_chunk(pair + 1, 0)
                store_y(pair, 2)
                load_chunk(pair + 1, 1)
                store_y(pair, 3)
                load_chunk(pair + 1, 2)
                load_chunk(pair + 1, 3)
            for c in range(4):
                store_y(GRP - 1, c)
            for s in range(2):
                sp.wait_ge(y_stored[s], 16 + 16 * 2 * GRP)

        @block.gpsimd
        def _(pool):
            pool.sem_inc(wo_done, 2)
            with pool.Fori(0, GRP) as pair:
                for g in range(2):
                    at = (slice(None), slice(None), bass.ts(pair * 2 + g, P))
                    pool.wait_ge(raw_o_loaded[g], pair * 16 + 16)
                    nc.gpsimd.tensor_copy(wo_h[at], raw_o[g][:]).then_inc(wo_high, 1)
                    pool.wait_ge(wo_high, pair * 2 + g + 1)
                    nc.gpsimd.tensor_tensor(wo_l[at], raw_o[g][:], wo_h[at].bitcast(f32), ALU.subtract).then_inc(wo_done, 1)

        @block.scalar
        def _(act):
            def exponent(pair, t, h):
                n, s = key_tiles(t) * P, (2 * t + h) % 4
                act.wait_ge(biased, pair * 32 + 2 * t + h + 1 + 2)
                nc.scalar.activation(prob[s][:, 0:n], prob[s][:, 0:n], ACT.Exp, bias=low[:, s:s + 1],
                                     scale=-1.0, accum_out=den[:, s:s + 1]).then_inc(expd, 1)

            def copy_turned(pair, t, e):
                m = min(4, 2 * key_tiles(t) - 4 * e)
                act.wait_ge(pv_done, pair * PTILES + t + 1)
                act.wait_ge(turned, pair * PER + BANKS[t] + e + 1)
                nc.scalar.activation(pt[t % 2][:, 4 * e:4 * e + m, :],
                                     pt_ps[(BANKS[t] + e) % 3][:, 0:m, :], ACT.Copy).then_inc(pt_copied, 1)

            def steps(pair, first):
                act.wait_ge(wo_done, pair * 2 + 2)
                for g in range(2):
                    act.dma_start(raw_o[g][:], w_all[pair * 2 + (NGROUPS + g), :, :, :]).then_inc(raw_o_loaded[g], 16)
                for t in range(PTILES):
                    for h in range(2):
                        exponent(pair, t, h)
                    if t == 0 and first:
                        continue
                    before = (pair, t - 1) if t >= 1 else (pair - 1, PTILES - 1)
                    for e in range(turned_banks(before[1])):
                        copy_turned(*before, e)

            steps(0, True)
            with act.Fori(1, GRP) as pair:
                steps(pair, False)
            for e in range(turned_banks(PTILES - 1)):
                copy_turned(GRP - 1, PTILES - 1, e)

        @block.vector
        def _(dve):
            dve.sem_inc(biased, 2)
            dve.sem_inc(pt_copied, 3)
            dve.sem_inc(y_ready, 1)
            def add_bias(pair, t, h):
                n, s = key_tiles(t) * P, (2 * t + h) % 4
                dve.wait_ge(scored, pair * 32 + 2 * t + h + 1)
                dve.nop(nofuse=True)
                if n > 512:
                    src = s_ps[h][:, :, 0:WIN // 2]
                    out, b = (a.rearrange("p (a b) -> p a b", a=2) for a in (prob[s][:], bias[:, h, :]))
                else:
                    src, out, b = s_ps[h][:, 0, 0:n], prob[s][:, 0:n], bias[:, h, WIN - n:WIN]
                nc.vector.tensor_tensor_reduce(out=out, in0=src, in1=b, scale=1.0, scalar=MASKED,
                                               op0=ALU.add, op1=ALU.min, accum_out=low[:, s:s + 1]).then_inc(biased, 1)

            def normalise(pair, t, h):
                n, s = key_tiles(t) * P, (2 * t + h) % 4
                dve.wait_ge(expd, pair * 32 + 2 * t + h + 1)
                nc.vector.reciprocal(rden[:, s:s + 1], den[:, s:s + 1]).then_inc(rden_ready, 1)
                dve.wait_ge(rden_ready, pair * 32 + 2 * t + h + 1)
                nc.vector.tensor_scalar(prob[s][:, 0:n], prob[s][:, 0:n], rden[:, s:s + 1], None,
                                        ALU.mult).then_inc(normed, 1)

            def gate(pair, t):
                c = t // 4
                if t % 4 == 0:
                    dve.wait_ge(y_stored[c % 2], pair * 32 + 16 * (c // 2) + 16)
                dve.wait_ge(pv_done, pair * PTILES + t + 1 + 2)
                nc.vector.scalar_tensor_tensor(
                    out=yst[c % 2][:, (t % 4) * P:(t % 4 + 1) * P], in0=o_ps[:, 0:P], scalar=0.5,
                    in1=z[:, t * P:(t + 1) * P], op0=ALU.mult, op1=ALU.mult).then_inc(y_ready, 1)

            nc.vector.memset(bias[HD:P, :, 0:HD], MASKED).then_inc(masked, 1)
            nc.vector.memset(bias[0:HD, :, WIN - HD:WIN], MASKED).then_inc(masked, 1)
            dve.wait_ge(masked, 2)
            def steps(pair, first):
                dve.wait_ge(bias_loaded, pair * 16 + 16)
                nc.vector.tensor_copy(bias[0:HD, :, 0:WIN - HD], bias_next[0:HD, :, 0:WIN - HD]).then_inc(bias_ready, 1)
                nc.vector.tensor_copy(bias[HD:P, :, HD:WIN], bias_next[HD:P, :, HD:WIN]).then_inc(bias_ready, 1)
                dve.wait_ge(bias_ready, pair * 2 + 2)
                for t in range(PTILES):
                    for h in range(2):
                        add_bias(pair, t, h)
                    for h in range(2):
                        normalise(pair, t, h)
                    if t >= 2:
                        gate(pair, t - 2)
                    elif not first:
                        gate(pair - 1, PTILES - 2 + t)

            steps(0, True)
            with dve.Fori(1, GRP) as pair:
                steps(pair, False)
            gate(GRP - 1, PTILES - 2)
            gate(GRP - 1, PTILES - 1)

        @block.tensor
        def _(pe):
            pe.sem_inc(pv_done, 2)

            def scores(pair, t):
                k0, n = (t + 1 - key_tiles(t)) * P, key_tiles(t) * P
                halves = [(0, 0, n)] if n <= 512 else [(0, 0, n // 2), (1, n // 2, n // 2)]
                if t % 4 == 0:
                    pe.wait_ge(chunk_loaded[t // 4], (pair + 1) * (16 * CHUNK_DMAS))
                for h in range(2):
                    pe.wait_ge(biased, pair * 32 + 2 * t + h + 1)
                    for b, at, m in halves:
                        for part in range(2):
                            last = nc.tensor.matmul(s_ps[h][:, b, 0:m], q[:, h, part, t * P:(t + 1) * P],
                                                    k[:, h, k0 + at:k0 + at + m], start=part == 0, stop=part == 1)
                    last.then_inc(scored, 1)

            def turn(pair, t):
                pe.wait_ge(normed, pair * 32 + 2 * t + 2)
                for e in range(turned_banks(t)):
                    pe.wait_ge(pt_copied, pair * PER + BANKS[t] + e + 1)
                    for i in range(4 * e, min(4 * e + 4, 2 * key_tiles(t))):
                        b, h = i // 2, i % 2
                        last = nc.tensor.transpose(pt_ps[(BANKS[t] + e) % 3][:, i - 4 * e, :],
                                                   prob[(2 * t + h) % 4][:, b * P:(b + 1) * P], ident[:])
                    last.then_inc(turned, 1)

            def weigh(pair, t):
                nk = key_tiles(t)
                pe.wait_ge(pt_copied, pair * PER + BANKS[t + 1] + 3)
                pe.wait_ge(y_ready, pair * PTILES + t + 1)
                for b in range(nk):
                    for h in range(2):
                        last = nc.tensor.matmul(o_ps[64 * h:64 * h + 64, 0:P],
                                                v[:, t + 1 - nk + b, 64 * h:64 * h + 64], pt[t % 2][:, 2 * b + h, :],
                                                start=b == 0, stop=b == nk - 1, skip_group_check=True)
                last.then_inc(pv_done, 1)

            def steps(pair, first):
                for t in range(PTILES):
                    scores(pair, t)
                    if t >= 2:
                        weigh(pair, t - 2)
                    elif not first:
                        weigh(pair - 1, PTILES - 2 + t)
                    if t >= 1:
                        turn(pair, t - 1)
                    elif not first:
                        turn(pair - 1, PTILES - 1)

            steps(0, True)
            with pe.Fori(1, GRP) as pair:
                steps(pair, False)
            weigh(GRP - 1, PTILES - 2)
            turn(GRP - 1, PTILES - 1)
            weigh(GRP - 1, PTILES - 1)


def output_projection(nc, x, ln_g, ln_b, cache_k, cache_v, s_z, s_y, s_skew, v_all, y_out, ident, qs, ks, wo_h, wo_l):
    f32, f32r = mybir.dt.float32, mybir.dt.float32r
    ALU = mybir.AluOpType
    ACT = mybir.ActivationFunctionType

    ctx = ExitStack()
    with ctx:
        def sb(name, shape, dt=f32):
            return ctx.enter_context(nc.sbuf_tensor(name, shape, dt))

        def sem(name):
            return ctx.enter_context(nc.semaphore(name))

        yr = [sb(f"yr{s}", [P, KC, P]) for s in range(2)]
        yh = [sb(f"yh{s}", [P, KC, P], f32r) for s in range(2)]
        yl = [sb(f"yl{s}", [P, KC, P], f32r) for s in range(2)]
        xt = [sb(f"xt{s}", [P, D]) for s in range(2)]
        r = [sb(f"r{s}", [P, D]) for s in range(2)]
        gain = sb("gain", [P, D])
        offset = sb("offset", [P, D])
        stats = sb("stats_o", [P, 2, 6])
        mv = sb("mv_o", [P, 2])
        rstd = sb("rstd_o", [P, 1])
        minus_half = sb("minus_half", [P, 1])
        eps = sb("eps_o", [P, 1])
        kc = sb("kc", [PAST, 512])
        vc = sb("vc", [PAST, 512])
        vnew = sb("vnew", [SN, 512])
        kt = sb("kt", [P, GRP, SKEYS])
        qd = sb("qd", [P, GRP, 2 * SN])
        sbias = sb("sbias", [P, SKEYS])
        sprob = sb("sprob", [P, SKEYS])
        slow = sb("slow", [P, 1])
        sden = sb("sden", [P, 1])
        srden = sb("srden", [P, 1])
        spt = sb("spt", [P, 2, P])
        zs = sb("zs", [P, GRP, P])
        ys = sb("ys", [P, GRP, P])

        out_ps = [ctx.enter_context(nc.psum_tensor(f"out_ps{b}", [P, 512], f32)) for b in range(4)]
        kt_ps = ctx.enter_context(nc.psum_tensor("kt_ps", [P, GRP, P], f32))
        ss_ps = ctx.enter_context(nc.psum_tensor("ss_ps", [P, 512], f32))
        spt_ps = ctx.enter_context(nc.psum_tensor("spt_ps", [P, 4, P], f32))
        so_ps = ctx.enter_context(nc.psum_tensor("so_ps", [P, 512], f32))

        par_loaded = sem("par_loaded_o")
        z_loaded = sem("z_loaded")
        sbias_loaded = sem("sbias_loaded")
        y_loaded = [sem(f"y_loaded{s}") for s in range(2)]
        xt_loaded = [sem(f"xt_loaded{s}") for s in range(2)]
        y_high = sem("y_high")
        y_split = sem("y_split")
        out_done = sem("out_done")
        out_read = sem("out_read")
        half_stats = sem("half_stats")
        mv_ready = sem("mv_ready_o")
        var_eps = sem("var_eps_o")
        rstd_ready = sem("rstd_ready_o")
        centred = sem("centred")
        gained = sem("gained")
        r_ready = sem("r_ready")
        r_stored = [sem(f"r_stored{s}") for s in range(2)]
        const_ready = sem("const_ready_o")
        kv_loaded = sem("kv_loaded")
        kc_turned = sem("kc_turned")
        kt_ready = sem("kt_ready")
        q_ready = sem("q_ready")
        s_scored = sem("s_scored")
        s_biased = sem("s_biased")
        s_expd = sem("s_expd")
        s_rden = sem("s_rden")
        s_normed = sem("s_normed")
        s_turned = sem("s_turned")
        s_pt = sem("s_pt")
        s_weighed = sem("s_weighed")
        ys_ready = sem("ys_ready")
        ys_stored = sem("ys_stored")

        block = ctx.enter_context(nc.Block())

        @block.sync
        def _(sp):
            for s in range(2):
                sp.sem_inc(r_stored[s], 16)

            def load_y(tile, s):
                sp.dma_start(yr[s][:], s_y[:, :, bass.ts(tile, P)].rearrange("k c t -> c k t")).then_inc(y_loaded[s], 16)

            def load_x(tile, s):
                sp.dma_start(xt[s][:], x[bass.ts(tile, P), :]).then_inc(xt_loaded[s], 16)

            def load_stream(b):
                sp.dma_start(kc[:], cache_k[b, :, :]).then_inc(kv_loaded, 16)
                sp.dma_start(vc[:], cache_v[b, :, :]).then_inc(kv_loaded, 16)
                sp.dma_start(vnew[:], v_all[bass.ds(b * SN + SEQ, SN), :]).then_inc(kv_loaded, 16)

            def store_tile(tile, s, count):
                sp.wait_ge(r_ready, count)
                sp.dma_start(y_out[bass.ts(tile, P), :], r[s][:]).then_inc(r_stored[s], 16)

            for s in range(2):
                load_y(s, s)
                load_x(s, s)
            load_stream(0)
            sp.dma_start(gain[:], ln_g.partition_broadcast(P)).then_inc(par_loaded, 16)
            sp.dma_start(offset[:], ln_b.partition_broadcast(P)).then_inc(par_loaded, 16)
            sp.dma_start(zs[:], s_z[:, :, SEQ:T].rearrange("g c t -> c g t")).then_inc(z_loaded, 16)
            for h in range(HEADS):
                src = skewed(s_skew, slice(h, h + 1), SN, PAST, SKEYS)[:, 0, :]
                sp.dma_start(sbias[h * SN:(h + 1) * SN, :], src).then_inc(sbias_loaded, 16)
            with sp.Fori(0, SB - 1) as i:
                for s in range(2):
                    sp.wait_ge(y_split, i * 2 + s + 1)
                    load_y(i * 2 + 2 + s, s)
                for s in range(2):
                    sp.wait_ge(out_read, i * 4 + 2 * s + 2 + 4)
                    load_x(i * 2 + 2 + s, s)
                    store_tile(i * 2 + s, s, i * 2 + s + 1)
                    if s == 0:
                        sp.wait_ge(ys_ready, i * 2 + 2)
                        load_stream(i + 1)
            sp.wait_ge(ys_ready, 2 * SB)
            sp.dma_start(s_y[GRP:2 * GRP, :, SEQ:T].rearrange("g c t -> c g t"), ys[:]).then_inc(ys_stored, 16)
            sp.wait_ge(ys_stored, 16)
            sp.wait_ge(y_split, PTILES - 1)
            load_y(TILES - 1, 0)
            sp.wait_ge(out_read, 2 * (PTILES - 1) + 4)
            load_x(TILES - 1, 0)
            store_tile(PTILES - 2, 0, PTILES - 1)
            store_tile(PTILES - 1, 1, PTILES)
            store_tile(TILES - 1, 0, TILES)
            sp.wait_ge(r_stored[0], 16 * (SB + 2))
            sp.wait_ge(r_stored[1], 16 * (SB + 1))

        @block.gpsimd
        def _(pool):
            nc.gpsimd.memset(minus_half[:], -0.5).then_inc(const_ready, 1)
            nc.gpsimd.memset(eps[:], EPS).then_inc(const_ready, 1)
            nc.gpsimd.memset(qd[:], 0.0).then_inc(const_ready, 1)
            pool.wait_ge(const_ready, 3)
            pool.wait_ge(par_loaded, 32)

            def finish(n, s):
                pool.wait_ge(mv_ready, n + 1)
                nc.gpsimd.tensor_tensor(rstd[:], mv[:, 1:2], eps[:], ALU.add).then_inc(var_eps, 1)
                pool.wait_ge(var_eps, n + 1)
                nc.gpsimd.tensor_tensor(rstd[:], rstd[:], minus_half[:], ALU.pow).then_inc(rstd_ready, 1)
                pool.wait_ge(centred, n + 1)
                nc.gpsimd.tensor_tensor(r[s][:], r[s][:], gain[:], ALU.mult).then_inc(gained, 1)
                pool.wait_ge(gained, n + 1)
                nc.gpsimd.tensor_tensor(r[s][:], r[s][:], offset[:], ALU.add).then_inc(r_ready, 1)

            with pool.Fori(0, SB) as i:
                for s in range(2):
                    finish(i * 2 + s, s)
            finish(PTILES, 0)

        @block.scalar
        def _(act):
            def high(n, s, loads):
                act.wait_ge(y_loaded[s], loads)
                act.wait_ge(out_done, n * 2 + 2)
                nc.scalar.activation(yh[s][:], yr[s][:], ACT.Copy).then_inc(y_high, 1)

            def stream(i, stage):
                if stage == 0:
                    act.wait_ge(kc_turned, i + 1)
                    nc.scalar.activation(kt[:, :, 0:PAST], kt_ps[:], ACT.Copy).then_inc(kt_ready, 1)
                if stage == 1:
                    act.wait_ge(s_biased, i + 1)
                    nc.scalar.activation(sprob[:], sprob[:], ACT.Exp, bias=slow[:], scale=-1.0,
                                         accum_out=sden[:]).then_inc(s_expd, 1)
                if stage == 2:
                    act.wait_ge(s_turned, i + 1)
                    nc.scalar.activation(spt[:, 0, :], spt_ps[:, 0, :], ACT.Copy).then_inc(s_pt, 1)
                    nc.scalar.activation(spt[0:SN, 1, :], spt_ps[0:SN, 1, :], ACT.Copy).then_inc(s_pt, 1)

            high(0, 0, 16)
            with act.Fori(0, SB) as i:
                stream(i, 0)
                high(i * 2 + 1, 1, i * 16 + 16)
                stream(i, 1)
                stream(i, 2)
                high(i * 2 + 2, 0, i * 16 + 32)

        @block.vector
        def _(dve):
            dve.sem_inc(out_read, 4)

            def low(n, s):
                dve.wait_ge(y_high, n + 1)
                nc.vector.tensor_tensor(yl[s][:], yr[s][:], yh[s][:].bitcast(f32), ALU.subtract).then_inc(y_split, 1)

            def residual(n, s, h, loads, stores):
                dve.wait_ge(out_done, n * 2 + h + 1 + 4)
                if h == 0:
                    dve.wait_ge(xt_loaded[s], loads)
                    dve.wait_ge(r_stored[s], stores)
                at = slice(512 * h, 512 * h + 512)
                nc.vector.scalar_tensor_tensor(out=r[s][:, at], in0=xt[s][:, at], scalar=ALPHA, in1=out_ps[2 * s + h][:],
                                               op0=ALU.mult, op1=ALU.add).then_inc(out_read, 1)
                dve.wait_ge(out_read, n * 2 + h + 1 + 4)
                nc.vector.bn_stats(stats[:, h, :], r[s][:, at]).then_inc(half_stats, 1)

            def centre(n, s):
                dve.wait_ge(half_stats, n * 2 + 2)
                dve.nop(nofuse=True)
                nc.vector.bn_aggr(mv[:], stats[:].rearrange("p h n -> p (h n)")).then_inc(mv_ready, 1)
                dve.wait_ge(rstd_ready, n + 1)
                nc.vector.tensor_scalar(r[s][:], r[s][:], mv[:, 0:1], rstd[:], ALU.subtract, ALU.mult).then_inc(centred, 1)

            def stream(i, stage):
                at = bass.ts(i, SN)
                if stage == 0:
                    nc.vector.tensor_copy(kt[:, :, PAST:SKEYS], ks[:, :, at]).then_inc(q_ready, 1)
                    nc.vector.tensor_copy(qd[0:HD, :, 0:SN], qs[0:HD, :, at]).then_inc(q_ready, 1)
                    nc.vector.tensor_copy(qd[HD:P, :, SN:2 * SN], qs[HD:P, :, at]).then_inc(q_ready, 1)
                if stage == 1:
                    dve.wait_ge(s_scored, i + 1)
                    dve.nop(nofuse=True)
                    nc.vector.tensor_tensor_reduce(out=sprob[:], in0=ss_ps[:, 0:SKEYS], in1=sbias[:], scale=1.0,
                                                   scalar=MASKED, op0=ALU.add, op1=ALU.min,
                                                   accum_out=slow[:]).then_inc(s_biased, 1)
                    dve.wait_ge(s_expd, i + 1)
                    nc.vector.reciprocal(srden[:], sden[:]).then_inc(s_rden, 1)
                    dve.wait_ge(s_rden, i + 1)
                    nc.vector.tensor_scalar(sprob[:], sprob[:], srden[:], None, ALU.mult).then_inc(s_normed, 1)
                if stage == 3:
                    dve.wait_ge(s_weighed, i + 1)
                    o = so_ps[:, 0:GRP * 2 * SN].rearrange("p (g t) -> p g t", g=GRP)
                    for h in range(2):
                        rows = slice(HD * h, HD * h + HD)
                        nc.vector.scalar_tensor_tensor(out=ys[rows, :, at], in0=o[rows, :, SN * h:SN * h + SN], scalar=0.5,
                                                       in1=zs[rows, :, at], op0=ALU.mult, op1=ALU.mult).then_inc(ys_ready, 1)

            dve.wait_ge(const_ready, 3)
            dve.wait_ge(sbias_loaded, 16 * HEADS)
            dve.wait_ge(z_loaded, 16)
            low(0, 0)
            with dve.Fori(0, SB) as i:
                stream(i, 0)
                low(i * 2 + 1, 1)
                residual(i * 2, 0, 0, i * 16 + 16, i * 16 + 16)
                stream(i, 1)
                residual(i * 2, 0, 1, None, None)
                centre(i * 2, 0)
                residual(i * 2 + 1, 1, 0, i * 16 + 16, i * 16 + 16)
                stream(i, 3)
                low(i * 2 + 2, 0)
                residual(i * 2 + 1, 1, 1, None, None)
                centre(i * 2 + 1, 1)
            for h in range(2):
                residual(PTILES, 0, h, 16 * (SB + 1), 16 * (SB + 1))
            centre(PTILES, 0)

        @block.tensor
        def _(pe):
            pe.sem_inc(out_done, 4)

            def project(n, s, h):
                if h == 0:
                    pe.wait_ge(y_split, n + 1)
                pe.wait_ge(out_read, n * 2 + h + 1)
                for c in range(KC):
                    for a, (y, w) in enumerate(((yh, wo_h), (yh, wo_l), (yl, wo_h))):
                        last = nc.tensor.matmul(out_ps[2 * s + h][:], y[s][:, c, :], w[:, c, 512 * h:512 * h + 512],
                                                start=c == 0 and a == 0, stop=c == KC - 1 and a == 2)
                last.then_inc(out_done, 1)

            def stream(i, stage):
                if stage == 0:
                    pe.wait_ge(kv_loaded, i * 48 + 48)
                    for p in range(GRP):
                        last = nc.tensor.transpose(kt_ps[:, p, :], kc[:, p * P:(p + 1) * P], ident[:])
                    last.then_inc(kc_turned, 1)
                if stage == 1:
                    pe.wait_ge(kt_ready, i + 1)
                    pe.wait_ge(q_ready, i * 3 + 3)
                    for p in range(GRP):
                        last = nc.tensor.matmul(ss_ps[2 * SN * p:2 * SN * (p + 1), 0:SKEYS], qd[:, p, :], kt[:, p, :],
                                                start=True, stop=True)
                    last.then_inc(s_scored, 1)
                if stage == 2:
                    pe.wait_ge(s_normed, i + 1)
                    nc.tensor.transpose(spt_ps[:, 0, :], sprob[:, 0:PAST], ident[:])
                    nc.tensor.transpose(spt_ps[0:SN, 1, :], sprob[:, PAST:SKEYS], ident[:]).then_inc(s_turned, 1)
                if stage == 3:
                    pe.wait_ge(s_pt, i * 2 + 2)
                    for p in range(GRP):
                        cols = slice(2 * SN * p, 2 * SN * (p + 1))
                        nc.tensor.matmul(so_ps[:, cols], vc[:, p * P:(p + 1) * P], spt[:, 0, cols], start=True, stop=False)
                        last = nc.tensor.matmul(so_ps[:, cols], vnew[:, p * P:(p + 1) * P], spt[0:SN, 1, cols],
                                                start=False, stop=True)
                    last.then_inc(s_weighed, 1)

            with pe.Fori(0, SB) as i:
                for e in range(4):
                    stream(i, e)
                    project(i * 2 + e // 2, e // 2, e % 2)
            for h in range(2):
                project(PTILES, 0, h)


def lay_out(x_prompt, x_sample, cache_k, cache_v, w_in, w_sgu, b_sgu, ln_v_g, ln_v_b, rel_bias, w_out, ln_g, ln_b):
    c = np.ascontiguousarray
    w_in, w_out = np.asarray(w_in)[0], np.asarray(w_out)[0]
    base = {"u": 0, "va": 512, "za": 1024, "q": 1536, "k": 2048, "v": 2560, "z": 3072}
    first = [base[kind] + (2 * i + h) * P for i in range(LOOP_A) for kind, h in GELU_GROUPS]
    first += [base[kind] + p * P for p in range(LOOP_B) for kind in PAIR_GROUPS]
    groups = [w_in[:, f:f + P] for f in first] + [w_out[:, n * P:(n + 1) * P] for n in range(KC)]
    w_all = np.stack([g.reshape(KC, P, P).transpose(1, 0, 2) for g in groups])
    return {
        "x": c(np.concatenate([np.asarray(x_prompt).reshape(SEQ, D), np.asarray(x_sample).reshape(SB * SN, D)])),
        "w_all": c(w_all),
        "w_sgu": c(np.asarray(w_sgu)[0]), "b_sgu": c(np.asarray(b_sgu).reshape(-1)),
        "ln_v_g": c(np.asarray(ln_v_g)[0]), "ln_v_b": c(np.asarray(ln_v_b)[0]),
        "rel_rev": c(np.asarray(rel_bias)[0][:, ::-1]),
        "ln_g": c(np.asarray(ln_g)[0]), "ln_b": c(np.asarray(ln_b)[0]),
        "cache_k": c(np.asarray(cache_k).reshape(SB, PAST, HEADS * HD)),
        "cache_v": c(np.asarray(cache_v).reshape(SB, PAST, HEADS * HD)),
    }


def kernel(x_prompt, x_sample, cache_k, cache_v, w_in, w_sgu, b_sgu, ln_v_g, ln_v_b, rel_bias, w_out, ln_g, ln_b):
    import concourse.bacc as bacc
    from concourse.bass_utils import run_bass_kernel_spmd

    arrays = lay_out(x_prompt, x_sample, cache_k, cache_v, w_in, w_sgu, b_sgu, ln_v_g, ln_v_b, rel_bias, w_out,
                     ln_g, ln_b)
    nc = bacc.Bacc("TRN2", target_bir_lowering=False, num_devices=1)
    args = {n: nc.dram_tensor(n, a.shape, mybir.dt.from_np(a.dtype), kind="ExternalInput").ap()
            for n, a in arrays.items()}
    outs = {"y_out": (T, D), "v_all": (T, HEADS * HD), "k_tail": (T - SEQ + KEEP, HEADS * HD), "gv_out": (SB * SN, 512)}
    for n, shape in outs.items():
        args[n] = nc.dram_tensor(n, shape, mybir.dt.float32, kind="ExternalOutput").ap()
    hybrid_stream_step(nc, **args)
    r = run_bass_kernel_spmd(nc, [arrays], core_ids=[0]).results[0]
    y, v, k, gv = r["y_out"], r["v_all"], r["k_tail"], r["gv_out"]
    heads = (HEADS, HD)
    return (y[:SEQ].reshape(1, SEQ, D), y[SEQ:].reshape(SB, SN, D),
            k[:KEEP].reshape(1, 1, KEEP, *heads), v[SEQ - KEEP:SEQ].reshape(1, 1, KEEP, *heads),
            k[KEEP:].reshape(1, SB, SN, *heads), v[SEQ:].reshape(1, SB, SN, *heads),
            gv.reshape(1, SB, SN, 512))
```

```python
import numpy as np
import concourse.bass as bass
from concourse import mybir
from contextlib import ExitStack

P = 128
D = 1024
KC = D // P
SEQ = 2048
SB, SN = 8, 16
T = SEQ + SB * SN
TILES = T // P
PTILES = SEQ // P
GRP = 4
HD = 64
HEADS = 8
PAST = 128
SKEYS = PAST + SN
WIN = 640
CLIP = 128
REL = 6 * P
KEEP = 512
NGROUPS = 28
CHUNKS = [(0, 512), (512, 512), (1024, 384), (1408, 384), (1792, 384)]
NCH = len(CHUNKS)
ALPHA = 2.0 ** 0.25
EPS = 1e-5
QSCALE = -(HD ** -0.5)
MASKED = 3.0e38

GATE_GROUPS = ["u", "za"]
PAIR_GROUPS = ["q", "k", "v", "z"]
LOOP_B = 4


def chunk_tiles(c):
    return list(range(CHUNKS[c][0] // P, (CHUNKS[c][0] + CHUNKS[c][1]) // P))


def opening():
    steps = [("turn", chunk_tiles(0)), ("project", 0, 0), ("turn", chunk_tiles(1)), ("project", 1, 0)]
    for c in range(1, NCH):
        ahead = chunk_tiles(c + 1) if c + 1 < NCH else []
        steps += [("turn", ahead[:2]), ("project", 0, c), ("turn", ahead[2:]), ("project", 1, c)]
    return steps


XSLOTS = 4


STORED_B = [16 * GRP * len(range(s, NCH, 2)) for s in range(2)]
ALL_STORED_B = [16 + n + 16 * 2 * NCH * LOOP_B for n in STORED_B]


def hybrid_stream_step(nc, x, w_all, w_sgu, b_sgu, ln_v_g, ln_v_b, rel_rev, ln_g, ln_b,
                       cache_k, cache_v, y_out, v_all, k_tail, gv_out):
    f32, f32r = mybir.dt.float32, mybir.dt.float32r
    ALU = mybir.AluOpType
    ACT = mybir.ActivationFunctionType

    ctx = ExitStack()
    with ctx:
        def dram(name, shape, dt=f32):
            return nc.dram_tensor(name, shape, dt).ap()

        s_gate = dram("s_gate", [GRP, P, T])
        s_va = dram("s_va", [GRP, P, T])
        s_q = dram("s_q", [2, GRP, P, SEQ])
        s_k = dram("s_k", [2, GRP, P, SEQ])
        s_z = dram("s_z", [GRP, P, T])
        s_y = dram("s_y", [2 * GRP, P, T])
        s_rel = dram("s_rel", [HEADS, REL])
        s_skew = dram("s_skew", [HEADS, P, REL + 1])

        outer = ctx.enter_context(ExitStack())

        def sb(stack, name, shape, dt=f32):
            return stack.enter_context(nc.sbuf_tensor(name, shape, dt))

        ident = sb(outer, "ident", [P, P])
        big = sb(outer, "big", [P, T])
        par = sb(outer, "par", [P, 4 * 512])
        st_b = [sb(outer, f"st_b{s}", [P, 512]) for s in range(2)]
        bias_next = sb(outer, "bias_next", [P, 2 * WIN])
        wts = sb(outer, "wts", [P, GRP, P])
        minus_half = sb(outer, "minus_half", [P, 1])
        eps = sb(outer, "eps", [P, 1])
        qs = sb(outer, "qs", [P, GRP, P])
        ks = sb(outer, "ks", [P, GRP, P])

        bias_loaded = ctx.enter_context(nc.semaphore("bias_loaded"))
        st_b_stored = [ctx.enter_context(nc.semaphore(f"st_b_stored{s}")) for s in range(2)]
        input_projection(nc, x, w_all, w_sgu, b_sgu, ln_v_g, ln_v_b, rel_rev, s_gate, s_va, s_q, s_k, s_z, s_y,
                         s_rel, s_skew, v_all, k_tail, ident, big, par, bias_next, wts, minus_half, eps, qs, ks, st_b,
                     bias_loaded, st_b_stored)
        wo_h = sb(outer, "wo_h", [P, KC, D], mybir.dt.float32r)
        wo_l = sb(outer, "wo_l", [P, KC, D], mybir.dt.float32r)
        yh = [sb(outer, "yh0", [P, KC, P], mybir.dt.float32r)]
        yl = [sb(outer, "yl0", [P, KC, P], mybir.dt.float32r)]
        kc = sb(outer, "kc", [PAST, 512])
        k_loaded = ctx.enter_context(nc.semaphore("k_loaded"))
        y_loaded = [ctx.enter_context(nc.semaphore(f"y_loaded{s}")) for s in range(2)]
        xt_loaded = [ctx.enter_context(nc.semaphore(f"xt_loaded{s}")) for s in range(2)]
        y_high = ctx.enter_context(nc.semaphore("y_high"))
        y_split = ctx.enter_context(nc.semaphore("y_split"))
        y_stored = [ctx.enter_context(nc.semaphore(f"y_stored{s}")) for s in range(2)]
        attention(nc, x, cache_k, w_all, s_q, s_k, s_z, s_y, s_skew, v_all, gv_out, ident, big, par, bias_next, wts,
                  minus_half, eps, bias_loaded, st_b, st_b_stored, wo_h, wo_l, yh, yl, y_loaded, xt_loaded,
                  y_high, y_split, y_stored, kc, k_loaded)
        output_projection(nc, x, ln_g, ln_b, cache_k, cache_v, s_z, s_y, s_skew, v_all, y_out, ident, big, par,
                          minus_half, eps, qs, ks, wo_h, wo_l, yh, yl, y_loaded, xt_loaded, y_high, y_split, y_stored, kc, k_loaded)


def input_projection(nc, x, w_all, w_sgu, b_sgu, ln_v_g, ln_v_b, rel_rev, s_gate, s_va, s_q, s_k, s_z, s_y,
                     s_rel, s_skew, v_all, k_tail, ident, big, par, bias_next, wts, minus_half, eps, qs, ks, st_b,
                     bias_loaded, st_b_stored):
    f32, f32r = mybir.dt.float32, mybir.dt.float32r
    ALU = mybir.AluOpType
    ACT = mybir.ActivationFunctionType

    ctx = ExitStack()
    with ctx:
        def sb(name, shape, dt=f32):
            return ctx.enter_context(nc.sbuf_tensor(name, shape, dt))

        def sem(name):
            return ctx.enter_context(nc.semaphore(name))

        xh = sb("xh", [P, KC, T], f32r)
        xl = sb("xl", [P, KC, T], f32r)
        raw = [sb(f"raw{s}", [P, KC, P]) for s in range(2)]
        wh = [sb(f"wh{s}", [P, KC, P], f32r) for s in range(2)]
        wl = [sb(f"wl{s}", [P, KC, P], f32r) for s in range(2)]
        x_in = [buf[:, s * D:(s + 1) * D] for buf in (big, par) for s in range(2)]
        lnvg, lnvb = par[:, 0:512], par[:, 512:1024]
        bs, bss = (par[:, a:a + 512].rearrange("p (g t) -> p g t", g=GRP) for a in (1024, 1536))
        va_t = big[:, 0:512].rearrange("p (g t) -> p g t", g=GRP)
        gate_t = big[:, 512:1024].rearrange("p (g t) -> p g t", g=GRP)
        vn = big[:, 1024:1536]
        ya = big[:, 1536:2048].rearrange("p (g t) -> p g t", g=GRP)
        st_a = [sb(f"st_a{s}", [P, 512]) for s in range(2)]
        kf = bias_next[:, 0:640]
        kn = bias_next[:, 640:1024].rearrange("p (n c) -> p n c", n=3)
        vt = sb("vt", [P, 512])
        wt = sb("wt", [P, GRP, P])
        stats = sb("stats", [P, 6])
        mv = sb("mv", [P, 2])
        rstd = sb("rstd", [P, 1])

        bank = [ctx.enter_context(nc.psum_tensor(f"bank{c}", [P, 512], f32)) for c in range(NCH)]
        tg_ps = ctx.enter_context(nc.psum_tensor("tg_ps", [P, 512], f32))
        tv_ps = ctx.enter_context(nc.psum_tensor("tv_ps", [P, 512], f32))
        mix_ps = ctx.enter_context(nc.psum_tensor("mix_ps", [P, 512], f32))

        par_loaded = sem("par_loaded")
        blocks_loaded = sem("blocks_loaded")
        const_ready = sem("const_ready")
        zeroed = sem("zeroed")
        wt_turned = sem("wt_turned")
        wt_ready = sem("wt_ready")
        bss_ready = sem("bss_ready")
        rel_loaded = sem("rel_loaded")
        rel_filled = sem("rel_filled")
        rel_negated = sem("rel_negated")
        rel_stored = sem("rel_stored")
        x_loaded = [sem(f"x_loaded{s}") for s in range(XSLOTS)]
        x_turned = sem("x_turned")
        xh_done = sem("xh_done")
        xbank_free = sem("xbank_free")
        raw_loaded = [sem(f"raw_loaded{s}") for s in range(2)]
        wh_done = sem("wh_done")
        w_ready = sem("w_ready")
        proj_done = sem("proj_done")
        evac = [sem(f"evac{c}") for c in range(NCH)]
        act_read = sem("act_read")
        gate_full = sem("gate_full")
        st_a_stored = [sem(f"st_a_stored{s}") for s in range(2)]
        kf_full = sem("kf_full")
        tv_done = sem("tv_done")
        tv_copied = sem("tv_copied")
        kn_stored = sem("kn_stored")
        va_loaded = sem("va_loaded")
        gate_loaded = sem("gate_loaded")
        tg_done = sem("tg_done")
        tg_read = sem("tg_read")
        stats_ready = sem("stats_ready")
        mv_ready = sem("mv_ready")
        var_eps = sem("var_eps")
        rstd_ready = sem("rstd_ready")
        vn_step = sem("vn_step")
        vn_ready = sem("vn_ready")
        mix_done = sem("mix_done")
        mix_read = sem("mix_read")
        ya_full = sem("ya_full")
        ya_stored = sem("ya_stored")

        block = ctx.enter_context(nc.Block())

        A_J, B_J = len(GATE_GROUPS), len(PAIR_GROUPS)
        N_A = GRP + GRP * A_J
        HALVES = 2 * TILES
        STORED_A = [16 * GRP * NCH // 2] * 2
        x_banks = [tg_ps, tv_ps, mix_ps]

        @block.sync
        def _(sp):
            for s in range(2):
                sp.sem_inc(st_a_stored[s], 16)
                sp.sem_inc(st_b_stored[s], 16)
            sp.sem_inc(kn_stored, 16)
            sp.sem_inc(ya_stored, 16)

            def load_x(tile):
                s = tile % XSLOTS
                sp.dma_start(x_in[s], x[bass.ts(tile, P), :]).then_inc(x_loaded[s], 16)

            def store_va(g, c, e):
                t0, n = CHUNKS[c]
                sp.wait_ge(evac[c], g + 2)
                sp.dma_start(s_va[g, :, t0:t0 + n], st_a[e % 2][:, 0:n]).then_inc(st_a_stored[e % 2], 16)

            for tile in range(XSLOTS):
                load_x(tile)
            sp.dma_start(wt[:], w_sgu.rearrange("g t s -> t g s")).then_inc(par_loaded, 16)
            sp.wait_ge(zeroed, 1)
            for b in range(SB):
                sp.dma_start(wts[b * SN:(b + 1) * SN, :, b * SN:(b + 1) * SN],
                             w_sgu[:, 0:SN, 0:SN].rearrange("g t s -> t g s")).then_inc(blocks_loaded, 16)
            sp.dma_start(kf[0:HEADS, 0:2 * CLIP + 1], rel_rev).then_inc(rel_loaded, 16)
            e = 0
            for step in opening():
                if step[0] == "turn":
                    for tile in step[1]:
                        if tile + XSLOTS < TILES:
                            sp.wait_ge(x_turned, 2 * tile + 2)
                            load_x(tile + XSLOTS)
                else:
                    store_va(step[1], step[2], e)
                    e += 1
            sp.wait_ge(x_turned, 2 * TILES)
            sp.dma_start(lnvg, ln_v_g.partition_broadcast(P)).then_inc(par_loaded, 16)
            sp.dma_start(lnvb, ln_v_b.partition_broadcast(P)).then_inc(par_loaded, 16)
            sp.dma_start(par[:, 1024:1536], b_sgu.partition_broadcast(P)).then_inc(par_loaded, 16)

            sp.wait_ge(rel_negated, 2)
            flat = REL - (2 * CLIP + 1)
            sp.dma_start(s_rel[:, 0:flat], vt[0:HEADS, 0:flat]).then_inc(rel_stored, 16)
            sp.dma_start(s_rel[:, flat:REL], kf[0:HEADS, 0:2 * CLIP + 1]).then_inc(rel_stored, 16)
            sp.wait_ge(rel_stored, 32)
            for h in range(HEADS):
                sp.dma_start(s_skew[h, :, 0:REL], s_rel[h, :].partition_broadcast(P)).then_inc(rel_stored, 16)

            for g in (2, 3):
                for c in range(NCH):
                    store_va(g, c, g * NCH + c)
            with sp.Fori(0, GRP) as i:
                for c, (t0, n) in enumerate(CHUNKS):
                    sp.wait_ge(gate_full, i * NCH + c + 1 + NCH)
                    sp.dma_start(s_gate[i, :, t0:t0 + n], st_b[c % 2][:, 0:n]).then_inc(st_b_stored[c % 2], 16)

            def load_gmlp(tile):
                sp.dma_start(va_t, s_va[:, :, bass.ts(tile, P)].rearrange("g c t -> c g t")).then_inc(va_loaded, 16)
                sp.dma_start(gate_t, s_gate[:, :, bass.ts(tile, P)].rearrange("g c t -> c g t")).then_inc(gate_loaded, 16)

            for s in range(2):
                sp.wait_ge(st_a_stored[s], 16 + STORED_A[s])
                sp.wait_ge(st_b_stored[s], 16 + STORED_B[s])
            load_gmlp(0)

            def store_kn(c, p):
                t0, nt = ((1536, 2), (1792, 3))[c]
                sp.wait_ge(tv_copied, p * 7 + c + 2)
                sp.dma_start(k_tail[t0 - 1536:t0 - 1536 + nt * P, bass.ts(p, P)].rearrange("(n t) c -> t n c", t=P),
                             kn[:, 0:nt, :]).then_inc(kn_stored, 16)

            def store_vn(c, p):
                t0, n = CHUNKS[c]
                sp.wait_ge(tv_copied, p * 7 + c + 4)
                sp.dma_start(v_all[t0:t0 + n, bass.ts(p, P)].rearrange("(n t) c -> t n c", t=P),
                             st_b[c % 2][:, 0:n].rearrange("t (n c) -> t n c", c=P)).then_inc(st_b_stored[c % 2], 16)

            with sp.Fori(0, LOOP_B) as p:
                for j, kind in enumerate(PAIR_GROUPS):
                    for c, (t0, n) in enumerate(CHUNKS):
                        m = min(n, SEQ - t0)
                        if c == NCH - 1:
                            sp.wait_ge(ya_full, p * 4 + j + 1)
                            sp.dma_start(s_y[0:GRP, :, bass.ts(p * 4 + j, P)].rearrange("g c t -> c g t"),
                                         ya).then_inc(ya_stored, 16)
                            load_gmlp(p * 4 + j + 1)
                        if kind in "qk":
                            e = 5 * j + c
                            dst = s_q if kind == "q" else s_k
                            sp.wait_ge(evac[c], N_A + p * B_J + j + 2)
                            sp.dma_start(dst[0, p, :, t0:t0 + m], st_a[e % 2][:, 0:m]).then_inc(st_a_stored[e % 2], 16)
                            sp.dma_start(dst[1, p, :, t0:t0 + m], st_b[e % 2][:, 0:m]).then_inc(st_b_stored[e % 2], 16)
                        if kind == "z":
                            if c == 0:
                                store_vn(4, p)
                            e = 15 + c
                            sp.wait_ge(evac[c], N_A + p * B_J + j + 2)
                            sp.dma_start(s_z[p, :, t0:t0 + n], st_b[e % 2][:, 0:n]).then_inc(st_b_stored[e % 2], 16)
                        if kind == "k" and c == 4:
                            store_kn(0, p)
                        if kind == "v":
                            if c == 0:
                                store_kn(1, p)
                            else:
                                store_vn(c - 1, p)

            sp.wait_ge(va_loaded, 16 * TILES)
            sp.wait_ge(gate_loaded, 16 * TILES)
            sp.wait_ge(ya_stored, 16 + 16 * PTILES)
            sp.wait_ge(kn_stored, 16 + 16 * 2 * LOOP_B)
            sp.wait_ge(rel_stored, 16 * (2 + HEADS))
            sp.dma_start(bias_next[:].rearrange("p (h j) -> p h j", h=2),
                         skewed(s_skew, slice(0, 2), P, WIN - P, WIN)).then_inc(bias_loaded, 16)
            for s in range(2):
                sp.wait_ge(st_a_stored[s], 16 + STORED_A[s] + 16 * 5 * LOOP_B)

        @block.gpsimd
        def _(pool):
            nc.gpsimd.memset(minus_half[:], -0.5).then_inc(const_ready, 1)
            nc.gpsimd.memset(eps[:], EPS).then_inc(const_ready, 1)
            nc.gpsimd.memset(ident[:], 1.0).then_inc(const_ready, 1)
            nc.gpsimd.memset(wts[:], 0.0).then_inc(zeroed, 1)
            nc.gpsimd.memset(vt[:], 0.0).then_inc(rel_filled, 1)
            pool.wait_ge(const_ready, 3)
            nc.gpsimd.affine_select(out=ident[:], in_=ident[:], compare_op=ALU.is_equal, fill=0.0, base=0,
                                    pattern=[[-1, P]], channel_multiplier=1).then_inc(const_ready, 1)
            for v, held, need in ((wt, par_loaded, 64), (wts, blocks_loaded, 16 * SB)):
                pool.wait_ge(held, need)
                nc.gpsimd.affine_select(out=v[:], in_=v[:], compare_op=ALU.is_ge, fill=0.0, base=0,
                                        pattern=[[0, GRP], [-1, P]], channel_multiplier=1).then_inc(const_ready, 1)

            def gmlp(n):
                pool.wait_ge(mv_ready, n + 1)
                nc.gpsimd.tensor_tensor(rstd[:], mv[:, 1:2], eps[:], ALU.add).then_inc(var_eps, 1)
                pool.wait_ge(var_eps, n + 1)
                nc.gpsimd.tensor_tensor(rstd[:], rstd[:], minus_half[:], ALU.pow).then_inc(rstd_ready, 1)
                pool.wait_ge(tg_read, n + 2)
                nc.gpsimd.tensor_tensor(vn, vn, lnvg, ALU.mult).then_inc(vn_step, 1)
                pool.wait_ge(vn_step, n + 1)
                nc.gpsimd.tensor_tensor(vn, vn, lnvb, ALU.add).then_inc(vn_ready, 1)
                pool.wait_ge(mix_read, n + 2)
                pool.wait_ge(gate_loaded, n * 16 + 16)
                nc.gpsimd.tensor_tensor(ya, ya, gate_t, ALU.mult).then_inc(ya_full, 1)

            with pool.Fori(0, PTILES) as n:
                gmlp(n)

        @block.scalar
        def _(act):
            def load_w(n, s):
                act.dma_start(raw[s][:], w_all[n, :, :, :]).then_inc(raw_loaded[s], 16)

            def high_part(s, loads):
                act.wait_ge(raw_loaded[s], loads * 16)
                nc.scalar.activation(wh[s][:], raw[s][:], ACT.Copy).then_inc(wh_done, 1)

            def x_high(half):
                act.wait_ge(x_turned, half + 1)
                k0 = 4 * (half % 2)
                nc.scalar.activation(xh[:, k0:k0 + 4, bass.ts(half // 2, P)],
                                     x_banks[half % 3][:].rearrange("p (k t) -> p k t", k=4), ACT.Copy).then_inc(xh_done, 1)

            def split(n, s, loads):
                act.wait_ge(w_ready, n)
                load_w(n + 1, 1 - s)
                high_part(s, loads)

            def gelu_va(order, c, e):
                act.wait_ge(proj_done, order + 1)
                act.wait_ge(st_a_stored[e % 2], 16 * (e // 2) + 16)
                n = CHUNKS[c][1]
                nc.scalar.activation(st_a[e % 2][:, 0:n], bank[c][:, 0:n], ACT.Gelu).then_inc(evac[c], 1)

            load_w(0, 0)
            e = 0
            for step in opening():
                if step[0] == "turn":
                    for tile in step[1]:
                        x_high(2 * tile)
                        x_high(2 * tile + 1)
                        if tile == 1:
                            load_w(1, 1)
                            high_part(0, 1)
                        if tile == 3:
                            high_part(1, 1)
                else:
                    gelu_va(e, step[2], e)
                    e += 1
                    if step[1:] == (1, 0):
                        act.wait_ge(w_ready, 1)
                        load_w(2, 0)
                    if step[1:] == (0, NCH - 1):
                        split(2, 0, 2)
            for g in (2, 3):
                for c in range(NCH):
                    gelu_va(g * NCH + c, c, g * NCH + c)
                    if c == 1:
                        split(g + 1, (g + 1) % 2, (g + 1) // 2 + 1)
            with act.Fori(0, GRP) as i:
                for j, kind in enumerate(GATE_GROUPS):
                    for c, (t0, n) in enumerate(CHUNKS):
                        act.wait_ge(proj_done, GRP * NCH + i * (A_J * NCH) + NCH * j + c + 1)
                        src = bank[c][:, 0:n]
                        if kind == "u":
                            act.wait_ge(gate_full, i * NCH + c + 1)
                            nc.scalar.activation(big[:, t0:t0 + n], src, ACT.Gelu).then_inc(evac[c], 1)
                        else:
                            act.wait_ge(st_b_stored[c % 2], i * (STORED_B[c % 2] // GRP) + 16 * (c // 2) + 16)
                            nc.scalar.activation(st_b[c % 2][:, 0:n], src, ACT.Tanh, scale=0.5).then_inc(act_read, 1)
                        if c == 1:
                            split(GRP + i * A_J + j + 1, (j + 1) % 2, GRP // 2 + i + (j + 1) // 2 + 1)
            with act.Fori(0, LOOP_B) as p:
                for j, kind in enumerate(PAIR_GROUPS):
                    for c, (t0, n) in enumerate(CHUNKS):
                        act.wait_ge(proj_done, 5 * N_A + p * (5 * B_J) + 5 * j + c + 1)
                        src = bank[c][:, 0:n]
                        e = 5 * j + c
                        if kind in "qk":
                            act.wait_ge(st_a_stored[e % 2], STORED_A[e % 2] + p * 80 + 16 * (e // 2) + 16)
                            scale = QSCALE if kind == "q" else 1.0
                            if kind == "q" and c == 4:
                                nc.scalar.activation(qs[:, p, :], src[:, 256:384], ACT.Copy, scale=scale)
                            if kind == "k" and c == 3:
                                nc.scalar.activation(kf[:, 0:256], src[:, 128:384], ACT.Copy).then_inc(kf_full, 1)
                            if kind == "k" and c == 4:
                                nc.scalar.activation(ks[:, p, :], src[:, 256:384], ACT.Copy)
                                nc.scalar.activation(kf[:, 256:640], src, ACT.Copy).then_inc(kf_full, 1)
                            nc.scalar.activation(st_a[e % 2][:, 0:n].bitcast(f32r), src, ACT.Copy,
                                                 scale=scale).then_inc(act_read, 1)
                        elif kind == "v":
                            if c > 0:
                                act.wait_ge(tv_done, p * 7 + 2 + c)
                            nc.scalar.activation(vt[:, 0:n], src, ACT.Copy).then_inc(evac[c], 1)
                        else:
                            act.wait_ge(st_b_stored[e % 2], STORED_B[e % 2] + p * 160 + 16 * (e // 2) + 16)
                            nc.scalar.activation(st_b[e % 2][:, 0:n], src, ACT.Tanh, scale=0.5).then_inc(act_read, 1)
                        if c == 1:
                            split(N_A + p * B_J + j + 1, (j + 1) % 2, N_A // 2 + p * (B_J // 2) + (j + 1) // 2 + 1)

            act.wait_ge(raw_loaded[1], 16 * (NGROUPS // 2 + 1))

        @block.vector
        def _(dve):
            dve.sem_inc(xbank_free, 3)
            dve.sem_inc(tv_copied, 1)
            dve.sem_inc(tg_read, 1)
            dve.sem_inc(mix_read, 1)
            dve.sem_inc(gate_full, NCH)
            for c in range(NCH):
                dve.sem_inc(evac[c], 1)

            def low_part(n, s):
                dve.wait_ge(wh_done, n + 1)
                nc.vector.tensor_tensor(wl[s][:], raw[s][:], wh[s][:].bitcast(f32), ALU.subtract).then_inc(w_ready, 1)

            def x_low(half):
                dve.wait_ge(xh_done, half + 1)
                k0 = 4 * (half % 2)
                at = (slice(None), slice(k0, k0 + 4), bass.ts(half // 2, P))
                nc.vector.tensor_tensor(xl[at], x_banks[half % 3][:].rearrange("p (k t) -> p k t", k=4),
                                        xh[at].bitcast(f32), ALU.subtract).then_inc(xbank_free, 1)

            for step in opening():
                if step[0] == "turn":
                    for tile in step[1]:
                        x_low(2 * tile)
                        x_low(2 * tile + 1)
                        if tile == 1:
                            low_part(0, 0)
                        if tile == 3:
                            low_part(1, 1)
            low_part(2, 0)
            dve.wait_ge(rel_loaded, 16)
            dve.wait_ge(rel_filled, 1)
            nc.vector.tensor_scalar(kf[0:HEADS, 0:2 * CLIP + 1], kf[0:HEADS, 0:2 * CLIP + 1], -1.0, None,
                                    ALU.mult).then_inc(rel_negated, 1)
            dve.wait_ge(rel_negated, 1)
            nc.vector.tensor_scalar(vt[0:HEADS, :], vt[0:HEADS, :], kf[0:HEADS, 0:1], None, ALU.add).then_inc(rel_negated, 1)
            low_part(3, 1)
            dve.wait_ge(wt_turned, 1)
            nc.vector.tensor_copy(wt[:].rearrange("p g t -> p (g t)"), tg_ps[:]).then_inc(wt_ready, 1)
            dve.wait_ge(wt_turned, 2)
            nc.vector.tensor_copy(wts[:].rearrange("p g t -> p (g t)"), tv_ps[:]).then_inc(wt_ready, 1)
            dve.wait_ge(par_loaded, 64)
            for b in range(SB):
                nc.vector.tensor_copy(bss[:, :, b * SN:(b + 1) * SN], bs[:, :, 0:SN]).then_inc(bss_ready, 1)
            low_part(4, 0)

            def silu_twice(n, c, st, handed):
                dve.wait_ge(act_read, handed)
                nc.vector.scalar_tensor_tensor(out=st, in0=st, scalar=1.0, in1=bank[c][:, 0:n], op0=ALU.add,
                                               op1=ALU.mult).then_inc(evac[c], 1)

            with dve.Fori(0, GRP) as i:
                for j, kind in enumerate(GATE_GROUPS):
                    for c, (t0, n) in enumerate(CHUNKS):
                        if kind == "za":
                            st = st_b[c % 2][:, 0:n]
                            silu_twice(n, c, st, i * NCH + c + 1)
                            dve.wait_ge(evac[c], GRP + i * A_J + j + 2)
                            nc.vector.scalar_tensor_tensor(out=st, in0=st, scalar=0.5, in1=big[:, t0:t0 + n],
                                                           op0=ALU.mult, op1=ALU.mult).then_inc(gate_full, 1)
                        if c == 1:
                            low_part(GRP + i * A_J + j + 1, (j + 1) % 2)

            def gmlp_stats(n):
                dve.wait_ge(tg_done, n + 1)
                nc.vector.bn_stats(stats[:], tg_ps[:]).then_inc(stats_ready, 1)
                dve.wait_ge(stats_ready, n + 1)
                dve.nop(nofuse=True)
                nc.vector.bn_aggr(mv[:], stats[:]).then_inc(mv_ready, 1)

            def gmlp_normalise(n):
                dve.wait_ge(rstd_ready, n + 1)
                nc.vector.tensor_scalar(vn, tg_ps[:], mv[:, 0:1], rstd[:], ALU.subtract, ALU.mult).then_inc(tg_read, 1)

            def gmlp_mixed(n):
                dve.wait_ge(mix_done, n + 1)
                dve.wait_ge(ya_stored, n * 16 + 16)
                nc.vector.tensor_tensor(ya, mix_ps[:].rearrange("p (g t) -> p g t", g=GRP), bs,
                                        ALU.add).then_inc(mix_read, 1)

            def copy_kn(c, p):
                nt = (2, 3)[c]
                dve.wait_ge(tv_done, p * 7 + c + 1)
                dve.wait_ge(kn_stored, p * 32 + 16 * c + 16)
                nc.vector.tensor_copy(kn[:, 0:nt, :].rearrange("t n c -> t (n c)"),
                                      tv_ps[:, 0:nt * P]).then_inc(tv_copied, 1)

            def copy_vn(c, p):
                n = CHUNKS[c][1]
                dve.wait_ge(tv_done, p * 7 + 3 + c)
                dve.wait_ge(st_b_stored[c % 2], STORED_B[c % 2] + p * 160 + 16 * ((10 + c) // 2) + 16)
                nc.vector.tensor_copy(st_b[c % 2][:, 0:n], tv_ps[:, 0:n]).then_inc(tv_copied, 1)

            with dve.Fori(0, LOOP_B) as p:
                for j, kind in enumerate(PAIR_GROUPS):
                    for c, (t0, n) in enumerate(CHUNKS):
                        e = 5 * j + c
                        if kind in "qk":
                            dve.wait_ge(act_read, 20 + p * 15 + e + 1)
                            dve.wait_ge(st_b_stored[e % 2], STORED_B[e % 2] + p * 160 + 16 * (e // 2) + 16)
                            nc.vector.scalar_tensor_tensor(
                                out=st_b[e % 2][:, 0:n].bitcast(f32r), in0=bank[c][:, 0:n],
                                scalar=QSCALE if kind == "q" else 1.0, in1=st_a[e % 2][:, 0:n],
                                op0=ALU.mult, op1=ALU.subtract).then_inc(evac[c], 1)
                        if kind == "z":
                            silu_twice(n, c, st_b[e % 2][:, 0:n], 20 + p * 15 + 10 + c + 1)
                        if c == 0:
                            gmlp_stats(p * 4 + j)
                        if c == 1:
                            gmlp_normalise(p * 4 + j)
                            low_part(N_A + p * B_J + j + 1, (j + 1) % 2)
                        if c == 3:
                            gmlp_mixed(p * 4 + j)
                        if kind == "k" and c == 4:
                            copy_kn(0, p)
                        if kind == "v":
                            if c == 0:
                                copy_kn(1, p)
                            else:
                                copy_vn(c - 1, p)
                        if kind == "z" and c == 0:
                            copy_vn(4, p)
            dve.wait_ge(bss_ready, SB)

        @block.tensor
        def _(pe):
            pe.wait_ge(const_ready, 4)

            def turn_x(tile):
                pe.wait_ge(x_loaded[tile % XSLOTS], 16 * (tile // XSLOTS + 1))
                for half in (2 * tile, 2 * tile + 1):
                    pe.wait_ge(xbank_free, half + 1)
                    for k in range(4):
                        kc = 4 * (half % 2) + k
                        last = nc.tensor.transpose(x_banks[half % 3][:, k * P:(k + 1) * P],
                                                   x_in[tile % XSLOTS][:, kc * P:(kc + 1) * P], ident[:])
                    last.then_inc(x_turned, 1)

            def project(n, c, s):
                t0, width = CHUNKS[c]
                if c == 0:
                    pe.wait_ge(w_ready, n + 1)
                pe.wait_ge(evac[c], n + 1)
                for kc in range(KC):
                    for a, (w, xx) in enumerate(((wh, xh), (wh, xl), (wl, xh))):
                        last = nc.tensor.matmul(bank[c][:, 0:width], w[s][:, kc, :], xx[:, kc, t0:t0 + width],
                                                start=kc == 0 and a == 0, stop=kc == KC - 1 and a == 2)
                last.then_inc(proj_done, 1)

            for step in opening():
                if step[0] == "turn":
                    for tile in step[1]:
                        turn_x(tile)
                else:
                    _, g, c = step
                    if g == 0:
                        pe.wait_ge(xbank_free, 2 * chunk_tiles(c)[-1] + 2 + 3)
                    project(g, c, g)
            for c in range(NCH):
                project(2, c, 0)
            for n, (held, dst) in enumerate(((wt, tg_ps), (wts, tv_ps))):
                pe.wait_ge(const_ready, 5 + n)
                for g in range(GRP):
                    last = nc.tensor.transpose(dst[:, g * P:(g + 1) * P], held[:, g, :], ident[:])
                last.then_inc(wt_turned, 1)
            for c in range(NCH):
                project(3, c, 1)
            pe.wait_ge(wt_ready, 2)
            with pe.Fori(0, GRP) as i:
                for j in range(A_J):
                    for c in range(NCH):
                        project(GRP + i * A_J + j, c, j % 2)

            def turn_va(n):
                pe.wait_ge(va_loaded, n * 16 + 16)
                pe.wait_ge(tg_read, n + 1)
                for g in range(GRP):
                    last = nc.tensor.transpose(tg_ps[:, g * P:(g + 1) * P], va_t[:, g, :], ident[:])
                last.then_inc(tg_done, 1)

            def mix(n):
                pe.wait_ge(vn_ready, n + 1)
                pe.wait_ge(mix_read, n + 1)
                for g in range(GRP):
                    last = nc.tensor.matmul(mix_ps[:, g * P:(g + 1) * P], vn[:, g * P:(g + 1) * P], wt[:, g, :],
                                            start=True, stop=True)
                last.then_inc(mix_done, 1)

            def turn_k(c, p):
                pe.wait_ge(kf_full, p * 2 + c + 1)
                pe.wait_ge(tv_copied, p * 7 + c + 1)
                for n, t in enumerate(((0, 1), (2, 3, 4))[c]):
                    last = nc.tensor.transpose(tv_ps[:, n * P:(n + 1) * P], kf[:, t * P:(t + 1) * P], ident[:])
                last.then_inc(tv_done, 1)

            def turn_v(c, p):
                pe.wait_ge(evac[c], N_A + p * B_J + 2 + 2)
                pe.wait_ge(tv_copied, p * 7 + 3 + c)
                for n in range(CHUNKS[c][1] // P):
                    last = nc.tensor.transpose(tv_ps[:, n * P:(n + 1) * P], vt[:, n * P:(n + 1) * P], ident[:])
                last.then_inc(tv_done, 1)

            with pe.Fori(0, LOOP_B) as p:
                for j, kind in enumerate(PAIR_GROUPS):
                    for c in range(NCH):
                        project(N_A + p * B_J + j, c, j % 2)
                        if c == 0:
                            turn_va(p * 4 + j)
                        if c == 3:
                            mix(p * 4 + j)
                        if kind == "k" and c == 4:
                            turn_k(0, p)
                        if kind == "v":
                            if c == 0:
                                turn_k(1, p)
                            else:
                                turn_v(c - 1, p)
                        if kind == "z" and c == 0:
                            turn_v(4, p)


def skewed(s_skew, heads, queries, past, keys):
    first = WIN - 1 - past
    flat = s_skew.rearrange("h i m -> h (i m)")[heads, first:first + queries * REL]
    return flat.rearrange("h (i m) -> i h m", m=REL)[:, :, 0:keys]


def key_tiles(t):
    return min(t, 4) + 1


def turned_banks(t):
    return -(-2 * key_tiles(t) // 4)


def attention(nc, x, cache_k, w_all, s_q, s_k, s_z, s_y, s_skew, v_all, gv_out, ident, big, par, bias_next, wts,
              minus_half, eps, bias_loaded, st_b, st_b_stored, wo_h, wo_l, yh, yl, y_loaded, xt_loaded,
                  y_high, y_split, y_stored, kc, k_loaded):
    f32, f32r = mybir.dt.float32, mybir.dt.float32r
    ALU = mybir.AluOpType
    ACT = mybir.ActivationFunctionType

    ctx = ExitStack()
    with ctx:
        def sb(name, shape, dt=f32):
            return ctx.enter_context(nc.sbuf_tensor(name, shape, dt))

        def sem(name):
            return ctx.enter_context(nc.semaphore(name))

        q = sb("q", [P, 2, 2, SEQ], f32r)
        k = sb("k", [P, 2, SEQ], f32r)
        v = sb("v", [P, PTILES, P])
        z = sb("z", [P, SEQ])
        bias_next = bias_next[:].rearrange("p (h j) -> p h j", h=2)
        bias = sb("bias", [P, 2, WIN])
        prob = [sb(f"prob{s}", [P, WIN]) for s in range(4)]
        low = sb("low", [P, 4])
        den = sb("den", [P, 4])
        rden = sb("rden", [P, 4])
        pt = [sb(f"pt{s}", [P, 10, P]) for s in range(2)]
        yst = st_b
        raw_o = [sb(f"raw_o{s}", [P, KC, P]) for s in range(2)]

        s_ps = [ctx.enter_context(nc.psum_tensor(f"s_ps{h}", [P, 2, 512], f32)) for h in range(2)]
        pt_ps = [ctx.enter_context(nc.psum_tensor(f"pt_ps{e}", [P, 4, P], f32)) for e in range(3)]
        o_ps = ctx.enter_context(nc.psum_tensor("o_ps", [P, 512], f32))

        qk_loaded = [sem(f"qk_loaded{c}") for c in range(4)]
        vz_loaded = [sem(f"vz_loaded{c}") for c in range(4)]
        first_loaded = sem("first_loaded")
        masked = sem("masked")
        bias_ready = sem("bias_ready")
        scored = sem("scored")
        biased = sem("biased")
        expd = sem("expd")
        rden_ready = sem("rden_ready")
        normed = sem("normed")
        turned = sem("turned")
        pt_copied = sem("pt_copied")
        pv_done = sem("pv_done")
        y_ready = sem("y_ready")
        raw_o_loaded = [sem(f"raw_o_loaded{s}") for s in range(2)]
        wo_high = sem("wo_high")
        wo_done = sem("wo_done")

        va_t, gate_t, ya = (big[:, a:a + 512].rearrange("p (g t) -> p g t", g=GRP) for a in (0, 512, 1536))
        vn = big[:, 1024:1536]
        lnvg, lnvb = par[:, 0:512], par[:, 512:1024]
        bss = par[:, 1536:2048].rearrange("p (g t) -> p g t", g=GRP)
        tg_ps, mix_ps = pt_ps[2][:].rearrange("p g t -> p (g t)"), o_ps
        stats = sb("stats_s", [P, 6])
        mv = sb("mv_s", [P, 2])
        rstd = sb("rstd_s", [P, 1])
        tg_done = sem("tg_done_s")
        stats_ready = sem("stats_ready_s")
        mv_ready = sem("mv_ready_s")
        var_eps = sem("var_eps_s")
        rstd_ready = sem("rstd_ready_s")
        vn_step = sem("vn_step_s")
        mix_done = sem("mix_done_s")
        ya_step = sem("ya_step_s")
        tail_stored = sem("tail_stored")

        QK_DMAS, VZ_DMAS = 6, 2
        BANKS = [0]
        for t in range(PTILES):
            BANKS.append(BANKS[-1] + turned_banks(t))
        assert BANKS[-1] % 3 == 0
        PER = BANKS[-1]

        block = ctx.enter_context(nc.Block())

        @block.sync
        def _(sp):
            for s in range(2):
                sp.sem_inc(y_stored[s], 16)

            def load_bias(pair):
                sp.dma_start(bias_next, skewed(s_skew, bass.ts(pair, 2), P, WIN - P, WIN)).then_inc(bias_loaded, 16)

            def load_qk(pair, at, loaded):
                for part in range(2):
                    qsrc = s_q[part, pair, :, at].rearrange("(h d) t -> d h t", h=2)
                    for half in range(2):
                        sp.dma_start(q[64 * half:64 * half + 64, :, part, at].bitcast(f32), qsrc).then_inc(loaded, 16)
                    ksrc = s_k[part, pair, :, at].rearrange("(h d) t -> d h t", h=2)
                    sp.dma_start(k[64 * part:64 * part + 64, :, at].bitcast(f32), ksrc).then_inc(loaded, 16)

            def load_vz(pair, c):
                at = slice(512 * c, 512 * c + 512)
                sp.dma_start(v[:, 4 * c:4 * c + 4, :],
                             v_all[at, bass.ts(pair, P)].rearrange("(n t) c -> t n c", t=P)).then_inc(vz_loaded[c], 16)
                sp.dma_start(z[:, at], s_z[pair, :, at]).then_inc(vz_loaded[c], 16)

            def load_chunk(pair, c):
                load_qk(pair, slice(512 * c, 512 * c + 512), qk_loaded[c])
                load_vz(pair, c)

            def store_y(pair, c):
                sp.wait_ge(y_ready, pair * PTILES + 4 * c + 4 + 1)
                sp.dma_start(s_y[pair + GRP, :, 512 * c:512 * c + 512], yst[c % 2][:]).then_inc(y_stored[c % 2], 16)

            load_qk(0, slice(0, 2 * P), first_loaded)
            load_qk(0, slice(2 * P, 4 * P), qk_loaded[0])
            for s in range(2):
                sp.wait_ge(st_b_stored[s], ALL_STORED_B[s])
            load_vz(0, 0)
            for c in range(1, 4):
                load_chunk(0, c)
            sp.wait_ge(vn_step, 3)
            sp.dma_start(gv_out, vn).then_inc(tail_stored, 16)
            sp.wait_ge(ya_step, 2)
            sp.dma_start(s_y[0:GRP, :, SEQ:T].rearrange("g c t -> c g t"), ya).then_inc(tail_stored, 16)
            for s in range(2):
                sp.dma_start(par[:, s * D:(s + 1) * D], x[bass.ts(s, P), :]).then_inc(xt_loaded[s], 16)
            sp.wait_ge(tail_stored, 32)
            with sp.Fori(0, GRP - 1) as pair:
                sp.wait_ge(bias_ready, pair * 2 + 2)
                load_bias(pair + 1)
                store_y(pair, 0)
                store_y(pair, 1)
                load_chunk(pair + 1, 0)
                store_y(pair, 2)
                load_chunk(pair + 1, 1)
                store_y(pair, 3)
                load_chunk(pair + 1, 2)
                load_chunk(pair + 1, 3)
            sp.dma_start(kc[:], cache_k[0, :, :]).then_inc(k_loaded, 16)
            store_y(GRP - 1, 0)
            sp.wait_ge(y_stored[0], 16 * 2 * GRP)
            for s in range(2):
                sp.dma_start(big[:, s * D:(s + 1) * D].rearrange("p (k t) -> p k t", k=KC),
                             s_y[:, :, bass.ts(s, P)].rearrange("k c t -> c k t")).then_inc(y_loaded[s], 16)
            for c in range(1, 4):
                store_y(GRP - 1, c)

        @block.gpsimd
        def _(pool):
            pool.sem_inc(wo_done, 2)
            pool.wait_ge(mv_ready, 1)
            nc.gpsimd.tensor_tensor(rstd[:], mv[:, 1:2], eps[:], ALU.add).then_inc(var_eps, 1)
            pool.wait_ge(var_eps, 1)
            nc.gpsimd.tensor_tensor(rstd[:], rstd[:], minus_half[:], ALU.pow).then_inc(rstd_ready, 1)
            pool.wait_ge(vn_step, 1)
            nc.gpsimd.tensor_tensor(vn, vn, lnvg, ALU.mult).then_inc(vn_step, 1)
            pool.wait_ge(vn_step, 2)
            nc.gpsimd.tensor_tensor(vn, vn, lnvb, ALU.add).then_inc(vn_step, 1)
            pool.wait_ge(ya_step, 1)
            nc.gpsimd.tensor_tensor(ya, ya, gate_t, ALU.mult).then_inc(ya_step, 1)
            with pool.Fori(0, GRP) as pair:
                for g in range(2):
                    at = (slice(None), slice(None), bass.ts(pair * 2 + g, P))
                    pool.wait_ge(raw_o_loaded[g], pair * 16 + 16)
                    nc.gpsimd.tensor_copy(wo_h[at], raw_o[g][:]).then_inc(wo_high, 1)
                    pool.wait_ge(wo_high, pair * 2 + g + 1)
                    nc.gpsimd.tensor_tensor(wo_l[at], raw_o[g][:], wo_h[at].bitcast(f32), ALU.subtract).then_inc(wo_done, 1)

        @block.scalar
        def _(act):
            def exponent(pair, t, h):
                n, s = key_tiles(t) * P, (2 * t + h) % 4
                act.wait_ge(biased, pair * 32 + 2 * t + h + 1 + 2)
                nc.scalar.activation(prob[s][:, 0:n], prob[s][:, 0:n], ACT.Exp, bias=low[:, s:s + 1],
                                     scale=-1.0, accum_out=den[:, s:s + 1]).then_inc(expd, 1)

            def copy_turned(pair, t, e):
                m = min(4, 2 * key_tiles(t) - 4 * e)
                act.wait_ge(pv_done, pair * PTILES + t + 1)
                act.wait_ge(turned, pair * PER + BANKS[t] + e + 1)
                nc.scalar.activation(pt[t % 2][:, 4 * e:4 * e + m, :],
                                     pt_ps[(BANKS[t] + e) % 3][:, 0:m, :], ACT.Copy).then_inc(pt_copied, 1)

            def steps(pair, first):
                act.wait_ge(wo_done, pair * 2 + 2)
                for g in range(2):
                    act.dma_start(raw_o[g][:], w_all[pair * 2 + (NGROUPS + g), :, :, :]).then_inc(raw_o_loaded[g], 16)
                for t in range(PTILES):
                    for h in range(2):
                        exponent(pair, t, h)
                    if t == 0 and first:
                        continue
                    before = (pair, t - 1) if t >= 1 else (pair - 1, PTILES - 1)
                    for e in range(turned_banks(before[1])):
                        copy_turned(*before, e)

            steps(0, True)
            with act.Fori(1, GRP) as pair:
                steps(pair, False)
            act.wait_ge(y_loaded[0], 16)
            nc.scalar.activation(yh[0][:], big[:, 0:D].rearrange("p (k t) -> p k t", k=KC), ACT.Copy).then_inc(y_high, 1)
            for e in range(turned_banks(PTILES - 1)):
                copy_turned(GRP - 1, PTILES - 1, e)

        @block.vector
        def _(dve):
            dve.sem_inc(biased, 2)
            dve.sem_inc(pt_copied, 3)
            dve.wait_ge(tg_done, 1)
            nc.vector.bn_stats(stats[:], tg_ps).then_inc(stats_ready, 1)
            dve.wait_ge(stats_ready, 1)
            nc.vector.bn_aggr(mv[:], stats[:]).then_inc(mv_ready, 1)
            dve.wait_ge(rstd_ready, 1)
            nc.vector.tensor_scalar(vn, tg_ps, mv[:, 0:1], rstd[:], ALU.subtract, ALU.mult).then_inc(vn_step, 1)
            def add_bias(pair, t, h):
                n, s = key_tiles(t) * P, (2 * t + h) % 4
                dve.wait_ge(scored, pair * 32 + 2 * t + h + 1)
                dve.nop(nofuse=True)
                if n > 512:
                    src = s_ps[h][:, :, 0:WIN // 2]
                    out, b = (a.rearrange("p (a b) -> p a b", a=2) for a in (prob[s][:], bias[:, h, :]))
                else:
                    src, out, b = s_ps[h][:, 0, 0:n], prob[s][:, 0:n], bias[:, h, WIN - n:WIN]
                nc.vector.tensor_tensor_reduce(out=out, in0=src, in1=b, scale=1.0, scalar=MASKED,
                                               op0=ALU.add, op1=ALU.min, accum_out=low[:, s:s + 1]).then_inc(biased, 1)

            def normalise(pair, t, h):
                n, s = key_tiles(t) * P, (2 * t + h) % 4
                dve.wait_ge(expd, pair * 32 + 2 * t + h + 1)
                nc.vector.reciprocal(rden[:, s:s + 1], den[:, s:s + 1]).then_inc(rden_ready, 1)
                dve.wait_ge(rden_ready, pair * 32 + 2 * t + h + 1)
                nc.vector.tensor_scalar(prob[s][:, 0:n], prob[s][:, 0:n], rden[:, s:s + 1], None,
                                        ALU.mult).then_inc(normed, 1)

            def gate(pair, t):
                c = t // 4
                if t % 4 == 0:
                    dve.wait_ge(y_stored[c % 2], pair * 32 + 16 * (c // 2) + 16)
                dve.wait_ge(pv_done, pair * PTILES + t + 1 + 2)
                nc.vector.scalar_tensor_tensor(
                    out=yst[c % 2][:, (t % 4) * P:(t % 4 + 1) * P], in0=o_ps[:, 0:P], scalar=0.5,
                    in1=z[:, t * P:(t + 1) * P], op0=ALU.mult, op1=ALU.mult).then_inc(y_ready, 1)

            nc.vector.memset(bias[HD:P, :, 0:HD], MASKED).then_inc(masked, 1)
            nc.vector.memset(bias[0:HD, :, WIN - HD:WIN], MASKED).then_inc(masked, 1)
            dve.wait_ge(masked, 2)
            def steps(pair, first):
                dve.wait_ge(bias_loaded, pair * 16 + 16)
                nc.vector.tensor_copy(bias[0:HD, :, 0:WIN - HD], bias_next[0:HD, :, 0:WIN - HD]).then_inc(bias_ready, 1)
                nc.vector.tensor_copy(bias[HD:P, :, HD:WIN], bias_next[HD:P, :, HD:WIN]).then_inc(bias_ready, 1)
                dve.wait_ge(bias_ready, pair * 2 + 2)
                for t in range(PTILES):
                    for h in range(2):
                        add_bias(pair, t, h)
                    for h in range(2):
                        normalise(pair, t, h)
                    if t == 1 and first:
                        dve.wait_ge(mix_done, 1)
                        nc.vector.tensor_tensor(ya, mix_ps[:].rearrange("p (g t) -> p g t", g=GRP), bss,
                                                ALU.add).then_inc(ya_step, 1)
                        dve.wait_ge(ya_step, 1)
                        dve.sem_inc(y_ready, 1)
                    if t >= 2:
                        gate(pair, t - 2)
                    elif not first:
                        gate(pair - 1, PTILES - 2 + t)

            steps(0, True)
            with dve.Fori(1, GRP) as pair:
                steps(pair, False)
            gate(GRP - 1, PTILES - 2)
            dve.wait_ge(y_high, 1)
            nc.vector.tensor_tensor(yl[0][:], big[:, 0:D].rearrange("p (k t) -> p k t", k=KC), yh[0][:].bitcast(f32),
                                    ALU.subtract).then_inc(y_split, 1)
            gate(GRP - 1, PTILES - 1)

        @block.tensor
        def _(pe):
            pe.sem_inc(pv_done, 2)

            def scores(pair, t, first):
                k0, n = (t + 1 - key_tiles(t)) * P, key_tiles(t) * P
                halves = [(0, 0, n)] if n <= 512 else [(0, 0, n // 2), (1, n // 2, n // 2)]
                if t == 0 and first:
                    pe.wait_ge(first_loaded, 16 * QK_DMAS)
                elif t % 4 == 0 or (t == 2 and first):
                    pe.wait_ge(qk_loaded[t // 4], (pair + 1) * (16 * QK_DMAS))
                for h in range(2):
                    pe.wait_ge(biased, pair * 32 + 2 * t + h + 1)
                    for b, at, m in halves:
                        for part in range(2):
                            last = nc.tensor.matmul(s_ps[h][:, b, 0:m], q[:, h, part, t * P:(t + 1) * P],
                                                    k[:, h, k0 + at:k0 + at + m], start=part == 0, stop=part == 1)
                    last.then_inc(scored, 1)

            def turn(pair, t):
                pe.wait_ge(normed, pair * 32 + 2 * t + 2)
                for e in range(turned_banks(t)):
                    pe.wait_ge(pt_copied, pair * PER + BANKS[t] + e + 1)
                    for i in range(4 * e, min(4 * e + 4, 2 * key_tiles(t))):
                        b, h = i // 2, i % 2
                        last = nc.tensor.transpose(pt_ps[(BANKS[t] + e) % 3][:, i - 4 * e, :],
                                                   prob[(2 * t + h) % 4][:, b * P:(b + 1) * P], ident[:])
                    last.then_inc(turned, 1)

            def weigh(pair, t):
                nk = key_tiles(t)
                if t % 4 == 0:
                    pe.wait_ge(vz_loaded[t // 4], (pair + 1) * (16 * VZ_DMAS))
                pe.wait_ge(pt_copied, pair * PER + BANKS[t + 1] + 3)
                pe.wait_ge(y_ready, pair * PTILES + t + 1)
                for b in range(nk):
                    for h in range(2):
                        last = nc.tensor.matmul(o_ps[64 * h:64 * h + 64, 0:P],
                                                v[:, t + 1 - nk + b, 64 * h:64 * h + 64], pt[t % 2][:, 2 * b + h, :],
                                                start=b == 0, stop=b == nk - 1, skip_group_check=True)
                last.then_inc(pv_done, 1)

            def steps(pair, first):
                for t in range(PTILES):
                    scores(pair, t, first)
                    if t == 1 and first:
                        pe.wait_ge(vn_step, 3)
                        for g in range(GRP):
                            last = nc.tensor.matmul(mix_ps[:, g * P:(g + 1) * P], vn[:, g * P:(g + 1) * P],
                                                    wts[:, g, :], start=True, stop=True)
                        last.then_inc(mix_done, 1)
                    if t >= 2:
                        weigh(pair, t - 2)
                    elif not first:
                        weigh(pair - 1, PTILES - 2 + t)
                    if t >= 1:
                        turn(pair, t - 1)
                    elif not first:
                        turn(pair - 1, PTILES - 1)

            for g in range(GRP):
                last = nc.tensor.transpose(tg_ps[:, g * P:(g + 1) * P], va_t[:, g, :], ident[:])
            last.then_inc(tg_done, 1)
            steps(0, True)
            with pe.Fori(1, GRP) as pair:
                steps(pair, False)
            weigh(GRP - 1, PTILES - 2)
            turn(GRP - 1, PTILES - 1)
            weigh(GRP - 1, PTILES - 1)


def output_projection(nc, x, ln_g, ln_b, cache_k, cache_v, s_z, s_y, s_skew, v_all, y_out, ident, big, par,
                      minus_half, eps, qs, ks, wo_h, wo_l, yh, yl, y_loaded, xt_loaded, y_high, y_split, y_stored, kc, k_loaded):
    f32, f32r = mybir.dt.float32, mybir.dt.float32r
    ALU = mybir.AluOpType
    ACT = mybir.ActivationFunctionType

    ctx = ExitStack()
    with ctx:
        def sb(name, shape, dt=f32):
            return ctx.enter_context(nc.sbuf_tensor(name, shape, dt))

        def sem(name):
            return ctx.enter_context(nc.semaphore(name))

        yr = [big[:, s * D:(s + 1) * D].rearrange("p (k t) -> p k t", k=KC) for s in range(2)]
        xt = [par[:, s * D:(s + 1) * D] for s in range(2)]
        yh = yh + [sb("yh1", [P, KC, P], f32r)]
        yl = yl + [sb("yl1", [P, KC, P], f32r)]
        r = [sb(f"r{s}", [P, D]) for s in range(2)]
        gain = sb("gain", [P, D])
        offset = sb("offset", [P, D])
        stats = sb("stats_o", [P, 2, 6])
        mv = sb("mv_o", [P, 2])
        rstd = sb("rstd_o", [P, 1])
        SHARE = 5 * P
        vc = sb("vc", [PAST, 512])
        vnew = sb("vnew", [SN, 512])
        kt = sb("kt", [P, GRP, SKEYS])
        qd = sb("qd", [P, GRP, 2 * SN])
        sbias = sb("sbias", [P, SKEYS])
        sprob = sb("sprob", [P, SKEYS])
        slow = sb("slow", [P, 1])
        sden = sb("sden", [P, 1])
        srden = sb("srden", [P, 1])
        spt = sb("spt", [P, 2, P])
        zs = sb("zs", [P, GRP, P])
        ys = sb("ys", [P, GRP, P])

        out_ps = [ctx.enter_context(nc.psum_tensor(f"out_ps{b}", [P, 512], f32)) for b in range(4)]
        kt_ps = ctx.enter_context(nc.psum_tensor("kt_ps", [P, GRP, P], f32))
        ss_ps = ctx.enter_context(nc.psum_tensor("ss_ps", [P, 512], f32))
        spt_ps = ctx.enter_context(nc.psum_tensor("spt_ps", [P, 4, P], f32))
        so_ps = ctx.enter_context(nc.psum_tensor("so_ps", [P, 512], f32))

        par_loaded = sem("par_loaded_o")
        z_loaded = sem("z_loaded")
        sbias_loaded = sem("sbias_loaded")
        out_done = sem("out_done")
        out_read = sem("out_read")
        half_stats = sem("half_stats")
        mv_ready = sem("mv_ready_o")
        var_eps = sem("var_eps_o")
        rstd_ready = sem("rstd_ready_o")
        centred = sem("centred")
        gained = sem("gained")
        r_ready = sem("r_ready")
        r_stored = [sem(f"r_stored{s}") for s in range(2)]
        const_ready = sem("const_ready_o")
        v_loaded = sem("v_loaded")
        kc_turned = sem("kc_turned")
        kt_ready = sem("kt_ready")
        q_ready = sem("q_ready")
        s_scored = sem("s_scored")
        s_biased = sem("s_biased")
        s_expd = sem("s_expd")
        s_rden = sem("s_rden")
        s_normed = sem("s_normed")
        s_turned = sem("s_turned")
        s_pt = sem("s_pt")
        s_weighed = sem("s_weighed")
        ys_ready = sem("ys_ready")
        last_gained = sem("last_gained")
        last_part = sem("last_part")

        block = ctx.enter_context(nc.Block())

        @block.sync
        def _(sp):
            for s in range(2):
                sp.sem_inc(r_stored[s], 16)

            def load_y(tile, s):
                sp.dma_start(yr[s], s_y[:, :, bass.ts(tile, P)].rearrange("k c t -> c k t")).then_inc(y_loaded[s], 16)

            def load_x(tile, s):
                sp.dma_start(xt[s], x[bass.ts(tile, P), :]).then_inc(xt_loaded[s], 16)

            def load_keys(b):
                sp.dma_start(kc[:], cache_k[b, :, :]).then_inc(k_loaded, 16)

            def load_values(b):
                sp.dma_start(vc[:], cache_v[b, :, :]).then_inc(v_loaded, 16)
                sp.dma_start(vnew[:], v_all[bass.ds(b * SN + SEQ, SN), :]).then_inc(v_loaded, 16)

            def store_tile(tile, s, count):
                sp.wait_ge(r_ready, count)
                sp.dma_start(y_out[bass.ts(tile, P), :], r[s][:]).then_inc(r_stored[s], 16)

            for h in range(HEADS):
                src = skewed(s_skew, slice(h, h + 1), SN, PAST, SKEYS)[:, 0, :]
                sp.dma_start(sbias[h * SN:(h + 1) * SN, :], src).then_inc(sbias_loaded, 16)
            load_values(0)
            sp.dma_start(gain[:], ln_g.partition_broadcast(P)).then_inc(par_loaded, 16)
            sp.dma_start(offset[:], ln_b.partition_broadcast(P)).then_inc(par_loaded, 16)
            sp.dma_start(zs[:], s_z[:, :, SEQ:T].rearrange("g c t -> c g t")).then_inc(z_loaded, 16)
            for s in range(2):
                sp.wait_ge(y_stored[s], 16 + 16 * 2 * GRP)
            with sp.Fori(0, SB - 1) as i:
                for s in range(2):
                    sp.wait_ge(y_split, i * 2 + s + 1)
                    load_y(i * 2 + 2 + s, s)
                sp.wait_ge(kc_turned, i + 1)
                load_keys(i + 1)
                for s in range(2):
                    sp.wait_ge(out_read, i * 4 + 2 * s + 2 + 4)
                    load_x(i * 2 + 2 + s, s)
                    if s == 0:
                        sp.wait_ge(ys_ready, i * 2 + 2)
                        load_values(i + 1)
                    store_tile(i * 2 + s, s, i * 2 + s + 1)
            sp.wait_ge(y_split, PTILES - 1)
            sp.dma_start(yr[0][:, 0:GRP, :], s_y[0:GRP, :, SEQ:T].rearrange("k c t -> c k t")).then_inc(y_loaded[0], 16)
            sp.wait_ge(out_read, 2 * (PTILES - 1) + 4)
            load_x(TILES - 1, 0)
            store_tile(PTILES - 2, 0, PTILES - 1)
            store_tile(PTILES - 1, 1, PTILES)
            last = bass.ts(TILES - 1, P)
            sp.wait_ge(last_part, 1)
            sp.dma_start(y_out[last, 0:SHARE], r[0][:, 0:SHARE]).then_inc(r_stored[0], 16)
            sp.wait_ge(r_ready, TILES)
            sp.dma_start(y_out[last, SHARE:D], r[0][:, SHARE:D]).then_inc(r_stored[0], 16)
            sp.wait_ge(r_stored[0], 16 * (SB + 3))
            sp.wait_ge(r_stored[1], 16 * (SB + 1))

        @block.gpsimd
        def _(pool):
            nc.gpsimd.memset(qd[:], 0.0).then_inc(const_ready, 1)
            pool.wait_ge(const_ready, 1)
            pool.wait_ge(par_loaded, 32)

            def finish(n, s, at):
                pool.wait_ge(mv_ready, n + 1)
                nc.gpsimd.tensor_tensor(rstd[:], mv[:, 1:2], eps[:], ALU.add).then_inc(var_eps, 1)
                pool.wait_ge(var_eps, n + 1)
                nc.gpsimd.tensor_tensor(rstd[:], rstd[:], minus_half[:], ALU.pow).then_inc(rstd_ready, 1)
                pool.wait_ge(centred, n + 1)
                nc.gpsimd.tensor_tensor(r[s][:, at], r[s][:, at], gain[:, at], ALU.mult).then_inc(gained, 1)
                pool.wait_ge(gained, n + 1)
                nc.gpsimd.tensor_tensor(r[s][:, at], r[s][:, at], offset[:, at], ALU.add).then_inc(r_ready, 1)

            with pool.Fori(0, SB) as i:
                for s in range(2):
                    finish(i * 2 + s, s, slice(0, D))
            finish(PTILES, 0, slice(SHARE, D))

        @block.scalar
        def _(act):
            def high(n, s, loads):
                act.wait_ge(y_loaded[s], loads)
                act.wait_ge(out_done, n * 2 + 2)
                nc.scalar.activation(yh[s][:], yr[s], ACT.Copy).then_inc(y_high, 1)

            def step(i, last):
                stream(i, 0)
                high(i * 2 + 1, 1, i * 16 + 16)
                stream(i, 1)
                stream(i, 2)
                if not last:
                    high(i * 2 + 2, 0, i * 16 + 32)

            def stream(i, stage):
                if stage == 0:
                    act.wait_ge(kc_turned, i + 1)
                    nc.scalar.activation(kt[:, :, 0:PAST], kt_ps[:], ACT.Copy).then_inc(kt_ready, 1)
                if stage == 1:
                    act.wait_ge(s_biased, i + 1)
                    nc.scalar.activation(sprob[:], sprob[:], ACT.Exp, bias=slow[:], scale=-1.0,
                                         accum_out=sden[:]).then_inc(s_expd, 1)
                if stage == 2:
                    act.wait_ge(s_turned, i + 1)
                    nc.scalar.activation(spt[:, 0, :], spt_ps[:, 0, :], ACT.Copy).then_inc(s_pt, 1)
                    nc.scalar.activation(spt[0:SN, 1, :], spt_ps[0:SN, 1, :], ACT.Copy).then_inc(s_pt, 1)

            with act.Fori(0, SB - 1) as i:
                step(i, False)
            step(SB - 1, True)
            act.wait_ge(y_loaded[0], 16 * (SB + 1))
            act.wait_ge(out_done, 2 * PTILES + 2)
            nc.scalar.activation(yh[0][:, 0:GRP, :], yr[0][:, 0:GRP, :], ACT.Copy).then_inc(y_high, 1)
            act.wait_ge(ys_ready, 2 * SB)
            nc.scalar.activation(yh[0][:, GRP:KC, :], ys[:], ACT.Copy).then_inc(y_high, 1)

        @block.vector
        def _(dve):
            dve.sem_inc(out_read, 4)

            def low(n, s):
                dve.wait_ge(y_high, n + 1)
                nc.vector.tensor_tensor(yl[s][:], yr[s], yh[s][:].bitcast(f32), ALU.subtract).then_inc(y_split, 1)

            def residual(n, s, h, loads, stores):
                dve.wait_ge(out_done, n * 2 + h + 1 + 4)
                if h == 0:
                    dve.wait_ge(xt_loaded[s], loads)
                    dve.wait_ge(r_stored[s], stores)
                at = slice(512 * h, 512 * h + 512)
                nc.vector.scalar_tensor_tensor(out=r[s][:, at], in0=xt[s][:, at], scalar=ALPHA, in1=out_ps[2 * s + h][:],
                                               op0=ALU.mult, op1=ALU.add).then_inc(out_read, 1)
                dve.wait_ge(out_read, n * 2 + h + 1 + 4)
                nc.vector.bn_stats(stats[:, h, :], r[s][:, at]).then_inc(half_stats, 1)

            def centre(n, s):
                dve.wait_ge(half_stats, n * 2 + 2)
                dve.nop(nofuse=True)
                nc.vector.bn_aggr(mv[:], stats[:].rearrange("p h n -> p (h n)")).then_inc(mv_ready, 1)
                dve.wait_ge(rstd_ready, n + 1)
                nc.vector.tensor_scalar(r[s][:], r[s][:], mv[:, 0:1], rstd[:], ALU.subtract, ALU.mult).then_inc(centred, 1)

            def stream(i, stage):
                at = bass.ts(i, SN)
                if stage == 0:
                    nc.vector.tensor_copy(kt[:, :, PAST:SKEYS], ks[:, :, at]).then_inc(q_ready, 1)
                    nc.vector.tensor_copy(qd[0:HD, :, 0:SN], qs[0:HD, :, at]).then_inc(q_ready, 1)
                    nc.vector.tensor_copy(qd[HD:P, :, SN:2 * SN], qs[HD:P, :, at]).then_inc(q_ready, 1)
                if stage == 1:
                    dve.wait_ge(sbias_loaded, 16 * HEADS)
                    dve.wait_ge(s_scored, i + 1)
                    dve.nop(nofuse=True)
                    nc.vector.tensor_tensor_reduce(out=sprob[:], in0=ss_ps[:, 0:SKEYS], in1=sbias[:], scale=1.0,
                                                   scalar=MASKED, op0=ALU.add, op1=ALU.min,
                                                   accum_out=slow[:]).then_inc(s_biased, 1)
                    dve.wait_ge(s_expd, i + 1)
                    nc.vector.reciprocal(srden[:], sden[:]).then_inc(s_rden, 1)
                    dve.wait_ge(s_rden, i + 1)
                    nc.vector.tensor_scalar(sprob[:], sprob[:], srden[:], None, ALU.mult).then_inc(s_normed, 1)
                if stage == 3:
                    dve.wait_ge(z_loaded, 16)
                    dve.wait_ge(s_weighed, i + 1)
                    o = so_ps[:, 0:GRP * 2 * SN].rearrange("p (g t) -> p g t", g=GRP)
                    for h in range(2):
                        rows = slice(HD * h, HD * h + HD)
                        nc.vector.scalar_tensor_tensor(out=ys[rows, :, at], in0=o[rows, :, SN * h:SN * h + SN], scalar=0.5,
                                                       in1=zs[rows, :, at], op0=ALU.mult, op1=ALU.mult).then_inc(ys_ready, 1)

            dve.wait_ge(const_ready, 1)

            def step(i, last):
                stream(i, 0)
                low(i * 2 + 1, 1)
                residual(i * 2, 0, 0, i * 16 + 16, i * 16 + 16)
                stream(i, 1)
                residual(i * 2, 0, 1, None, None)
                centre(i * 2, 0)
                residual(i * 2 + 1, 1, 0, i * 16 + 16, i * 16 + 16)
                stream(i, 3)
                if last:
                    dve.wait_ge(y_high, PTILES + 1)
                    nc.vector.tensor_tensor(yl[0][:, 0:GRP, :], yr[0][:, 0:GRP, :], yh[0][:, 0:GRP, :].bitcast(f32),
                                            ALU.subtract).then_inc(y_split, 1)
                    dve.wait_ge(y_high, PTILES + 2)
                    nc.vector.tensor_tensor(yl[0][:, GRP:KC, :], ys[:], yh[0][:, GRP:KC, :].bitcast(f32),
                                            ALU.subtract).then_inc(y_split, 1)
                else:
                    low(i * 2 + 2, 0)
                residual(i * 2 + 1, 1, 1, None, None)
                centre(i * 2 + 1, 1)

            with dve.Fori(0, SB - 1) as i:
                step(i, False)
            step(SB - 1, True)
            for h in range(2):
                residual(PTILES, 0, h, 16 * (SB + 1), 16 * (SB + 1))
            centre(PTILES, 0)
            at = slice(0, SHARE)
            dve.wait_ge(centred, PTILES + 1)
            nc.vector.tensor_tensor(r[0][:, at], r[0][:, at], gain[:, at], ALU.mult).then_inc(last_gained, 1)
            dve.wait_ge(last_gained, 1)
            nc.vector.tensor_tensor(r[0][:, at], r[0][:, at], offset[:, at], ALU.add).then_inc(last_part, 1)

        @block.tensor
        def _(pe):
            pe.sem_inc(out_done, 4)

            def project(n, s, h):
                if h == 0:
                    pe.wait_ge(y_split, n + 1)
                pe.wait_ge(out_read, n * 2 + h + 1)
                for c in range(KC):
                    for a, (y, w) in enumerate(((yh, wo_h), (yh, wo_l), (yl, wo_h))):
                        last = nc.tensor.matmul(out_ps[2 * s + h][:], y[s][:, c, :], w[:, c, 512 * h:512 * h + 512],
                                                start=c == 0 and a == 0, stop=c == KC - 1 and a == 2)
                last.then_inc(out_done, 1)

            def stream(i, stage):
                if stage == 0:
                    pe.wait_ge(k_loaded, i * 16 + 16)
                    for p in range(GRP):
                        last = nc.tensor.transpose(kt_ps[:, p, :], kc[:, p * P:(p + 1) * P], ident[:])
                    last.then_inc(kc_turned, 1)
                if stage == 1:
                    pe.wait_ge(kt_ready, i + 1)
                    pe.wait_ge(q_ready, i * 3 + 3)
                    for p in range(GRP):
                        last = nc.tensor.matmul(ss_ps[2 * SN * p:2 * SN * (p + 1), 0:SKEYS], qd[:, p, :], kt[:, p, :],
                                                start=True, stop=True)
                    last.then_inc(s_scored, 1)
                if stage == 2:
                    pe.wait_ge(s_normed, i + 1)
                    nc.tensor.transpose(spt_ps[:, 0, :], sprob[:, 0:PAST], ident[:])
                    nc.tensor.transpose(spt_ps[0:SN, 1, :], sprob[:, PAST:SKEYS], ident[:]).then_inc(s_turned, 1)
                if stage == 3:
                    pe.wait_ge(s_pt, i * 2 + 2)
                    pe.wait_ge(v_loaded, i * 32 + 32)
                    for p in range(GRP):
                        cols = slice(2 * SN * p, 2 * SN * (p + 1))
                        nc.tensor.matmul(so_ps[:, cols], vc[:, p * P:(p + 1) * P], spt[:, 0, cols], start=True, stop=False)
                        last = nc.tensor.matmul(so_ps[:, cols], vnew[:, p * P:(p + 1) * P], spt[0:SN, 1, cols],
                                                start=False, stop=True)
                    last.then_inc(s_weighed, 1)

            with pe.Fori(0, SB) as i:
                for e in range(4):
                    stream(i, e)
                    project(i * 2 + e // 2, e // 2, e % 2)
            pe.wait_ge(y_split, PTILES + 2)
            for h in range(2):
                project(PTILES, 0, h)


def lay_out(x_prompt, x_sample, cache_k, cache_v, w_in, w_sgu, b_sgu, ln_v_g, ln_v_b, rel_bias, w_out, ln_g, ln_b):
    c = np.ascontiguousarray
    w_in, w_out = np.asarray(w_in)[0], np.asarray(w_out)[0]
    base = {"u": 0, "va": 512, "za": 1024, "q": 1536, "k": 2048, "v": 2560, "z": 3072}
    first = [base["va"] + g * P for g in range(GRP)]
    first += [base[kind] + g * P for g in range(GRP) for kind in GATE_GROUPS]
    first += [base[kind] + p * P for p in range(LOOP_B) for kind in PAIR_GROUPS]
    groups = [w_in[:, f:f + P] for f in first] + [w_out[:, n * P:(n + 1) * P] for n in range(KC)]
    w_all = np.stack([g.reshape(KC, P, P).transpose(1, 0, 2) for g in groups])
    return {
        "x": c(np.concatenate([np.asarray(x_prompt).reshape(SEQ, D), np.asarray(x_sample).reshape(SB * SN, D)])),
        "w_all": c(w_all),
        "w_sgu": c(np.asarray(w_sgu)[0]), "b_sgu": c(np.asarray(b_sgu).reshape(-1)),
        "ln_v_g": c(np.asarray(ln_v_g)[0]), "ln_v_b": c(np.asarray(ln_v_b)[0]),
        "rel_rev": c(np.asarray(rel_bias)[0][:, ::-1]),
        "ln_g": c(np.asarray(ln_g)[0]), "ln_b": c(np.asarray(ln_b)[0]),
        "cache_k": c(np.asarray(cache_k).reshape(SB, PAST, HEADS * HD)),
        "cache_v": c(np.asarray(cache_v).reshape(SB, PAST, HEADS * HD)),
    }


def kernel(x_prompt, x_sample, cache_k, cache_v, w_in, w_sgu, b_sgu, ln_v_g, ln_v_b, rel_bias, w_out, ln_g, ln_b):
    import concourse.bacc as bacc
    from concourse.bass_utils import run_bass_kernel_spmd

    arrays = lay_out(x_prompt, x_sample, cache_k, cache_v, w_in, w_sgu, b_sgu, ln_v_g, ln_v_b, rel_bias, w_out,
                     ln_g, ln_b)
    nc = bacc.Bacc("TRN2", target_bir_lowering=False, num_devices=1)
    args = {n: nc.dram_tensor(n, a.shape, mybir.dt.from_np(a.dtype), kind="ExternalInput").ap()
            for n, a in arrays.items()}
    outs = {"y_out": (T, D), "v_all": (T, HEADS * HD), "k_tail": (T - SEQ + KEEP, HEADS * HD), "gv_out": (SB * SN, 512)}
    for n, shape in outs.items():
        args[n] = nc.dram_tensor(n, shape, mybir.dt.float32, kind="ExternalOutput").ap()
    hybrid_stream_step(nc, **args)
    r = run_bass_kernel_spmd(nc, [arrays], core_ids=[0]).results[0]
    y, v, k, gv = r["y_out"], r["v_all"], r["k_tail"], r["gv_out"]
    heads = (HEADS, HD)
    return (y[:SEQ].reshape(1, SEQ, D), y[SEQ:].reshape(SB, SN, D),
            k[:KEEP].reshape(1, 1, KEEP, *heads), v[SEQ - KEEP:SEQ].reshape(1, 1, KEEP, *heads),
            k[KEEP:].reshape(1, SB, SN, *heads), v[SEQ:].reshape(1, SB, SN, *heads),
            gv.reshape(1, SB, SN, 512))
```

```python
import numpy as np
import concourse.bass as bass
from concourse import mybir
from contextlib import ExitStack

P = 128
D = 1024
KC = D // P
SEQ = 2048
SB, SN = 8, 16
T = SEQ + SB * SN
TILES = T // P
PTILES = SEQ // P
GRP = 4
HD = 64
HEADS = 8
PAST = 128
SKEYS = PAST + SN
WIN = 640
CLIP = 128
REL = 6 * P
KEEP = 512
NGROUPS = 28
CHUNKS = [(0, 512), (512, 512), (1024, 384), (1408, 384), (1792, 384)]
NCH = len(CHUNKS)
ALPHA = 2.0 ** 0.25
EPS = 1e-5
QSCALE = -(HD ** -0.5)
MASKED = 3.0e38

GATE_GROUPS = ["u", "za"]
PAIR_GROUPS = ["q", "k", "v", "z"]
LOOP_B = 4


def opening():
    return [("split", 0), ("project", 0, 0), ("split", 1), ("project", 1, 0), ("project", 0, 1), ("split", 2),
            ("project", 1, 1), ("split", 3), ("project", 0, 2), ("split", 4), ("project", 0, 3), ("project", 1, 2),
            ("project", 0, 4), ("project", 1, 3), ("project", 1, 4)]


PIECES = 4


STORED_B = [16 * GRP * len(range(s, NCH, 2)) for s in range(2)]
ALL_STORED_B = [16 + n + 16 * 2 * NCH * LOOP_B for n in STORED_B]


def hybrid_stream_step(nc, x, x_t, w_all, w_sgu, b_sgu, ln_v_g, ln_v_b, rel_rev, ln_g, ln_b,
                       cache_k, cache_v, y_out, v_all, k_tail, gv_out):
    f32, f32r = mybir.dt.float32, mybir.dt.float32r

    ctx = ExitStack()
    with ctx:
        def dram(name, shape, dt=f32):
            return nc.dram_tensor(name, shape, dt).ap()

        s_gate = dram("s_gate", [GRP, P, T])
        s_va = dram("s_va", [GRP, P, T])
        s_q = dram("s_q", [2, GRP, P, SEQ])
        s_k = dram("s_k", [2, GRP, P, SEQ])
        s_z = dram("s_z", [GRP, P, T])
        s_y = dram("s_y", [2 * GRP, P, T])
        s_rel = dram("s_rel", [HEADS, REL])
        s_skew = dram("s_skew", [HEADS, P, REL + 1])

        outer = ctx.enter_context(ExitStack())

        def sb(stack, name, shape, dt=f32):
            return stack.enter_context(nc.sbuf_tensor(name, shape, dt))

        ident = sb(outer, "ident", [P, P])
        big = sb(outer, "big", [P, T])
        par = sb(outer, "par", [P, 4 * 512])
        st_b = [sb(outer, f"st_b{s}", [P, 512]) for s in range(2)]
        bias_next = sb(outer, "bias_next", [P, 2 * WIN])
        wts = sb(outer, "wts", [P, GRP, P])
        minus_half = sb(outer, "minus_half", [P, 1])
        eps = sb(outer, "eps", [P, 1])
        qs = sb(outer, "qs", [P, GRP, P])
        ks = sb(outer, "ks", [P, GRP, P])

        bias_loaded = ctx.enter_context(nc.semaphore("bias_loaded"))
        st_b_stored = [ctx.enter_context(nc.semaphore(f"st_b_stored{s}")) for s in range(2)]
        input_projection(nc, x_t, w_all, w_sgu, b_sgu, ln_v_g, ln_v_b, rel_rev, s_gate, s_va, s_q, s_k, s_z, s_y,
                         s_rel, s_skew, v_all, k_tail, ident, big, par, bias_next, wts, minus_half, eps, qs, ks, st_b,
                         bias_loaded, st_b_stored)
        wo_h = sb(outer, "wo_h", [P, KC, D], f32r)
        wo_l = sb(outer, "wo_l", [P, KC, D], f32r)
        yh = [sb(outer, "yh0", [P, KC, P], f32r)]
        yl = [sb(outer, "yl0", [P, KC, P], f32r)]
        kt = sb(outer, "kt", [P, GRP, SKEYS])
        k_loaded = ctx.enter_context(nc.semaphore("k_loaded"))
        y_loaded = [ctx.enter_context(nc.semaphore(f"y_loaded{s}")) for s in range(2)]
        xt_loaded = [ctx.enter_context(nc.semaphore(f"xt_loaded{s}")) for s in range(2)]
        y_high = ctx.enter_context(nc.semaphore("y_high"))
        y_split = ctx.enter_context(nc.semaphore("y_split"))
        y_stored = [ctx.enter_context(nc.semaphore(f"y_stored{s}")) for s in range(2)]
        attention(nc, x, cache_k, w_all, s_q, s_k, s_z, s_y, s_skew, v_all, gv_out, ident, big, par, bias_next, wts,
                  minus_half, eps, bias_loaded, st_b, st_b_stored, wo_h, wo_l, yh, yl, y_loaded, xt_loaded,
                  y_high, y_split, y_stored, kt, k_loaded)
        output_projection(nc, x, ln_g, ln_b, cache_k, cache_v, s_z, s_y, s_skew, v_all, y_out, ident, big, par,
                          minus_half, eps, qs, ks, wo_h, wo_l, yh, yl, y_loaded, xt_loaded, y_high, y_split, y_stored, kt, k_loaded)


def input_projection(nc, x_t, w_all, w_sgu, b_sgu, ln_v_g, ln_v_b, rel_rev, s_gate, s_va, s_q, s_k, s_z, s_y,
                     s_rel, s_skew, v_all, k_tail, ident, big, par, bias_next, wts, minus_half, eps, qs, ks, st_b,
                     bias_loaded, st_b_stored):
    f32, f32r = mybir.dt.float32, mybir.dt.float32r
    ALU = mybir.AluOpType
    ACT = mybir.ActivationFunctionType

    ctx = ExitStack()
    with ctx:
        def sb(name, shape, dt=f32):
            return ctx.enter_context(nc.sbuf_tensor(name, shape, dt))

        def sem(name):
            return ctx.enter_context(nc.semaphore(name))

        xh = sb("xh", [P, KC, T], f32r)
        xl = sb("xl", [P, KC, T], f32r)
        raw = [sb(f"raw{s}", [P, KC, P]) for s in range(2)]
        wh = [sb(f"wh{s}", [P, KC, P], f32r) for s in range(2)]
        wl = [sb(f"wl{s}", [P, KC, P], f32r) for s in range(2)]
        x_in = [buf[:, s * D:(s + 1) * D] for buf in (big, par) for s in range(2)]
        lnvg, lnvb = par[:, 0:512], par[:, 512:1024]
        bs, bss = (par[:, a:a + 512].rearrange("p (g t) -> p g t", g=GRP) for a in (1024, 1536))
        va_t = big[:, 0:512].rearrange("p (g t) -> p g t", g=GRP)
        gate_t = big[:, 512:1024].rearrange("p (g t) -> p g t", g=GRP)
        vn = big[:, 1024:1536]
        ya = big[:, 1536:2048].rearrange("p (g t) -> p g t", g=GRP)
        st_a = [sb(f"st_a{s}", [P, 512]) for s in range(2)]
        kf = bias_next[:, 0:640]
        vt = sb("vt", [P, 512])
        wt = sb("wt", [P, GRP, P])
        stats = sb("stats", [P, 6])
        mv = sb("mv", [P, 2])
        rstd = sb("rstd", [P, 1])

        bank = [ctx.enter_context(nc.psum_tensor(f"bank{c}", [P, 512], f32)) for c in range(NCH)]
        tg_ps = ctx.enter_context(nc.psum_tensor("tg_ps", [P, 512], f32))
        tv_ps = ctx.enter_context(nc.psum_tensor("tv_ps", [P, 512], f32))
        mix_ps = ctx.enter_context(nc.psum_tensor("mix_ps", [P, 512], f32))

        par_loaded = sem("par_loaded")
        blocks_loaded = sem("blocks_loaded")
        const_ready = sem("const_ready")
        zeroed = sem("zeroed")
        bss_ready = sem("bss_ready")
        rel_loaded = sem("rel_loaded")
        rel_filled = sem("rel_filled")
        rel_negated = sem("rel_negated")
        rel_stored = sem("rel_stored")
        x_loaded = [sem(f"x_loaded{s}") for s in range(PIECES)]
        xh_done = sem("xh_done")
        x_split = sem("x_split")
        raw_loaded = [sem(f"raw_loaded{s}") for s in range(2)]
        wh_done = sem("wh_done")
        w_ready = sem("w_ready")
        proj_done = sem("proj_done")
        evac = [sem(f"evac{c}") for c in range(NCH)]
        act_read = sem("act_read")
        gate_full = sem("gate_full")
        st_a_stored = [sem(f"st_a_stored{s}") for s in range(2)]
        kf_full = sem("kf_full")
        tv_done = sem("tv_done")
        tv_copied = sem("tv_copied")
        kf_stored = sem("kf_stored")
        va_loaded = sem("va_loaded")
        gate_loaded = sem("gate_loaded")
        tg_done = sem("tg_done")
        tg_read = sem("tg_read")
        stats_ready = sem("stats_ready")
        mv_ready = sem("mv_ready")
        var_eps = sem("var_eps")
        rstd_ready = sem("rstd_ready")
        vn_ready = sem("vn_ready")
        mix_done = sem("mix_done")
        mix_read = sem("mix_read")
        ya_full = sem("ya_full")
        ya_stored = sem("ya_stored")

        block = ctx.enter_context(nc.Block())

        A_J, B_J = len(GATE_GROUPS), len(PAIR_GROUPS)
        N_A = GRP + GRP * A_J
        STORED_A = [16 * GRP * NCH // 2] * 2

        def piece(m):
            t0, n = CHUNKS[m // PIECES]
            k0 = 2 * (m % PIECES)
            held = x_in[m % PIECES][:, 0:2 * n].rearrange("p (k t) -> p k t", k=2)
            return held, (slice(None), slice(k0, k0 + 2), slice(t0, t0 + n))

        @block.sync
        def _(sp):
            for s in range(2):
                sp.sem_inc(st_a_stored[s], 16)
                sp.sem_inc(st_b_stored[s], 16)
            sp.sem_inc(kf_stored, 16)
            sp.sem_inc(ya_stored, 16)

            def load_x(m):
                held, at = piece(m)
                sp.dma_start(held, x_t[at]).then_inc(x_loaded[m % PIECES], 16)

            def store_va(g, c, e):
                t0, n = CHUNKS[c]
                sp.wait_ge(evac[c], g + 2)
                sp.dma_start(s_va[g, :, t0:t0 + n], st_a[e % 2][:, 0:n]).then_inc(st_a_stored[e % 2], 16)

            for m in range(PIECES):
                load_x(m)
            sp.dma_start(wt[:], w_sgu).then_inc(par_loaded, 16)
            sp.wait_ge(zeroed, 1)
            for b in range(SB):
                sp.dma_start(wts[b * SN:(b + 1) * SN, :, b * SN:(b + 1) * SN],
                             w_sgu[0:SN, :, 0:SN]).then_inc(blocks_loaded, 16)
            sp.dma_start(kf[0:HEADS, 0:2 * CLIP + 1], rel_rev).then_inc(rel_loaded, 16)
            e = 0
            for step in opening():
                if step[0] == "split":
                    for m in range(PIECES * step[1], PIECES * (step[1] + 1)):
                        if m + PIECES < PIECES * NCH:
                            sp.wait_ge(x_split, m + 1)
                            load_x(m + PIECES)
                else:
                    store_va(step[1], step[2], e)
                    e += 1
            sp.wait_ge(x_split, PIECES * NCH)
            sp.dma_start(lnvg, ln_v_g.partition_broadcast(P)).then_inc(par_loaded, 16)
            sp.dma_start(lnvb, ln_v_b.partition_broadcast(P)).then_inc(par_loaded, 16)
            sp.dma_start(par[:, 1024:1536], b_sgu.partition_broadcast(P)).then_inc(par_loaded, 16)

            sp.wait_ge(rel_negated, 2)
            flat = REL - (2 * CLIP + 1)
            sp.dma_start(s_rel[:, 0:flat], vt[0:HEADS, 0:flat]).then_inc(rel_stored, 16)
            sp.dma_start(s_rel[:, flat:REL], kf[0:HEADS, 0:2 * CLIP + 1]).then_inc(rel_stored, 16)
            sp.wait_ge(rel_stored, 32)
            for h in range(HEADS):
                sp.dma_start(s_skew[h, :, 0:REL], s_rel[h, :].partition_broadcast(P)).then_inc(rel_stored, 16)

            for g in (2, 3):
                for c in range(NCH):
                    store_va(g, c, g * NCH + c)
            with sp.Fori(0, GRP) as i:
                for c, (t0, n) in enumerate(CHUNKS):
                    sp.wait_ge(gate_full, i * NCH + c + 1 + NCH)
                    sp.dma_start(s_gate[i, :, t0:t0 + n], st_b[c % 2][:, 0:n]).then_inc(st_b_stored[c % 2], 16)

            def load_gmlp(tile):
                sp.dma_start(va_t, s_va[:, :, bass.ts(tile, P)].rearrange("g c t -> c g t")).then_inc(va_loaded, 16)
                sp.dma_start(gate_t, s_gate[:, :, bass.ts(tile, P)].rearrange("g c t -> c g t")).then_inc(gate_loaded, 16)

            for s in range(2):
                sp.wait_ge(st_a_stored[s], 16 + STORED_A[s])
                sp.wait_ge(st_b_stored[s], 16 + STORED_B[s])
            load_gmlp(0)

            def store_k(p):
                sp.wait_ge(kf_full, p * 2 + 2)
                sp.dma_start(k_tail[p, :, :], kf).then_inc(kf_stored, 16)

            def store_vn(c, p):
                t0, n = CHUNKS[c]
                sp.wait_ge(tv_copied, p * NCH + c + 2)
                sp.dma_start(v_all[t0:t0 + n, bass.ts(p, P)].rearrange("(n t) c -> t n c", t=P),
                             st_b[c % 2][:, 0:n].rearrange("t (n c) -> t n c", c=P)).then_inc(st_b_stored[c % 2], 16)

            with sp.Fori(0, LOOP_B) as p:
                for j, kind in enumerate(PAIR_GROUPS):
                    for c, (t0, n) in enumerate(CHUNKS):
                        m = min(n, SEQ - t0)
                        if c == NCH - 1:
                            sp.wait_ge(ya_full, p * 4 + j + 1)
                            sp.dma_start(s_y[0:GRP, :, bass.ts(p * 4 + j, P)].rearrange("g c t -> c g t"),
                                         ya).then_inc(ya_stored, 16)
                            load_gmlp(p * 4 + j + 1)
                        if kind in "qk":
                            e = 5 * j + c
                            dst = s_q if kind == "q" else s_k
                            sp.wait_ge(evac[c], N_A + p * B_J + j + 2)
                            sp.dma_start(dst[0, p, :, t0:t0 + m], st_a[e % 2][:, 0:m]).then_inc(st_a_stored[e % 2], 16)
                            sp.dma_start(dst[1, p, :, t0:t0 + m], st_b[e % 2][:, 0:m]).then_inc(st_b_stored[e % 2], 16)
                        if kind == "z":
                            if c == 0:
                                store_vn(4, p)
                            e = 15 + c
                            sp.wait_ge(evac[c], N_A + p * B_J + j + 2)
                            sp.dma_start(s_z[p, :, t0:t0 + n], st_b[e % 2][:, 0:n]).then_inc(st_b_stored[e % 2], 16)
                        if kind == "k" and c == 4:
                            store_k(p)
                        if kind == "v" and c > 0:
                            store_vn(c - 1, p)

            sp.wait_ge(kf_stored, 16 + 16 * LOOP_B)
            sp.wait_ge(rel_stored, 16 * (2 + HEADS))
            sp.dma_start(bias_next[:].rearrange("p (h j) -> p h j", h=2),
                         skewed(s_skew, slice(0, 2), P, WIN - P, WIN)).then_inc(bias_loaded, 16)
            sp.wait_ge(va_loaded, 16 * TILES)
            sp.wait_ge(gate_loaded, 16 * TILES)
            sp.wait_ge(ya_stored, 16 + 16 * PTILES)
            for s in range(2):
                sp.wait_ge(st_a_stored[s], 16 + STORED_A[s] + 16 * 5 * LOOP_B)

        @block.gpsimd
        def _(pool):
            nc.gpsimd.memset(minus_half[:], -0.5).then_inc(const_ready, 1)
            nc.gpsimd.memset(eps[:], EPS).then_inc(const_ready, 1)
            nc.gpsimd.memset(ident[:], 1.0).then_inc(const_ready, 1)
            nc.gpsimd.memset(wts[:], 0.0).then_inc(zeroed, 1)
            nc.gpsimd.memset(vt[:], 0.0).then_inc(rel_filled, 1)
            pool.wait_ge(const_ready, 3)
            nc.gpsimd.affine_select(out=ident[:], in_=ident[:], compare_op=ALU.is_equal, fill=0.0, base=0,
                                    pattern=[[-1, P]], channel_multiplier=1).then_inc(const_ready, 1)
            for v, held, need in ((wt, par_loaded, 64), (wts, blocks_loaded, 16 * SB)):
                pool.wait_ge(held, need)
                nc.gpsimd.affine_select(out=v[:], in_=v[:], compare_op=ALU.is_ge, fill=0.0, base=0,
                                        pattern=[[0, GRP], [1, P]], channel_multiplier=-1).then_inc(const_ready, 1)

            def gmlp(n):
                pool.wait_ge(mv_ready, n + 1)
                nc.gpsimd.tensor_tensor(rstd[:], mv[:, 1:2], eps[:], ALU.add).then_inc(var_eps, 1)
                pool.wait_ge(var_eps, n + 1)
                nc.gpsimd.tensor_tensor(rstd[:], rstd[:], minus_half[:], ALU.pow).then_inc(rstd_ready, 1)
                pool.wait_ge(mix_read, n + 2)
                pool.wait_ge(gate_loaded, n * 16 + 16)
                nc.gpsimd.tensor_tensor(ya, ya, gate_t, ALU.mult).then_inc(ya_full, 1)

            with pool.Fori(0, PTILES) as n:
                gmlp(n)

        @block.scalar
        def _(act):
            def load_w(n, s):
                act.dma_start(raw[s][:], w_all[n, :, :, :]).then_inc(raw_loaded[s], 16)

            def high_part(s, loads):
                act.wait_ge(raw_loaded[s], loads * 16)
                nc.scalar.activation(wh[s][:], raw[s][:], ACT.Copy).then_inc(wh_done, 1)

            def x_high(m):
                held, at = piece(m)
                act.wait_ge(x_loaded[m % PIECES], 16 * (m // PIECES + 1))
                nc.scalar.activation(xh[at], held, ACT.Copy).then_inc(xh_done, 1)

            def split(n, s, loads):
                act.wait_ge(w_ready, n)
                load_w(n + 1, 1 - s)
                high_part(s, loads)

            def gelu_va(order, c, e):
                act.wait_ge(proj_done, order + 1)
                act.wait_ge(st_a_stored[e % 2], 16 * (e // 2) + 16)
                n = CHUNKS[c][1]
                nc.scalar.activation(st_a[e % 2][:, 0:n], bank[c][:, 0:n], ACT.Gelu).then_inc(evac[c], 1)

            load_w(0, 0)
            high_part(0, 1)
            e = 0
            for step in opening():
                if step[0] == "split":
                    for m in range(PIECES * step[1], PIECES * (step[1] + 1)):
                        x_high(m)
                        if m == 0:
                            load_w(1, 1)
                    if step[1] == 0:
                        high_part(1, 1)
                else:
                    gelu_va(e, step[2], e)
                    e += 1
                    if step[1:] == (1, 0):
                        act.wait_ge(w_ready, 1)
                        load_w(2, 0)
                    if step[1:] == (0, NCH - 1):
                        split(2, 0, 2)
            for g in (2, 3):
                for c in range(NCH):
                    gelu_va(g * NCH + c, c, g * NCH + c)
                    if c == 1:
                        split(g + 1, (g + 1) % 2, (g + 1) // 2 + 1)
            act.wait_ge(x_split, PIECES * NCH)
            with act.Fori(0, GRP) as i:
                for j, kind in enumerate(GATE_GROUPS):
                    for c, (t0, n) in enumerate(CHUNKS):
                        act.wait_ge(proj_done, GRP * NCH + i * (A_J * NCH) + NCH * j + c + 1)
                        src = bank[c][:, 0:n]
                        if kind == "u":
                            act.wait_ge(gate_full, i * NCH + c + 1)
                            nc.scalar.activation(big[:, t0:t0 + n], src, ACT.Gelu).then_inc(evac[c], 1)
                        else:
                            act.wait_ge(st_b_stored[c % 2], i * (STORED_B[c % 2] // GRP) + 16 * (c // 2) + 16)
                            nc.scalar.activation(st_b[c % 2][:, 0:n], src, ACT.Tanh, scale=0.5).then_inc(act_read, 1)
                        if c == 1:
                            split(GRP + i * A_J + j + 1, (j + 1) % 2, GRP // 2 + i + (j + 1) // 2 + 1)
            with act.Fori(0, LOOP_B) as p:
                for j, kind in enumerate(PAIR_GROUPS):
                    for c, (t0, n) in enumerate(CHUNKS):
                        act.wait_ge(proj_done, 5 * N_A + p * (5 * B_J) + 5 * j + c + 1)
                        src = bank[c][:, 0:n]
                        e = 5 * j + c
                        if kind in "qk":
                            act.wait_ge(st_a_stored[e % 2], STORED_A[e % 2] + p * 80 + 16 * (e // 2) + 16)
                            scale = QSCALE if kind == "q" else 1.0
                            if kind == "q" and c == 4:
                                nc.scalar.activation(qs[:, p, :], src[:, 256:384], ACT.Copy, scale=scale)
                            if kind == "k" and c == 3:
                                act.wait_ge(kf_stored, p * 16 + 16)
                                nc.scalar.activation(kf[:, 0:256], src[:, 128:384], ACT.Copy).then_inc(kf_full, 1)
                            if kind == "k" and c == 4:
                                nc.scalar.activation(ks[:, p, :], src[:, 256:384], ACT.Copy)
                                nc.scalar.activation(kf[:, 256:640], src, ACT.Copy).then_inc(kf_full, 1)
                            nc.scalar.activation(st_a[e % 2][:, 0:n].bitcast(f32r), src, ACT.Copy,
                                                 scale=scale).then_inc(act_read, 1)
                        elif kind == "v":
                            if c > 0:
                                act.wait_ge(tv_done, p * NCH + c)
                            nc.scalar.activation(vt[:, 0:n], src, ACT.Copy).then_inc(evac[c], 1)
                        else:
                            act.wait_ge(st_b_stored[e % 2], STORED_B[e % 2] + p * 160 + 16 * (e // 2) + 16)
                            nc.scalar.activation(st_b[e % 2][:, 0:n], src, ACT.Tanh, scale=0.5).then_inc(act_read, 1)
                        if c == 1:
                            split(N_A + p * B_J + j + 1, (j + 1) % 2, N_A // 2 + p * (B_J // 2) + (j + 1) // 2 + 1)

            act.wait_ge(raw_loaded[1], 16 * (NGROUPS // 2 + 1))

        @block.vector
        def _(dve):
            dve.sem_inc(tv_copied, 1)
            dve.sem_inc(tg_read, 1)
            dve.sem_inc(mix_read, 1)
            dve.sem_inc(gate_full, NCH)
            for c in range(NCH):
                dve.sem_inc(evac[c], 1)

            def low_part(n, s):
                dve.wait_ge(wh_done, n + 1)
                nc.vector.tensor_tensor(wl[s][:], raw[s][:], wh[s][:].bitcast(f32), ALU.subtract).then_inc(w_ready, 1)

            def x_low(m):
                held, at = piece(m)
                dve.wait_ge(xh_done, m + 1)
                nc.vector.tensor_tensor(xl[at], held, xh[at].bitcast(f32), ALU.subtract).then_inc(x_split, 1)

            low_part(0, 0)
            for step in opening():
                if step[0] == "split":
                    for m in range(PIECES * step[1], PIECES * (step[1] + 1)):
                        x_low(m)
                    if step[1] == 0:
                        low_part(1, 1)
            low_part(2, 0)
            dve.wait_ge(rel_loaded, 16)
            dve.wait_ge(rel_filled, 1)
            nc.vector.tensor_scalar(kf[0:HEADS, 0:2 * CLIP + 1], kf[0:HEADS, 0:2 * CLIP + 1], -1.0, None,
                                    ALU.mult).then_inc(rel_negated, 1)
            dve.wait_ge(rel_negated, 1)
            nc.vector.tensor_scalar(vt[0:HEADS, :], vt[0:HEADS, :], kf[0:HEADS, 0:1], None, ALU.add).then_inc(rel_negated, 1)
            low_part(3, 1)
            dve.wait_ge(par_loaded, 64)
            for b in range(SB):
                nc.vector.tensor_copy(bss[:, :, b * SN:(b + 1) * SN], bs[:, :, 0:SN]).then_inc(bss_ready, 1)
            low_part(4, 0)

            def silu_twice(n, c, st, handed):
                dve.wait_ge(act_read, handed)
                nc.vector.scalar_tensor_tensor(out=st, in0=st, scalar=1.0, in1=bank[c][:, 0:n], op0=ALU.add,
                                               op1=ALU.mult).then_inc(evac[c], 1)

            with dve.Fori(0, GRP) as i:
                for j, kind in enumerate(GATE_GROUPS):
                    for c, (t0, n) in enumerate(CHUNKS):
                        if kind == "za":
                            st = st_b[c % 2][:, 0:n]
                            silu_twice(n, c, st, i * NCH + c + 1)
                            dve.wait_ge(evac[c], GRP + i * A_J + j + 2)
                            nc.vector.scalar_tensor_tensor(out=st, in0=st, scalar=0.5, in1=big[:, t0:t0 + n],
                                                           op0=ALU.mult, op1=ALU.mult).then_inc(gate_full, 1)
                        if c == 1:
                            low_part(GRP + i * A_J + j + 1, (j + 1) % 2)

            def gmlp_stats(n):
                dve.wait_ge(tg_done, n + 1)
                nc.vector.bn_stats(stats[:], tg_ps[:]).then_inc(stats_ready, 1)
                dve.wait_ge(stats_ready, n + 1)
                dve.nop(nofuse=True)
                nc.vector.bn_aggr(mv[:], stats[:]).then_inc(mv_ready, 1)

            def gmlp_normalise(n):
                dve.wait_ge(mv_ready, n + 1)
                nc.vector.scalar_tensor_tensor(out=vn, in0=tg_ps[:], scalar=mv[:, 0:1], in1=lnvg, op0=ALU.subtract,
                                               op1=ALU.mult).then_inc(tg_read, 1)
                dve.wait_ge(tg_read, n + 2)
                dve.wait_ge(rstd_ready, n + 1)
                nc.vector.scalar_tensor_tensor(out=vn, in0=vn, scalar=rstd[:], in1=lnvb, op0=ALU.mult,
                                               op1=ALU.add).then_inc(vn_ready, 1)

            def gmlp_mixed(n):
                dve.wait_ge(mix_done, n + 1)
                dve.wait_ge(ya_stored, n * 16 + 16)
                nc.vector.tensor_tensor(ya, mix_ps[:].rearrange("p (g t) -> p g t", g=GRP), bs,
                                        ALU.add).then_inc(mix_read, 1)

            def copy_vn(c, p):
                n = CHUNKS[c][1]
                dve.wait_ge(tv_done, p * NCH + c + 1)
                dve.wait_ge(st_b_stored[c % 2], STORED_B[c % 2] + p * 160 + 16 * ((10 + c) // 2) + 16)
                nc.vector.tensor_copy(st_b[c % 2][:, 0:n], tv_ps[:, 0:n]).then_inc(tv_copied, 1)

            with dve.Fori(0, LOOP_B) as p:
                for j, kind in enumerate(PAIR_GROUPS):
                    for c, (t0, n) in enumerate(CHUNKS):
                        e = 5 * j + c
                        if kind in "qk":
                            dve.wait_ge(act_read, 20 + p * 15 + e + 1)
                            dve.wait_ge(st_b_stored[e % 2], STORED_B[e % 2] + p * 160 + 16 * (e // 2) + 16)
                            nc.vector.scalar_tensor_tensor(
                                out=st_b[e % 2][:, 0:n].bitcast(f32r), in0=bank[c][:, 0:n],
                                scalar=QSCALE if kind == "q" else 1.0, in1=st_a[e % 2][:, 0:n],
                                op0=ALU.mult, op1=ALU.subtract).then_inc(evac[c], 1)
                        if kind == "z":
                            silu_twice(n, c, st_b[e % 2][:, 0:n], 20 + p * 15 + 10 + c + 1)
                        if c == 0:
                            gmlp_stats(p * 4 + j)
                        if c == 1:
                            gmlp_normalise(p * 4 + j)
                            low_part(N_A + p * B_J + j + 1, (j + 1) % 2)
                        if c == 3:
                            gmlp_mixed(p * 4 + j)
                        if kind == "v" and c > 0:
                            copy_vn(c - 1, p)
                        if kind == "z" and c == 0:
                            copy_vn(4, p)
            dve.wait_ge(bss_ready, SB)

        @block.tensor
        def _(pe):
            def project(n, c, s, splitting=False):
                t0, width = CHUNKS[c]
                if c == 0:
                    pe.wait_ge(w_ready, n + 1)
                pe.wait_ge(evac[c], n + 1)
                for kc in range(KC):
                    if splitting and kc % 2 == 0:
                        pe.wait_ge(x_split, PIECES * c + kc // 2 + 1)
                    for a, (w, xx) in enumerate(((wh, xh), (wh, xl), (wl, xh))):
                        last = nc.tensor.matmul(bank[c][:, 0:width], w[s][:, kc, :], xx[:, kc, t0:t0 + width],
                                                start=kc == 0 and a == 0, stop=kc == KC - 1 and a == 2)
                last.then_inc(proj_done, 1)

            for step in opening():
                if step[0] == "project":
                    _, g, c = step
                    project(g, c, g, splitting=g == 0)
            for g in (2, 3):
                for c in range(NCH):
                    project(g, c, g % 2)
            with pe.Fori(0, GRP) as i:
                for j in range(A_J):
                    for c in range(NCH):
                        project(GRP + i * A_J + j, c, j % 2)

            pe.wait_ge(const_ready, 6)

            def turn_va(n):
                pe.wait_ge(va_loaded, n * 16 + 16)
                pe.wait_ge(tg_read, n + 1)
                for g in range(GRP):
                    last = nc.tensor.transpose(tg_ps[:, g * P:(g + 1) * P], va_t[:, g, :], ident[:])
                last.then_inc(tg_done, 1)

            def mix(n):
                pe.wait_ge(vn_ready, n + 1)
                pe.wait_ge(mix_read, n + 1)
                for g in range(GRP):
                    last = nc.tensor.matmul(mix_ps[:, g * P:(g + 1) * P], vn[:, g * P:(g + 1) * P], wt[:, g, :],
                                            start=True, stop=True)
                last.then_inc(mix_done, 1)

            def turn_v(c, p):
                pe.wait_ge(evac[c], N_A + p * B_J + 2 + 2)
                pe.wait_ge(tv_copied, p * NCH + c + 1)
                for n in range(CHUNKS[c][1] // P):
                    last = nc.tensor.transpose(tv_ps[:, n * P:(n + 1) * P], vt[:, n * P:(n + 1) * P], ident[:])
                last.then_inc(tv_done, 1)

            with pe.Fori(0, LOOP_B) as p:
                for j, kind in enumerate(PAIR_GROUPS):
                    for c in range(NCH):
                        project(N_A + p * B_J + j, c, j % 2)
                        if c == 0:
                            turn_va(p * 4 + j)
                        if c == 3:
                            mix(p * 4 + j)
                        if kind == "v" and c > 0:
                            turn_v(c - 1, p)
                        if kind == "z" and c == 0:
                            turn_v(4, p)


def skewed(s_skew, heads, queries, past, keys):
    first = WIN - 1 - past
    flat = s_skew.rearrange("h i m -> h (i m)")[heads, first:first + queries * REL]
    return flat.rearrange("h (i m) -> i h m", m=REL)[:, :, 0:keys]


def key_tiles(t):
    return min(t, 4) + 1


def turned_banks(t):
    return -(-2 * key_tiles(t) // 4)


def attention(nc, x, cache_k, w_all, s_q, s_k, s_z, s_y, s_skew, v_all, gv_out, ident, big, par, bias_next, wts,
              minus_half, eps, bias_loaded, st_b, st_b_stored, wo_h, wo_l, yh, yl, y_loaded, xt_loaded,
                  y_high, y_split, y_stored, kt, k_loaded):
    f32, f32r = mybir.dt.float32, mybir.dt.float32r
    ALU = mybir.AluOpType
    ACT = mybir.ActivationFunctionType

    ctx = ExitStack()
    with ctx:
        def sb(name, shape, dt=f32):
            return ctx.enter_context(nc.sbuf_tensor(name, shape, dt))

        def sem(name):
            return ctx.enter_context(nc.semaphore(name))

        q = sb("q", [P, 2, 2, SEQ], f32r)
        k = sb("k", [P, 2, SEQ], f32r)
        v = sb("v", [P, PTILES, P])
        z = sb("z", [P, SEQ])
        bias_next = bias_next[:].rearrange("p (h j) -> p h j", h=2)
        bias = sb("bias", [P, 2, WIN])
        prob = [sb(f"prob{s}", [P, WIN]) for s in range(4)]
        low = sb("low", [P, 4])
        den = sb("den", [P, 4])
        rden = sb("rden", [P, 4])
        pt = [sb(f"pt{s}", [P, 10, P]) for s in range(2)]
        yst = st_b
        raw_o = [sb(f"raw_o{s}", [P, KC, P]) for s in range(2)]

        s_ps = [ctx.enter_context(nc.psum_tensor(f"s_ps{h}", [P, 2, 512], f32)) for h in range(2)]
        pt_ps = [ctx.enter_context(nc.psum_tensor(f"pt_ps{e}", [P, 4, P], f32)) for e in range(3)]
        o_ps = ctx.enter_context(nc.psum_tensor("o_ps", [P, 512], f32))

        qk_loaded = [sem(f"qk_loaded{c}") for c in range(4)]
        vz_loaded = [sem(f"vz_loaded{c}") for c in range(4)]
        first_loaded = sem("first_loaded")
        masked = sem("masked")
        bias_ready = sem("bias_ready")
        scored = sem("scored")
        biased = sem("biased")
        expd = sem("expd")
        rden_ready = sem("rden_ready")
        normed = sem("normed")
        turned = sem("turned")
        pt_copied = sem("pt_copied")
        pv_done = sem("pv_done")
        y_ready = sem("y_ready")
        raw_o_loaded = [sem(f"raw_o_loaded{s}") for s in range(2)]
        wo_high = sem("wo_high")
        wo_done = sem("wo_done")

        va_t, gate_t, ya = (big[:, a:a + 512].rearrange("p (g t) -> p g t", g=GRP) for a in (0, 512, 1536))
        vn = big[:, 1024:1536]
        lnvg, lnvb = par[:, 0:512], par[:, 512:1024]
        bss = par[:, 1536:2048].rearrange("p (g t) -> p g t", g=GRP)
        tg_ps, mix_ps = pt_ps[2][:].rearrange("p g t -> p (g t)"), o_ps
        stats = sb("stats_s", [P, 6])
        mv = sb("mv_s", [P, 2])
        rstd = sb("rstd_s", [P, 1])
        tg_done = sem("tg_done_s")
        stats_ready = sem("stats_ready_s")
        mv_ready = sem("mv_ready_s")
        var_eps = sem("var_eps_s")
        rstd_ready = sem("rstd_ready_s")
        vn_step = sem("vn_step_s")
        mix_done = sem("mix_done_s")
        ya_step = sem("ya_step_s")
        tail_stored = sem("tail_stored")

        QK_DMAS, VZ_DMAS = 6, 2
        BANKS = [0]
        for t in range(PTILES):
            BANKS.append(BANKS[-1] + turned_banks(t))
        assert BANKS[-1] % 3 == 0
        PER = BANKS[-1]

        block = ctx.enter_context(nc.Block())

        @block.sync
        def _(sp):
            for s in range(2):
                sp.sem_inc(y_stored[s], 16)

            def load_bias(pair):
                sp.dma_start(bias_next, skewed(s_skew, bass.ts(pair, 2), P, WIN - P, WIN)).then_inc(bias_loaded, 16)

            def load_qk(pair, at, loaded):
                for part in range(2):
                    qsrc = s_q[part, pair, :, at].rearrange("(h d) t -> d h t", h=2)
                    for half in range(2):
                        sp.dma_start(q[64 * half:64 * half + 64, :, part, at].bitcast(f32), qsrc).then_inc(loaded, 16)
                    ksrc = s_k[part, pair, :, at].rearrange("(h d) t -> d h t", h=2)
                    sp.dma_start(k[64 * part:64 * part + 64, :, at].bitcast(f32), ksrc).then_inc(loaded, 16)

            def load_vz(pair, c):
                at = slice(512 * c, 512 * c + 512)
                sp.dma_start(v[:, 4 * c:4 * c + 4, :],
                             v_all[at, bass.ts(pair, P)].rearrange("(n t) c -> t n c", t=P)).then_inc(vz_loaded[c], 16)
                sp.dma_start(z[:, at], s_z[pair, :, at]).then_inc(vz_loaded[c], 16)

            def load_chunk(pair, c):
                load_qk(pair, slice(512 * c, 512 * c + 512), qk_loaded[c])
                load_vz(pair, c)

            def store_y(pair, c):
                sp.wait_ge(y_ready, pair * PTILES + 4 * c + 4 + 1)
                sp.dma_start(s_y[pair + GRP, :, 512 * c:512 * c + 512], yst[c % 2][:]).then_inc(y_stored[c % 2], 16)

            def load_wo(pair):
                sp.wait_ge(wo_done, pair * 2 + 2)
                for g in range(2):
                    sp.dma_start(raw_o[g][:], w_all[pair * 2 + (NGROUPS + g), :, :, :]).then_inc(raw_o_loaded[g], 16)

            load_qk(0, slice(0, 2 * P), first_loaded)
            load_qk(0, slice(2 * P, 4 * P), qk_loaded[0])
            for s in range(2):
                sp.wait_ge(st_b_stored[s], ALL_STORED_B[s])
            load_vz(0, 0)
            for c in range(1, 4):
                load_chunk(0, c)
            load_wo(0)
            sp.wait_ge(vn_step, 2)
            sp.dma_start(gv_out, vn).then_inc(tail_stored, 16)
            sp.wait_ge(ya_step, 2)
            sp.dma_start(s_y[0:GRP, :, SEQ:T].rearrange("g c t -> c g t"), ya).then_inc(tail_stored, 16)
            for s in range(2):
                sp.dma_start(par[:, s * D:(s + 1) * D], x[bass.ts(s, P), :]).then_inc(xt_loaded[s], 16)
            sp.wait_ge(tail_stored, 32)
            with sp.Fori(0, GRP - 1) as pair:
                sp.wait_ge(bias_ready, pair * 2 + 2)
                load_bias(pair + 1)
                store_y(pair, 0)
                store_y(pair, 1)
                load_chunk(pair + 1, 0)
                load_wo(pair + 1)
                store_y(pair, 2)
                load_chunk(pair + 1, 1)
                store_y(pair, 3)
                load_chunk(pair + 1, 2)
                load_chunk(pair + 1, 3)
            sp.dma_start(kt[:, :, 0:PAST], cache_k[0, :, :, :]).then_inc(k_loaded, 16)
            store_y(GRP - 1, 0)
            sp.wait_ge(y_stored[0], 16 * 2 * GRP)
            for s in range(2):
                sp.dma_start(big[:, s * D:(s + 1) * D].rearrange("p (k t) -> p k t", k=KC),
                             s_y[:, :, bass.ts(s, P)].rearrange("k c t -> c k t")).then_inc(y_loaded[s], 16)
            for c in range(1, 4):
                store_y(GRP - 1, c)

        @block.gpsimd
        def _(pool):
            pool.sem_inc(wo_done, 2)
            pool.wait_ge(mv_ready, 1)
            nc.gpsimd.tensor_tensor(rstd[:], mv[:, 1:2], eps[:], ALU.add).then_inc(var_eps, 1)
            pool.wait_ge(var_eps, 1)
            nc.gpsimd.tensor_tensor(rstd[:], rstd[:], minus_half[:], ALU.pow).then_inc(rstd_ready, 1)
            pool.wait_ge(ya_step, 1)
            nc.gpsimd.tensor_tensor(ya, ya, gate_t, ALU.mult).then_inc(ya_step, 1)
            with pool.Fori(0, GRP) as pair:
                for g in range(2):
                    at = (slice(None), slice(None), bass.ts(pair * 2 + g, P))
                    pool.wait_ge(raw_o_loaded[g], pair * 16 + 16)
                    nc.gpsimd.tensor_copy(wo_h[at], raw_o[g][:]).then_inc(wo_high, 1)
                    pool.wait_ge(wo_high, pair * 2 + g + 1)
                    nc.gpsimd.tensor_tensor(wo_l[at], raw_o[g][:], wo_h[at].bitcast(f32), ALU.subtract).then_inc(wo_done, 1)

        @block.scalar
        def _(act):
            def exponent(pair, t, h):
                n, s = key_tiles(t) * P, (2 * t + h) % 4
                act.wait_ge(biased, pair * 32 + 2 * t + h + 1 + 2)
                nc.scalar.activation(prob[s][:, 0:n], prob[s][:, 0:n], ACT.Exp, bias=low[:, s:s + 1],
                                     scale=-1.0, accum_out=den[:, s:s + 1]).then_inc(expd, 1)

            def copy_turned(pair, t, e):
                m = min(4, 2 * key_tiles(t) - 4 * e)
                act.wait_ge(pv_done, pair * PTILES + t + 1)
                act.wait_ge(turned, pair * PER + BANKS[t] + e + 1)
                nc.scalar.activation(pt[t % 2][:, 4 * e:4 * e + m, :],
                                     pt_ps[(BANKS[t] + e) % 3][:, 0:m, :], ACT.Copy).then_inc(pt_copied, 1)

            def steps(pair, first):
                for t in range(PTILES):
                    for h in range(2):
                        exponent(pair, t, h)
                    if t == 0 and first:
                        continue
                    before = (pair, t - 1) if t >= 1 else (pair - 1, PTILES - 1)
                    for e in range(turned_banks(before[1])):
                        copy_turned(*before, e)

            steps(0, True)
            with act.Fori(1, GRP) as pair:
                steps(pair, False)
            act.wait_ge(y_loaded[0], 16)
            nc.scalar.activation(yh[0][:], big[:, 0:D].rearrange("p (k t) -> p k t", k=KC), ACT.Copy).then_inc(y_high, 1)
            for e in range(turned_banks(PTILES - 1)):
                copy_turned(GRP - 1, PTILES - 1, e)

        @block.vector
        def _(dve):
            dve.sem_inc(biased, 2)
            dve.sem_inc(pt_copied, 3)
            dve.wait_ge(tg_done, 1)
            nc.vector.bn_stats(stats[:], tg_ps).then_inc(stats_ready, 1)
            dve.wait_ge(stats_ready, 1)
            nc.vector.bn_aggr(mv[:], stats[:]).then_inc(mv_ready, 1)
            dve.wait_ge(mv_ready, 1)
            nc.vector.scalar_tensor_tensor(out=vn, in0=tg_ps, scalar=mv[:, 0:1], in1=lnvg, op0=ALU.subtract,
                                           op1=ALU.mult).then_inc(vn_step, 1)
            dve.wait_ge(vn_step, 1)
            dve.wait_ge(rstd_ready, 1)
            nc.vector.scalar_tensor_tensor(out=vn, in0=vn, scalar=rstd[:], in1=lnvb, op0=ALU.mult,
                                           op1=ALU.add).then_inc(vn_step, 1)

            def add_bias(pair, t, h):
                n, s = key_tiles(t) * P, (2 * t + h) % 4
                dve.wait_ge(scored, pair * 32 + 2 * t + h + 1)
                dve.nop(nofuse=True)
                if n > 512:
                    src = s_ps[h][:, :, 0:WIN // 2]
                    out, b = (a.rearrange("p (a b) -> p a b", a=2) for a in (prob[s][:], bias[:, h, :]))
                else:
                    src, out, b = s_ps[h][:, 0, 0:n], prob[s][:, 0:n], bias[:, h, WIN - n:WIN]
                nc.vector.tensor_tensor_reduce(out=out, in0=src, in1=b, scale=1.0, scalar=MASKED,
                                               op0=ALU.add, op1=ALU.min, accum_out=low[:, s:s + 1]).then_inc(biased, 1)

            def normalise(pair, t, h):
                n, s = key_tiles(t) * P, (2 * t + h) % 4
                dve.wait_ge(expd, pair * 32 + 2 * t + h + 1)
                nc.vector.reciprocal(rden[:, s:s + 1], den[:, s:s + 1]).then_inc(rden_ready, 1)
                dve.wait_ge(rden_ready, pair * 32 + 2 * t + h + 1)
                nc.vector.tensor_scalar(prob[s][:, 0:n], prob[s][:, 0:n], rden[:, s:s + 1], None,
                                        ALU.mult).then_inc(normed, 1)

            def gate(pair, t):
                c = t // 4
                if t % 4 == 0:
                    dve.wait_ge(y_stored[c % 2], pair * 32 + 16 * (c // 2) + 16)
                dve.wait_ge(pv_done, pair * PTILES + t + 1 + 2)
                nc.vector.scalar_tensor_tensor(
                    out=yst[c % 2][:, (t % 4) * P:(t % 4 + 1) * P], in0=o_ps[:, 0:P], scalar=0.5,
                    in1=z[:, t * P:(t + 1) * P], op0=ALU.mult, op1=ALU.mult).then_inc(y_ready, 1)

            nc.vector.memset(bias[HD:P, :, 0:HD], MASKED).then_inc(masked, 1)
            nc.vector.memset(bias[0:HD, :, WIN - HD:WIN], MASKED).then_inc(masked, 1)
            dve.wait_ge(masked, 2)

            def steps(pair, first):
                dve.wait_ge(bias_loaded, pair * 16 + 16)
                nc.vector.tensor_copy(bias[0:HD, :, 0:WIN - HD], bias_next[0:HD, :, 0:WIN - HD]).then_inc(bias_ready, 1)
                nc.vector.tensor_copy(bias[HD:P, :, HD:WIN], bias_next[HD:P, :, HD:WIN]).then_inc(bias_ready, 1)
                dve.wait_ge(bias_ready, pair * 2 + 2)
                for t in range(PTILES):
                    for h in range(2):
                        add_bias(pair, t, h)
                    for h in range(2):
                        normalise(pair, t, h)
                    if t == 1 and first:
                        dve.wait_ge(mix_done, 1)
                        nc.vector.tensor_tensor(ya, mix_ps[:].rearrange("p (g t) -> p g t", g=GRP), bss,
                                                ALU.add).then_inc(ya_step, 1)
                        dve.wait_ge(ya_step, 1)
                        dve.sem_inc(y_ready, 1)
                    if t >= 2:
                        gate(pair, t - 2)
                    elif not first:
                        gate(pair - 1, PTILES - 2 + t)

            steps(0, True)
            with dve.Fori(1, GRP) as pair:
                steps(pair, False)
            gate(GRP - 1, PTILES - 2)
            dve.wait_ge(y_high, 1)
            nc.vector.tensor_tensor(yl[0][:], big[:, 0:D].rearrange("p (k t) -> p k t", k=KC), yh[0][:].bitcast(f32),
                                    ALU.subtract).then_inc(y_split, 1)
            gate(GRP - 1, PTILES - 1)

        @block.tensor
        def _(pe):
            pe.sem_inc(pv_done, 2)

            def scores(pair, t, first):
                k0, n = (t + 1 - key_tiles(t)) * P, key_tiles(t) * P
                halves = [(0, 0, n)] if n <= 512 else [(0, 0, n // 2), (1, n // 2, n // 2)]
                if t == 0 and first:
                    pe.wait_ge(first_loaded, 16 * QK_DMAS)
                elif t % 4 == 0 or (t == 2 and first):
                    pe.wait_ge(qk_loaded[t // 4], (pair + 1) * (16 * QK_DMAS))
                for h in range(2):
                    pe.wait_ge(biased, pair * 32 + 2 * t + h + 1)
                    for b, at, m in halves:
                        for part in range(2):
                            last = nc.tensor.matmul(s_ps[h][:, b, 0:m], q[:, h, part, t * P:(t + 1) * P],
                                                    k[:, h, k0 + at:k0 + at + m], start=part == 0, stop=part == 1)
                    last.then_inc(scored, 1)

            def turn(pair, t):
                pe.wait_ge(normed, pair * 32 + 2 * t + 2)
                for e in range(turned_banks(t)):
                    pe.wait_ge(pt_copied, pair * PER + BANKS[t] + e + 1)
                    for i in range(4 * e, min(4 * e + 4, 2 * key_tiles(t))):
                        b, h = i // 2, i % 2
                        last = nc.tensor.transpose(pt_ps[(BANKS[t] + e) % 3][:, i - 4 * e, :],
                                                   prob[(2 * t + h) % 4][:, b * P:(b + 1) * P], ident[:])
                    last.then_inc(turned, 1)

            def weigh(pair, t):
                nk = key_tiles(t)
                if t % 4 == 0:
                    pe.wait_ge(vz_loaded[t // 4], (pair + 1) * (16 * VZ_DMAS))
                pe.wait_ge(pt_copied, pair * PER + BANKS[t + 1] + 3)
                pe.wait_ge(y_ready, pair * PTILES + t + 1)
                for b in range(nk):
                    for h in range(2):
                        last = nc.tensor.matmul(o_ps[64 * h:64 * h + 64, 0:P],
                                                v[:, t + 1 - nk + b, 64 * h:64 * h + 64], pt[t % 2][:, 2 * b + h, :],
                                                start=b == 0, stop=b == nk - 1, skip_group_check=True)
                last.then_inc(pv_done, 1)

            def steps(pair, first):
                for t in range(PTILES):
                    scores(pair, t, first)
                    if t == 1 and first:
                        pe.wait_ge(vn_step, 2)
                        for g in range(GRP):
                            last = nc.tensor.matmul(mix_ps[:, g * P:(g + 1) * P], vn[:, g * P:(g + 1) * P],
                                                    wts[:, g, :], start=True, stop=True)
                        last.then_inc(mix_done, 1)
                    if t >= 2:
                        weigh(pair, t - 2)
                    elif not first:
                        weigh(pair - 1, PTILES - 2 + t)
                    if t >= 1:
                        turn(pair, t - 1)
                    elif not first:
                        turn(pair - 1, PTILES - 1)

            for g in range(GRP):
                last = nc.tensor.transpose(tg_ps[:, g * P:(g + 1) * P], va_t[:, g, :], ident[:])
            last.then_inc(tg_done, 1)
            steps(0, True)
            with pe.Fori(1, GRP) as pair:
                steps(pair, False)
            weigh(GRP - 1, PTILES - 2)
            turn(GRP - 1, PTILES - 1)
            weigh(GRP - 1, PTILES - 1)


def output_projection(nc, x, ln_g, ln_b, cache_k, cache_v, s_z, s_y, s_skew, v_all, y_out, ident, big, par,
                      minus_half, eps, qs, ks, wo_h, wo_l, yh, yl, y_loaded, xt_loaded, y_high, y_split, y_stored, kt, k_loaded):
    f32, f32r = mybir.dt.float32, mybir.dt.float32r
    ALU = mybir.AluOpType
    ACT = mybir.ActivationFunctionType

    ctx = ExitStack()
    with ctx:
        def sb(name, shape, dt=f32):
            return ctx.enter_context(nc.sbuf_tensor(name, shape, dt))

        def sem(name):
            return ctx.enter_context(nc.semaphore(name))

        yr = [big[:, s * D:(s + 1) * D].rearrange("p (k t) -> p k t", k=KC) for s in range(2)]
        xt = [par[:, s * D:(s + 1) * D] for s in range(2)]
        yh = yh + [sb("yh1", [P, KC, P], f32r)]
        yl = yl + [sb("yl1", [P, KC, P], f32r)]
        r = [sb(f"r{s}", [P, D]) for s in range(2)]
        gain = sb("gain", [P, D])
        offset = sb("offset", [P, D])
        stats = sb("stats_o", [P, 2, 6])
        mv = sb("mv_o", [P, 2])
        rstd = sb("rstd_o", [P, 1])
        vc = sb("vc", [PAST, 512])
        vnew = sb("vnew", [SN, 512])
        qd = sb("qd", [P, GRP, 2 * SN])
        sbias = sb("sbias", [P, SKEYS])
        sprob = sb("sprob", [P, SKEYS])
        slow = sb("slow", [P, 1])
        sden = sb("sden", [P, 1])
        srden = sb("srden", [P, 1])
        spt = sb("spt", [P, 2, P])
        zs = sb("zs", [P, GRP, P])
        ys = sb("ys", [P, GRP, P])

        out_ps = [ctx.enter_context(nc.psum_tensor(f"out_ps{b}", [P, 512], f32)) for b in range(4)]
        ss_ps = ctx.enter_context(nc.psum_tensor("ss_ps", [P, 512], f32))
        spt_ps = ctx.enter_context(nc.psum_tensor("spt_ps", [P, 4, P], f32))
        so_ps = ctx.enter_context(nc.psum_tensor("so_ps", [P, 512], f32))

        par_loaded = sem("par_loaded_o")
        z_loaded = sem("z_loaded")
        sbias_loaded = sem("sbias_loaded")
        out_done = sem("out_done")
        out_read = sem("out_read")
        half_stats = sem("half_stats")
        mv_ready = sem("mv_ready_o")
        var_eps = sem("var_eps_o")
        rstd_ready = sem("rstd_ready_o")
        centred = sem("centred")
        r_ready = sem("r_ready")
        r_stored = [sem(f"r_stored{s}") for s in range(2)]
        const_ready = sem("const_ready_o")
        v_loaded = sem("v_loaded")
        q_ready = sem("q_ready")
        s_scored = sem("s_scored")
        s_biased = sem("s_biased")
        s_expd = sem("s_expd")
        s_rden = sem("s_rden")
        s_normed = sem("s_normed")
        s_turned = sem("s_turned")
        s_pt = sem("s_pt")
        s_weighed = sem("s_weighed")
        ys_ready = sem("ys_ready")

        block = ctx.enter_context(nc.Block())

        @block.sync
        def _(sp):
            for s in range(2):
                sp.sem_inc(r_stored[s], 16)

            def load_y(tile, s):
                sp.dma_start(yr[s], s_y[:, :, bass.ts(tile, P)].rearrange("k c t -> c k t")).then_inc(y_loaded[s], 16)

            def load_x(tile, s):
                sp.dma_start(xt[s], x[bass.ts(tile, P), :]).then_inc(xt_loaded[s], 16)

            def load_keys(b):
                sp.dma_start(kt[:, :, 0:PAST], cache_k[b, :, :, :]).then_inc(k_loaded, 16)

            def load_values(b):
                sp.dma_start(vc[:], cache_v[b, :, :]).then_inc(v_loaded, 16)
                sp.dma_start(vnew[:], v_all[bass.ds(b * SN + SEQ, SN), :]).then_inc(v_loaded, 16)

            def store_tile(tile, s, count):
                sp.wait_ge(r_ready, count)
                sp.dma_start(y_out[bass.ts(tile, P), :], r[s][:]).then_inc(r_stored[s], 16)

            for h in range(HEADS):
                src = skewed(s_skew, slice(h, h + 1), SN, PAST, SKEYS)[:, 0, :]
                sp.dma_start(sbias[h * SN:(h + 1) * SN, :], src).then_inc(sbias_loaded, 16)
            load_values(0)
            sp.dma_start(gain[:], ln_g.partition_broadcast(P)).then_inc(par_loaded, 16)
            sp.dma_start(offset[:], ln_b.partition_broadcast(P)).then_inc(par_loaded, 16)
            sp.dma_start(zs[:], s_z[:, :, SEQ:T].rearrange("g c t -> c g t")).then_inc(z_loaded, 16)
            for s in range(2):
                sp.wait_ge(y_stored[s], 16 + 16 * 2 * GRP)
            with sp.Fori(0, SB - 1) as i:
                for s in range(2):
                    sp.wait_ge(y_split, i * 2 + s + 1)
                    load_y(i * 2 + 2 + s, s)
                sp.wait_ge(s_scored, i + 1)
                load_keys(i + 1)
                for s in range(2):
                    sp.wait_ge(out_read, i * 4 + 2 * s + 2 + 4)
                    load_x(i * 2 + 2 + s, s)
                    if s == 0:
                        sp.wait_ge(ys_ready, i * 2 + 2)
                        load_values(i + 1)
                    store_tile(i * 2 + s, s, i * 2 + s + 1)
            sp.wait_ge(y_split, PTILES - 1)
            sp.dma_start(yr[0][:, 0:GRP, :], s_y[0:GRP, :, SEQ:T].rearrange("k c t -> c k t")).then_inc(y_loaded[0], 16)
            sp.wait_ge(out_read, 2 * (PTILES - 1) + 4)
            load_x(TILES - 1, 0)
            store_tile(PTILES - 2, 0, PTILES - 1)
            store_tile(PTILES - 1, 1, PTILES)
            for part in range(2):
                at = slice(D // 2 * part, D // 2 * (part + 1))
                sp.wait_ge(r_ready, TILES + part)
                sp.dma_start(y_out[bass.ts(TILES - 1, P), at], r[0][:, at]).then_inc(r_stored[0], 16)
            sp.wait_ge(r_stored[0], 16 * (SB + 3))
            sp.wait_ge(r_stored[1], 16 * (SB + 1))

        @block.gpsimd
        def _(pool):
            nc.gpsimd.memset(qd[:], 0.0).then_inc(const_ready, 1)
            pool.wait_ge(const_ready, 1)

            def root(n):
                pool.wait_ge(mv_ready, n + 1)
                nc.gpsimd.tensor_tensor(rstd[:], mv[:, 1:2], eps[:], ALU.add).then_inc(var_eps, 1)
                pool.wait_ge(var_eps, n + 1)
                nc.gpsimd.tensor_tensor(rstd[:], rstd[:], minus_half[:], ALU.pow).then_inc(rstd_ready, 1)

            with pool.Fori(0, TILES) as n:
                root(n)

        @block.scalar
        def _(act):
            def high(n, s, loads):
                act.wait_ge(y_loaded[s], loads)
                act.wait_ge(out_done, n * 2 + 2)
                nc.scalar.activation(yh[s][:], yr[s], ACT.Copy).then_inc(y_high, 1)

            def step(i, last):
                high(i * 2 + 1, 1, i * 16 + 16)
                stream(i, 1)
                stream(i, 2)
                if not last:
                    high(i * 2 + 2, 0, i * 16 + 32)

            def stream(i, stage):
                if stage == 1:
                    act.wait_ge(s_biased, i + 1)
                    nc.scalar.activation(sprob[:], sprob[:], ACT.Exp, bias=slow[:], scale=-1.0,
                                         accum_out=sden[:]).then_inc(s_expd, 1)
                if stage == 2:
                    act.wait_ge(s_turned, i + 1)
                    nc.scalar.activation(spt[:, 0, :], spt_ps[:, 0, :], ACT.Copy).then_inc(s_pt, 1)
                    nc.scalar.activation(spt[0:SN, 1, :], spt_ps[0:SN, 1, :], ACT.Copy).then_inc(s_pt, 1)

            with act.Fori(0, SB - 1) as i:
                step(i, False)
            step(SB - 1, True)
            act.wait_ge(y_loaded[0], 16 * (SB + 1))
            act.wait_ge(out_done, 2 * PTILES + 2)
            nc.scalar.activation(yh[0][:, 0:GRP, :], yr[0][:, 0:GRP, :], ACT.Copy).then_inc(y_high, 1)
            act.wait_ge(ys_ready, 2 * SB)
            nc.scalar.activation(yh[0][:, GRP:KC, :], ys[:], ACT.Copy).then_inc(y_high, 1)

        @block.vector
        def _(dve):
            dve.sem_inc(out_read, 4)

            def low(n, s):
                dve.wait_ge(y_high, n + 1)
                nc.vector.tensor_tensor(yl[s][:], yr[s], yh[s][:].bitcast(f32), ALU.subtract).then_inc(y_split, 1)

            def residual(n, s, h, loads, stores):
                dve.wait_ge(out_done, n * 2 + h + 1 + 4)
                if h == 0:
                    dve.wait_ge(xt_loaded[s], loads)
                    dve.wait_ge(r_stored[s], stores)
                at = slice(512 * h, 512 * h + 512)
                nc.vector.scalar_tensor_tensor(out=r[s][:, at], in0=xt[s][:, at], scalar=ALPHA, in1=out_ps[2 * s + h][:],
                                               op0=ALU.mult, op1=ALU.add).then_inc(out_read, 1)
                dve.wait_ge(out_read, n * 2 + h + 1 + 4)
                nc.vector.bn_stats(stats[:, h, :], r[s][:, at]).then_inc(half_stats, 1)

            def finish(n, s, parts=1):
                dve.wait_ge(half_stats, n * 2 + 2)
                dve.nop(nofuse=True)
                nc.vector.bn_aggr(mv[:], stats[:].rearrange("p h n -> p (h n)")).then_inc(mv_ready, 1)
                dve.wait_ge(par_loaded, 32)
                dve.wait_ge(mv_ready, n + 1)
                nc.vector.scalar_tensor_tensor(out=r[s][:], in0=r[s][:], scalar=mv[:, 0:1], in1=gain[:],
                                               op0=ALU.subtract, op1=ALU.mult).then_inc(centred, 1)
                dve.wait_ge(centred, n + 1)
                dve.wait_ge(rstd_ready, n + 1)
                for part in range(parts):
                    at = slice(D // parts * part, D // parts * (part + 1))
                    nc.vector.scalar_tensor_tensor(out=r[s][:, at], in0=r[s][:, at], scalar=rstd[:], in1=offset[:, at],
                                                   op0=ALU.mult, op1=ALU.add).then_inc(r_ready, 1)

            def stream(i, stage):
                at = bass.ts(i, SN)
                if stage == 0:
                    nc.vector.tensor_copy(kt[:, :, PAST:SKEYS], ks[:, :, at]).then_inc(q_ready, 1)
                    nc.vector.tensor_copy(qd[0:HD, :, 0:SN], qs[0:HD, :, at]).then_inc(q_ready, 1)
                    nc.vector.tensor_copy(qd[HD:P, :, SN:2 * SN], qs[HD:P, :, at]).then_inc(q_ready, 1)
                if stage == 1:
                    dve.wait_ge(sbias_loaded, 16 * HEADS)
                    dve.wait_ge(s_scored, i + 1)
                    dve.nop(nofuse=True)
                    nc.vector.tensor_tensor_reduce(out=sprob[:], in0=ss_ps[:, 0:SKEYS], in1=sbias[:], scale=1.0,
                                                   scalar=MASKED, op0=ALU.add, op1=ALU.min,
                                                   accum_out=slow[:]).then_inc(s_biased, 1)
                    dve.wait_ge(s_expd, i + 1)
                    nc.vector.reciprocal(srden[:], sden[:]).then_inc(s_rden, 1)
                    dve.wait_ge(s_rden, i + 1)
                    nc.vector.tensor_scalar(sprob[:], sprob[:], srden[:], None, ALU.mult).then_inc(s_normed, 1)
                if stage == 3:
                    dve.wait_ge(z_loaded, 16)
                    dve.wait_ge(s_weighed, i + 1)
                    o = so_ps[:, 0:GRP * 2 * SN].rearrange("p (g t) -> p g t", g=GRP)
                    for h in range(2):
                        rows = slice(HD * h, HD * h + HD)
                        nc.vector.scalar_tensor_tensor(out=ys[rows, :, at], in0=o[rows, :, SN * h:SN * h + SN], scalar=0.5,
                                                       in1=zs[rows, :, at], op0=ALU.mult, op1=ALU.mult).then_inc(ys_ready, 1)

            dve.wait_ge(const_ready, 1)

            def step(i, last):
                stream(i, 0)
                low(i * 2 + 1, 1)
                residual(i * 2, 0, 0, i * 16 + 16, i * 16 + 16)
                stream(i, 1)
                residual(i * 2, 0, 1, None, None)
                finish(i * 2, 0)
                residual(i * 2 + 1, 1, 0, i * 16 + 16, i * 16 + 16)
                stream(i, 3)
                if last:
                    dve.wait_ge(y_high, PTILES + 1)
                    nc.vector.tensor_tensor(yl[0][:, 0:GRP, :], yr[0][:, 0:GRP, :], yh[0][:, 0:GRP, :].bitcast(f32),
                                            ALU.subtract).then_inc(y_split, 1)
                    dve.wait_ge(y_high, PTILES + 2)
                    nc.vector.tensor_tensor(yl[0][:, GRP:KC, :], ys[:], yh[0][:, GRP:KC, :].bitcast(f32),
                                            ALU.subtract).then_inc(y_split, 1)
                else:
                    low(i * 2 + 2, 0)
                residual(i * 2 + 1, 1, 1, None, None)
                finish(i * 2 + 1, 1)

            with dve.Fori(0, SB - 1) as i:
                step(i, False)
            step(SB - 1, True)
            for h in range(2):
                residual(PTILES, 0, h, 16 * (SB + 1), 16 * (SB + 1))
            finish(PTILES, 0, parts=2)

        @block.tensor
        def _(pe):
            pe.sem_inc(out_done, 4)

            def project(n, s, h):
                if h == 0:
                    pe.wait_ge(y_split, n + 1)
                pe.wait_ge(out_read, n * 2 + h + 1)
                for c in range(KC):
                    for a, (y, w) in enumerate(((yh, wo_h), (yh, wo_l), (yl, wo_h))):
                        last = nc.tensor.matmul(out_ps[2 * s + h][:], y[s][:, c, :], w[:, c, 512 * h:512 * h + 512],
                                                start=c == 0 and a == 0, stop=c == KC - 1 and a == 2)
                last.then_inc(out_done, 1)

            def stream(i, stage):
                if stage == 1:
                    pe.wait_ge(k_loaded, i * 16 + 16)
                    pe.wait_ge(q_ready, i * 3 + 3)
                    for p in range(GRP):
                        last = nc.tensor.matmul(ss_ps[2 * SN * p:2 * SN * (p + 1), 0:SKEYS], qd[:, p, :], kt[:, p, :],
                                                start=True, stop=True)
                    last.then_inc(s_scored, 1)
                if stage == 2:
                    pe.wait_ge(s_normed, i + 1)
                    nc.tensor.transpose(spt_ps[:, 0, :], sprob[:, 0:PAST], ident[:])
                    nc.tensor.transpose(spt_ps[0:SN, 1, :], sprob[:, PAST:SKEYS], ident[:]).then_inc(s_turned, 1)
                if stage == 3:
                    pe.wait_ge(s_pt, i * 2 + 2)
                    pe.wait_ge(v_loaded, i * 32 + 32)
                    for p in range(GRP):
                        cols = slice(2 * SN * p, 2 * SN * (p + 1))
                        nc.tensor.matmul(so_ps[:, cols], vc[:, p * P:(p + 1) * P], spt[:, 0, cols], start=True, stop=False)
                        last = nc.tensor.matmul(so_ps[:, cols], vnew[:, p * P:(p + 1) * P], spt[0:SN, 1, cols],
                                                start=False, stop=True)
                    last.then_inc(s_weighed, 1)

            with pe.Fori(0, SB) as i:
                for e in range(4):
                    stream(i, e)
                    project(i * 2 + e // 2, e // 2, e % 2)
            pe.wait_ge(y_split, PTILES + 2)
            for h in range(2):
                project(PTILES, 0, h)


def lay_out(x_prompt, x_sample, cache_k, cache_v, w_in, w_sgu, b_sgu, ln_v_g, ln_v_b, rel_bias, w_out, ln_g, ln_b):
    c = np.ascontiguousarray
    w_in, w_out = np.asarray(w_in)[0], np.asarray(w_out)[0]
    x = np.concatenate([np.asarray(x_prompt).reshape(SEQ, D), np.asarray(x_sample).reshape(SB * SN, D)])
    base = {"u": 0, "va": 512, "za": 1024, "q": 1536, "k": 2048, "v": 2560, "z": 3072}
    first = [base["va"] + g * P for g in range(GRP)]
    first += [base[kind] + g * P for g in range(GRP) for kind in GATE_GROUPS]
    first += [base[kind] + p * P for p in range(LOOP_B) for kind in PAIR_GROUPS]
    groups = [w_in[:, f:f + P] for f in first] + [w_out[:, n * P:(n + 1) * P] for n in range(KC)]
    w_all = np.stack([g.reshape(KC, P, P).transpose(1, 0, 2) for g in groups])
    return {
        "x": c(x),
        "x_t": c(x.T.reshape(KC, P, T).transpose(1, 0, 2)),
        "w_all": c(w_all),
        "w_sgu": c(np.asarray(w_sgu)[0].transpose(2, 0, 1)), "b_sgu": c(np.asarray(b_sgu).reshape(-1)),
        "ln_v_g": c(np.asarray(ln_v_g)[0]), "ln_v_b": c(np.asarray(ln_v_b)[0]),
        "rel_rev": c(np.asarray(rel_bias)[0][:, ::-1]),
        "ln_g": c(np.asarray(ln_g)[0]), "ln_b": c(np.asarray(ln_b)[0]),
        "cache_k": c(np.asarray(cache_k).reshape(SB, PAST, GRP, P).transpose(0, 3, 2, 1)),
        "cache_v": c(np.asarray(cache_v).reshape(SB, PAST, HEADS * HD)),
    }


def kernel(x_prompt, x_sample, cache_k, cache_v, w_in, w_sgu, b_sgu, ln_v_g, ln_v_b, rel_bias, w_out, ln_g, ln_b):
    import concourse.bacc as bacc
    from concourse.bass_utils import run_bass_kernel_spmd

    arrays = lay_out(x_prompt, x_sample, cache_k, cache_v, w_in, w_sgu, b_sgu, ln_v_g, ln_v_b, rel_bias, w_out,
                     ln_g, ln_b)
    nc = bacc.Bacc("TRN2", target_bir_lowering=False, num_devices=1)
    args = {n: nc.dram_tensor(n, a.shape, mybir.dt.from_np(a.dtype), kind="ExternalInput").ap()
            for n, a in arrays.items()}
    outs = {"y_out": (T, D), "v_all": (T, HEADS * HD), "k_tail": (GRP, P, T - SEQ + KEEP), "gv_out": (SB * SN, 512)}
    for n, shape in outs.items():
        args[n] = nc.dram_tensor(n, shape, mybir.dt.float32, kind="ExternalOutput").ap()
    hybrid_stream_step(nc, **args)
    r = run_bass_kernel_spmd(nc, [arrays], core_ids=[0]).results[0]
    y, v, k, gv = r["y_out"], r["v_all"], r["k_tail"], r["gv_out"]
    k = k.reshape(HEADS * HD, T - SEQ + KEEP).T
    heads = (HEADS, HD)
    return (y[:SEQ].reshape(1, SEQ, D), y[SEQ:].reshape(SB, SN, D),
            k[:KEEP].reshape(1, 1, KEEP, *heads), v[SEQ - KEEP:SEQ].reshape(1, 1, KEEP, *heads),
            k[KEEP:].reshape(1, SB, SN, *heads), v[SEQ:].reshape(1, SB, SN, *heads),
            gv.reshape(1, SB, SN, 512))
```
